# Optimizing a Trainium2 kernel written in Bass

```python
import math
import numpy as np
import jax
import jax.numpy as jnp
from jax import lax

D_MODEL = 2048
BATCH = 1
SEQ = 256
DEPTH = 1

HEAD_DIM = 128
N_HEADS = D_MODEL // HEAD_DIM
N_HEADS_DIL = (3 * N_HEADS) // 8
N_HEADS_NSA = N_HEADS - N_HEADS_DIL
NSA_KV_GROUPS = 2
NSA_GROUP = N_HEADS_NSA // NSA_KV_GROUPS
N_NSA_BRANCHES = 3
DIL_PAIRS = ((128, 1), (512, 4), (2048, 16))
CMP_BLOCK = 32
CMP_STRIDE = 16
CMP_HIDDEN = 256
SEL_BLOCK = 64
N_SELECT = 16
NSA_WINDOW = 512
D_FF = 5632
ROPE_THETA = 10000.0
QBLK = 128
LN_EPS = 1e-5
NEG = -1e30
FORCE_BONUS = 1e4

D_DIL = N_HEADS_DIL * HEAD_DIM
D_NSA = N_HEADS_NSA * HEAD_DIM
KV_W = NSA_KV_GROUPS * HEAD_DIM
IN_COLS = 3 * D_DIL + D_NSA + 6 * KV_W + N_HEADS_NSA * N_NSA_BRANCHES

kernel_name = "hybrid_dilated_nsa_macaron_deepnorm"

def layer_norm(x, g, b):
    xf = x.astype(jnp.float32)
    mu = xf.mean(-1, keepdims=True)
    var = jnp.square(xf - mu).mean(-1, keepdims=True)
    y = (xf - mu) * lax.rsqrt(var + LN_EPS) * g.astype(jnp.float32) + b.astype(jnp.float32)
    return y.astype(x.dtype)

def swiglu(x, w1, w3, w2):
    return (jax.nn.silu(x @ w1) * (x @ w3)) @ w2

def rope_tables(pos_f):
    inv_freq = ROPE_THETA ** (-jnp.arange(0, HEAD_DIM, 2, dtype=jnp.float32) / HEAD_DIM)
    ang = pos_f.astype(jnp.float32)[..., None] * inv_freq
    return jnp.cos(ang), jnp.sin(ang)

def apply_rope(x, cos, sin):
    xf = x.astype(jnp.float32)
    x1, x2 = jnp.split(xf, 2, axis=-1)
    c, s = cos[:, :, None, :], sin[:, :, None, :]
    return jnp.concatenate([x1 * c - x2 * s, x2 * c + x1 * s], axis=-1).astype(x.dtype)

def masked_softmax(s, mask):
    s = jnp.where(mask, s.astype(jnp.float32), NEG)
    m = s.max(-1, keepdims=True)
    e = jnp.where(mask, jnp.exp(s - m), 0.0)
    return e / jnp.maximum(e.sum(-1, keepdims=True), 1e-30)

def banded_causal_attention(q, k, v, window):
    N, H, L, D = q.shape
    n_prev = -(-window // QBLK)
    nb = -(-L // QBLK)
    Lp = nb * QBLK
    qb = jnp.pad(q, ((0, 0), (0, 0), (0, Lp - L), (0, 0))).reshape(N, H, nb, QBLK, D)
    pad_kv = ((0, 0), (0, 0), (n_prev * QBLK, Lp - L), (0, 0))
    kb = jnp.pad(k, pad_kv).reshape(N, H, nb + n_prev, QBLK, D)
    vb = jnp.pad(v, pad_kv).reshape(N, H, nb + n_prev, QBLK, D)
    kband = jnp.concatenate([kb[:, :, j:j + nb] for j in range(n_prev + 1)], axis=3)
    vband = jnp.concatenate([vb[:, :, j:j + nb] for j in range(n_prev + 1)], axis=3)
    s = jnp.einsum('nhbqd,nhbkd->nhbqk', qb, kband).astype(jnp.float32) * (D ** -0.5)
    qpos = jnp.arange(nb)[:, None] * QBLK + jnp.arange(QBLK)[None, :]
    kpos = jnp.arange(nb)[:, None] * QBLK - n_prev * QBLK + jnp.arange((n_prev + 1) * QBLK)[None, :]
    dist = qpos[:, :, None] - kpos[:, None, :]
    mask = (dist >= 0) & (dist <= window) & (kpos[:, None, :] >= 0)
    s = jnp.where(mask, s, NEG)
    m = s.max(-1, keepdims=True)
    e = jnp.exp(s - m)
    l = e.sum(-1)
    o = jnp.einsum('nhbqk,nhbkd->nhbqd', e, vband) / l[..., None]
    lse = m[..., 0] + jnp.log(l)
    return o.reshape(N, H, Lp, D)[:, :, :L], lse.reshape(N, H, Lp)[:, :, :L]

def dilated_attention(q, k, v):
    B, S, H, D = q.shape
    outs, lses = [], []
    for window, dil in DIL_PAIRS:
        L = S // dil

        def to_sub(t):
            return t.reshape(B, L, dil, H, D).transpose(0, 2, 3, 1, 4).reshape(B * dil, H, L, D)

        o, lse = banded_causal_attention(to_sub(q), to_sub(k), to_sub(v), window // dil)
        outs.append(o.reshape(B, dil, H, L, D).transpose(0, 3, 1, 2, 4).reshape(B, S, H, D))
        lses.append(lse.reshape(B, dil, H, L).transpose(0, 3, 1, 2).reshape(B, S, H))
    w = jax.nn.softmax(jnp.stack(lses, 0), axis=0)
    return (w[..., None] * jnp.stack(outs, 0)).sum(0).astype(q.dtype)

def native_sparse_attention(q, kc_tok, vc_tok, ks, vs, kw, vw, gates, positions,
                            cmp_pe, cmp_w1, cmp_b1, cmp_w2, cmp_b2):
    B, S, HN, D = q.shape
    G, HG = NSA_KV_GROUPS, NSA_GROUP
    scale = D ** -0.5
    n_cmp = (S - CMP_BLOCK) // CMP_STRIDE + 1
    n_sel = S // SEL_BLOCK
    k_sel = min(N_SELECT, n_sel)
    nb = S // QBLK

    cidx = np.arange(n_cmp)[:, None] * CMP_STRIDE + np.arange(CMP_BLOCK)[None, :]

    def compress(tok, j):
        blk = tok[:, cidx] + cmp_pe[j][None, None, :, None, :]
        flat = blk.transpose(0, 1, 3, 2, 4).reshape(B, n_cmp, G, CMP_BLOCK * D)
        hdn = jax.nn.gelu(flat @ cmp_w1[j] + cmp_b1[j])
        return hdn @ cmp_w2[j] + cmp_b2[j]

    pos_c = (positions[:, cidx[:, 0]] + positions[:, cidx[:, -1]]).astype(jnp.float32) * 0.5
    cos_c, sin_c = rope_tables(pos_c)
    kc = apply_rope(compress(kc_tok, 0), cos_c, sin_c).transpose(0, 2, 1, 3)
    vc = compress(vc_tok, 1).transpose(0, 2, 1, 3)
    cmp_end = jnp.asarray(cidx[:, -1])

    c_lo, c_hi = cidx[:, 0][:, None], cidx[:, -1][:, None]
    s_lo = (np.arange(n_sel) * SEL_BLOCK)[None, :]
    overlap = jnp.asarray(((c_lo <= s_lo + SEL_BLOCK - 1) & (c_hi >= s_lo)).astype(np.float32))
    sel_start = jnp.arange(n_sel) * SEL_BLOCK

    ks_blocks = ks.transpose(0, 2, 1, 3).reshape(B, G, n_sel, SEL_BLOCK, D)
    vs_blocks = vs.transpose(0, 2, 1, 3).reshape(B, G, n_sel, SEL_BLOCK, D)
    pad_w = ((0, 0), (0, 0), (NSA_WINDOW, 0), (0, 0))
    kw_pad = jnp.pad(kw.transpose(0, 2, 1, 3), pad_w)
    vw_pad = jnp.pad(vw.transpose(0, 2, 1, 3), pad_w)
    qg = q.reshape(B, S, G, HG, D).transpose(0, 2, 3, 1, 4)
    gg = gates.reshape(B, S, G, HG, N_NSA_BRANCHES).transpose(0, 2, 3, 1, 4)
    gather_blocks = jax.vmap(jax.vmap(lambda kb, ix: kb[ix]))

    def block_fn(i):
        t0 = i * QBLK
        t = t0 + jnp.arange(QBLK)
        qb = lax.dynamic_slice_in_dim(qg, t0, QBLK, axis=3)
        gb = lax.dynamic_slice_in_dim(gg, t0, QBLK, axis=3)
        s = jnp.einsum('bghqd,bgnd->bghqn', qb, kc) * scale
        p_cmp = masked_softmax(s, cmp_end[None, :] <= t[:, None])
        o_cmp = jnp.einsum('bghqn,bgnd->bghqd', p_cmp, vc)
        imp = p_cmp.sum(2) @ overlap
        valid = sel_start[None, :] <= t[:, None]
        cur = t // SEL_BLOCK
        jj = jnp.arange(n_sel)[None, :]
        forced = (jj == 0) | (jj == cur[:, None]) | (jj == cur[:, None] - 1)
        score = jnp.where(valid, imp + jnp.where(forced, FORCE_BONUS, 0.0), NEG)
        _, sel = lax.top_k(score, k_sel)
        sel_valid = jnp.take_along_axis(jnp.broadcast_to(valid, score.shape), sel, axis=-1)
        ks_g = gather_blocks(ks_blocks, sel).reshape(B, G, QBLK, k_sel * SEL_BLOCK, D)
        vs_g = gather_blocks(vs_blocks, sel).reshape(B, G, QBLK, k_sel * SEL_BLOCK, D)
        kpos = sel[..., None] * SEL_BLOCK + jnp.arange(SEL_BLOCK)
        smask = (sel_valid[..., None] & (kpos <= t[:, None, None])).reshape(B, G, QBLK, k_sel * SEL_BLOCK)
        s = jnp.einsum('bghqd,bgqkd->bghqk', qb, ks_g) * scale
        p = masked_softmax(s, smask[:, :, None])
        o_slc = jnp.einsum('bghqk,bgqkd->bghqd', p, vs_g)
        kwb = lax.dynamic_slice_in_dim(kw_pad, t0, QBLK + NSA_WINDOW, axis=2)
        vwb = lax.dynamic_slice_in_dim(vw_pad, t0, QBLK + NSA_WINDOW, axis=2)
        kpos_w = t0 - NSA_WINDOW + jnp.arange(QBLK + NSA_WINDOW)
        dist = t[:, None] - kpos_w[None, :]
        wmask = (dist >= 0) & (dist < NSA_WINDOW) & (kpos_w[None, :] >= 0)
        s = jnp.einsum('bghqd,bgkd->bghqk', qb, kwb) * scale
        p = masked_softmax(s, wmask)
        o_win = jnp.einsum('bghqk,bgkd->bghqd', p, vwb)
        return gb[..., 0:1] * o_cmp + gb[..., 1:2] * o_slc + gb[..., 2:3] * o_win

    out = lax.map(block_fn, jnp.arange(nb))
    return out.transpose(1, 0, 4, 2, 3, 5).reshape(B, S, HN, D).astype(q.dtype)

def split_in_proj(proj):
    sizes = (D_DIL, D_DIL, D_DIL, D_NSA, KV_W, KV_W, KV_W, KV_W, KV_W, KV_W,
             N_HEADS_NSA * N_NSA_BRANCHES)
    offs = [int(o) for o in np.cumsum(sizes)[:-1]]
    return jnp.split(proj, offs, axis=-1)

def hybrid_mixer(h, cos, sin, positions, w_in, gate_b, cmp_pe, cmp_w1, cmp_b1, cmp_w2, cmp_b2, w_out):
    B, S, _ = h.shape
    proj = h @ w_in
    qa, ka, va, qn, kc, vc, ks, vs, kw, vw, g = split_in_proj(proj)

    def heads(t, n):
        return t.reshape(B, S, n, HEAD_DIM)

    out_a = dilated_attention(apply_rope(heads(qa, N_HEADS_DIL), cos, sin),
                              apply_rope(heads(ka, N_HEADS_DIL), cos, sin),
                              heads(va, N_HEADS_DIL))
    gates = jax.nn.sigmoid((g + gate_b).astype(jnp.float32)).reshape(B, S, N_HEADS_NSA, N_NSA_BRANCHES)
    out_b = native_sparse_attention(
        apply_rope(heads(qn, N_HEADS_NSA), cos, sin),
        heads(kc, NSA_KV_GROUPS), heads(vc, NSA_KV_GROUPS),
        apply_rope(heads(ks, NSA_KV_GROUPS), cos, sin), heads(vs, NSA_KV_GROUPS),
        apply_rope(heads(kw, NSA_KV_GROUPS), cos, sin), heads(vw, NSA_KV_GROUPS),
        gates, positions, cmp_pe, cmp_w1, cmp_b1, cmp_w2, cmp_b2)
    mixed = jnp.concatenate([out_a, out_b.astype(out_a.dtype)], axis=2).reshape(B, S, D_MODEL)
    return (mixed @ w_out).astype(h.dtype)

def setup_inputs(seed: int = 0) -> dict:
    key = jax.random.key(seed)
    ks = jax.random.split(key, 24)
    beta = (8.0 * DEPTH) ** -0.25
    nrm = jax.random.normal
    f32 = jnp.float32
    return {
        "x": nrm(ks[0], (BATCH, SEQ, D_MODEL), f32),
        "positions": jnp.broadcast_to(jnp.arange(SEQ, dtype=jnp.int32), (BATCH, SEQ)),
        "ln1_g": 1.0 + 0.02 * nrm(ks[1], (DEPTH, D_MODEL), f32),
        "ln1_b": 0.02 * nrm(ks[2], (DEPTH, D_MODEL), f32),
        "ffn1_w1": nrm(ks[3], (DEPTH, D_MODEL, D_FF), f32) * D_MODEL ** -0.5,
        "ffn1_w3": nrm(ks[4], (DEPTH, D_MODEL, D_FF), f32) * D_MODEL ** -0.5,
        "ffn1_w2": nrm(ks[5], (DEPTH, D_FF, D_MODEL), f32) * D_FF ** -0.5 * beta,
        "w_in": nrm(ks[6], (DEPTH, D_MODEL, IN_COLS), f32) * D_MODEL ** -0.5,
        "gate_b": 0.1 * nrm(ks[7], (DEPTH, N_HEADS_NSA * N_NSA_BRANCHES), f32),
        "cmp_pe": 0.1 * nrm(ks[8], (DEPTH, 2, CMP_BLOCK, HEAD_DIM), f32),
        "cmp_w1": nrm(ks[9], (DEPTH, 2, CMP_BLOCK * HEAD_DIM, CMP_HIDDEN), f32) * (CMP_BLOCK * HEAD_DIM) ** -0.5,
        "cmp_b1": 0.02 * nrm(ks[10], (DEPTH, 2, CMP_HIDDEN), f32),
        "cmp_w2": nrm(ks[11], (DEPTH, 2, CMP_HIDDEN, HEAD_DIM), f32) * CMP_HIDDEN ** -0.5,
        "cmp_b2": 0.02 * nrm(ks[12], (DEPTH, 2, HEAD_DIM), f32),
        "w_out": nrm(ks[13], (DEPTH, D_MODEL, D_MODEL), f32) * D_MODEL ** -0.5 * beta,
        "ln2_g": 1.0 + 0.02 * nrm(ks[14], (DEPTH, D_MODEL), f32),
        "ln2_b": 0.02 * nrm(ks[15], (DEPTH, D_MODEL), f32),
        "ffn2_w1": nrm(ks[16], (DEPTH, D_MODEL, D_FF), f32) * D_MODEL ** -0.5,
        "ffn2_w3": nrm(ks[17], (DEPTH, D_MODEL, D_FF), f32) * D_MODEL ** -0.5,
        "ffn2_w2": nrm(ks[18], (DEPTH, D_FF, D_MODEL), f32) * D_FF ** -0.5 * beta,
        "ln3_g": 1.0 + 0.02 * nrm(ks[19], (DEPTH, D_MODEL), f32),
        "ln3_b": 0.02 * nrm(ks[20], (DEPTH, D_MODEL), f32),
    }

def reference(x, positions, ln1_g, ln1_b, ffn1_w1, ffn1_w3, ffn1_w2, w_in, gate_b,
              cmp_pe, cmp_w1, cmp_b1, cmp_w2, cmp_b2, w_out, ln2_g, ln2_b,
              ffn2_w1, ffn2_w3, ffn2_w2, ln3_g, ln3_b):
    alpha = (2.0 * DEPTH) ** 0.25
    cos, sin = rope_tables(positions.astype(jnp.float32))
    h = x
    for l in range(DEPTH):
        h = layer_norm(alpha * h + 0.5 * swiglu(h, ffn1_w1[l], ffn1_w3[l], ffn1_w2[l]), ln1_g[l], ln1_b[l])
        mix = hybrid_mixer(h, cos, sin, positions, w_in[l], gate_b[l], cmp_pe[l], cmp_w1[l],
                           cmp_b1[l], cmp_w2[l], cmp_b2[l], w_out[l])
        h = layer_norm(alpha * h + mix, ln2_g[l], ln2_b[l])
        h = layer_norm(alpha * h + 0.5 * swiglu(h, ffn2_w1[l], ffn2_w3[l], ffn2_w2[l]), ln3_g[l], ln3_b[l])
    return h


_drawn_inputs = setup_inputs


def setup_inputs(seed=0):
    import zlib

    import numpy as np

    out = dict(_drawn_inputs(seed))
    spreads = {}
    factors = {'ln1_g': 2.674,
     'gate_b': 8.0,
     'cmp_pe': 5.36,
     'cmp_b1': 36.083,
     'cmp_b2': 29.485,
     'ln2_g': 2.756,
     'ln2_b': 2.716,
     'ln3_g': 8.485,
     'ln3_b': 8.364,
     'ln1_b': 4.588}
    for name, (base, spread) in spreads.items():
        noise = np.random.default_rng([zlib.crc32(name.encode()), seed]).standard_normal(out[name].shape)
        drawn = base * np.exp(spread * noise) if base else spread * noise
        out[name] = jnp.asarray(drawn.astype(out[name].dtype))
    for name, factor in factors.items():
        out[name] = (out[name] * factor).astype(out[name].dtype)
    return out
```

```python
from contextlib import ExitStack

import concourse.bass as bass
from concourse import mybir

F32 = mybir.dt.float32
F32R = mybir.dt.float32r
I32 = mybir.dt.int32
ALU = mybir.AluOpType
ACT = mybir.ActivationFunctionType
AX = mybir.AxisListType

P = 128
SEQ = 256
NT = SEQ // P
DM = 2048
KT = DM // P
DFF = 5632
FT = DFF // P
HD = 128
N_DIL = 6
N_NSA = 10
KV_GROUPS = 2
NSA_GROUP = N_NSA // KV_GROUPS
N_BRANCH = 3
N_GATE = N_NSA * N_BRANCH
CMP_BLOCK = 32
CMP_STRIDE = 16
CMP_HIDDEN = 256
N_CMP = (SEQ - CMP_BLOCK) // CMP_STRIDE + 1
ROWS_CMP = KV_GROUPS * N_CMP
IN_COLS = 5150
GATE_COL = IN_COLS - N_GATE
SCALE = float(HD) ** -0.5
ALPHA = 2.0 ** 0.25
EPS = 1e-5

BK = 4
BN = 512
STAGES = 4
SPLITS = 2
UP_COLS = BN // 2
UP_CHUNKS = DFF // UP_COLS
UP_F = UP_COLS // P
DOWN_CHUNKS = DM // BN
PROJ_CHUNKS = 10
OUT_CHUNKS = DM // BN
DOWN_K = [4] * 8 + [3] * 4
DOWN_BLOCKS = len(DOWN_K)
assert sum(DOWN_K) == FT and DOWN_BLOCKS % STAGES == 0 and KT // BK == STAGES

Q_UP1 = 0
Q_DOWN1 = Q_UP1 + UP_CHUNKS
Q_PROJ = Q_DOWN1 + DOWN_CHUNKS * DOWN_BLOCKS // STAGES
Q_OUT = Q_PROJ + PROJ_CHUNKS
Q_UP2 = Q_OUT + OUT_CHUNKS
Q_DOWN2 = Q_UP2 + UP_CHUNKS
Q_END = Q_DOWN2 + DOWN_CHUNKS * DOWN_BLOCKS // STAGES

PROJ_FROM = [3584, 4096, 4608, 2048, 2560, 3072, 0, 512, 1024, 1536]
COL_KC, COL_VC, COL_KS, COL_VS, COL_KW, COL_VW = range(0, 1536, 256)
COL_VA_TAIL, COL_QN, COL_QA, COL_KA, COL_VA = 1536, 1792, 3072, 3840, 4608
PROJ_COLS = PROJ_CHUNKS * BN
ROPE_RUNS = [(1, COL_KS, 2), (2, COL_KW, 2), (3, COL_QN, 2), (4, 2048, 4), (5, 2560, 4),
             (6, 3072, 4), (7, 3584, 4), (8, 4096, 4)]
TURNED = [COL_KS, COL_KS + HD, COL_KW, COL_KW + HD] + list(range(COL_QN, COL_VA, HD))
T_KS, T_KW, T_QN, T_QA, T_KA = 0, 2, 4, 14, 20
CMP_K = 8
CMP_BLOCKS = 2 * CMP_BLOCK // CMP_K

TWO_PI_1, TWO_PI_2 = 6.28125, 0.0019350051879882812
TWO_PI_3 = 6.283185307179586 - TWO_PI_1 - TWO_PI_2
PI = 3.1415925
MAGIC = 12582912.0

UNITS = [(h, t, "dil") for h in range(N_DIL) for t in range(NT)]
UNITS += [(N_DIL + h, t, b) for h in range(N_NSA) for t in range(NT) for b in ("slc", "win")]
NU = len(UNITS)
HEAD_LAST = {h: max(u for u in range(NU) if UNITS[u][0] == h) for h in range(N_DIL + N_NSA)}
LAG_TURN, LAG_PV = 3, 4
E_RING = 4
STEP_CMP_OUT, STEP_CMP_TURN, STEP_CMP_SCORE = 1, 5, 7


def layer(nc, x, positions, ln1_g, ln1_b, ffn1_w1, ffn1_w3, ffn1_w2, w_in, gate_b, cmp_pe, cmp_w1,
          cmp_b1, cmp_w2, cmp_b2, w_out, ln2_g, ln2_b, ffn2_w1, ffn2_w3, ffn2_w2, ln3_g, ln3_b,
          inv_freq, dil_mask, causal_mask, cmp_mask, out):
    base = (nc.sbuf_base + 63) // 64 * 64

    def at(name, shape, dt, offset):
        return nc.alloc_sbuf_tensor_at(name, shape, dt, offset=base + offset)

    o = 0
    resid = at("resid", [P, NT, DM], F32, o)
    o += NT * DM * 4
    xT_hi = at("xT_hi", [P, KT, SEQ], F32R, o)
    xT_lo = at("xT_lo", [P, KT, SEQ], F32R, o + KT * SEQ * 4)
    ln3_g_bc = at("ln3_g_bc", [P, DM], F32, o)
    ln3_b_bc = at("ln3_b_bc", [P, DM], F32, o + DM * 4)
    o += 2 * KT * SEQ * 4
    HT = o
    hT_hi = at("hT_hi", [P, FT, SEQ], F32R, HT)
    hT_lo = at("hT_lo", [P, FT, SEQ], F32R, HT + FT * SEQ * 4)
    o += 2 * FT * SEQ * 4
    LN_BC2 = o - 2 * BN * 4
    stage = at("stage", [P, STAGES, BK, BN], F32, o)
    o += STAGES * BK * BN * 4
    w_hi = at("w_hi", [P, SPLITS, BK, BN], F32R, o)
    o += SPLITS * BK * BN * 4
    w_lo = at("w_lo", [P, SPLITS, BK, BN], F32R, o)
    o += SPLITS * BK * BN * 4
    SMALL = o
    silu = at("silu", [P, NT, UP_COLS], F32, o)
    gated = at("gated", [P, NT, UP_COLS], F32, o + 2048)
    turned_f32 = at("turned_f32", [P, 2, BN], F32, o)
    dmask = at("dmask", [P, SEQ], F32, o)
    cmask = at("cmask", [P, SEQ], F32, o + 1024)
    cmpm = at("cmpm", [P, 2, NT, N_CMP], F32, o + 2048)
    gates = at("gates", [P, NT, N_GATE], F32, o + 2304)
    gate_b_bc = at("gate_b_bc", [P, N_GATE], F32, o + 2560)
    rowmax = at("rowmax", [P, NU], F32, o + 2688)
    negmax = at("negmax", [P, NU], F32, o + 2912)
    rowsum = at("rowsum", [P, NU], F32, o + 3136)
    rinv = at("rinv", [P, NU], F32, o + 3360)
    wrow = at("wrow", [P, NU], F32, o + 3584)
    o += 4096
    ident = at("ident", [P, P], F32, o)
    o += 512
    vecs = at("vecs", [P, P], F32, o)
    vecsT = at("vecsT", [P, P], F32, o + 512)
    o += 1024
    cos_t = at("cos_t", [P, NT, HD // 2], F32, o)
    sin_t = at("sin_t", [P, NT, HD // 2], F32, o + 512)
    o += 1024
    cos_c = at("cos_c", [P, 2, HD // 2], F32, o)
    o += 512
    bn = at("bn", [P, NT, DM // BN, 6], F32, o)
    o += 192
    mv = at("mv", [P, NT, 2], F32, o)
    std = at("std", [P, NT], F32, o + 32)
    rstd = at("rstd", [P, NT], F32, o + 64)
    nmr = at("nmr", [P, NT], F32, o + 96)
    eps_t = at("eps_t", [P, 1], F32, o + 128)
    b1T = at("b1T", [P, 4], F32, o + 160)
    o += 192
    assert base + o <= nc.sbuf_usable_end

    o = HT
    proj = at("proj", [P, NT, PROJ_COLS], F32, o)
    o += NT * PROJ_COLS * 4
    FREE = o
    cstage = at("cstage", [P, CMP_K, CMP_HIDDEN], F32, o)
    c_hi = at("c_hi", [P, CMP_K, CMP_HIDDEN], F32R, o + 8192)
    c_lo = at("c_lo", [P, CMP_K, CMP_HIDDEN], F32R, o + 16384)
    wg = at("wg", [P, KT, N_GATE], F32, o)
    wg_hi = at("wg_hi", [P, KT, N_GATE], F32R, o + 8192)
    wg_lo = at("wg_lo", [P, KT, N_GATE], F32R, o + 16384)
    o += 24576
    tokT = at("tokT", [P, 4, SEQ], F32, o)
    o += 4096
    flat_hi = at("flat_hi", [P, 2 * CMP_BLOCK, ROWS_CMP], F32R, o)
    flat_lo = at("flat_lo", [P, 2 * CMP_BLOCK, ROWS_CMP], F32R, o + 7680)
    o += 15360
    flat = at("flat", [P, CMP_BLOCK, ROWS_CMP], F32, FREE)
    bc1 = at("bc1", [P, 2, BN], F32, o)
    rt = at("rt", [P, 2, 2, 2, HD // 2], F32, o)
    hid_part = at("hid_part", [P, CMP_BLOCKS, 2, ROWS_CMP], F32, o + 2048)
    o += 4096
    assert o <= HT + 2 * FT * SEQ * 4
    o = FREE
    qkT = at("qkT", [P, len(TURNED), SEQ], F32, o)
    o += len(TURNED) * SEQ * 4
    masked = at("masked", [P, 2, SEQ], F32, o)
    o += 2048
    probs = at("probs", [P, E_RING, SEQ], F32, o)
    o += E_RING * SEQ * 4
    probsT = at("probsT", [P, 2, NT, P], F32, o)
    o += 2048
    csc = at("csc", [P, NT, N_NSA, N_CMP], F32, o)
    cex = at("cex", [P, NT, N_NSA, N_CMP], F32, o + 1216)
    cpr = at("cpr", [P, NT, N_NSA, N_CMP], F32, o + 2432)
    cst = at("cst", [P, 4, NT, N_NSA], F32, o + 3648)
    o += 3968
    hidT = at("hidT", [P, 2, 2, ROWS_CMP], F32, o)
    hid_sum = at("hid_sum", [P, 2, 2, ROWS_CMP], F32, o + 480)
    o += 960
    kcT = at("kcT", [P, KV_GROUPS, N_CMP], F32, o)
    o += 128
    cw2 = at("cw2", [P, 4, HD], F32, o)
    o += 2048
    cprT = at("cprT", [N_CMP, 2, P], F32, o)
    o += 1024
    assert o <= FREE + 44032 + 2048
    kvc = at("kvc", [N_CMP, 4, HD], F32, o)
    b2_bc = at("b2_bc", [N_CMP, 2, HD], F32, o + 2048)
    crt = at("crt", [N_CMP, 2, KV_GROUPS, 2, HD // 2], F32, o + 3072)
    o += 5120
    assert o <= HT + 2 * FT * SEQ * 4
    bc2 = at("bc2", [P, 2, BN], F32, LN_BC2)
    pos_i = at("pos_i", [P, NT + 2], I32, HT)
    pos_f = at("pos_f", [P, NT + 2], F32, HT + 32)
    invf_bc = at("invf_bc", [P, HD // 2], F32, HT + 64)
    ang = at("ang", [P, 3, HD // 2], F32, HT + 1024)
    turns = at("turns", [P, 3, HD // 2], F32, HT + 2048)
    red = at("red", [P, 2, 3, HD // 2], F32, HT + 3072)
    b1rows = at("b1rows", [4, P], F32, HT + 5120)

    with ExitStack() as ctx:
        bank = [ctx.enter_context(nc.psum_tensor(f"bank{i}", [P, 512], F32)) for i in range(8)]

        def sem(name):
            return ctx.enter_context(nc.semaphore(name))

        stage_full = [sem(f"stage_full{s}") for s in range(STAGES)]
        hi_ready, lo_ready, block_used = sem("hi_ready"), sem("lo_ready"), sem("block_used")
        x_loaded = [sem(f"x_loaded{q}") for q in range(4)]
        vecs_loaded, pos_loaded = sem("vecs_loaded"), sem("pos_loaded")
        attn_loaded, wg_loaded, bc_loaded = sem("attn_loaded"), sem("wg_loaded"), sem("bc_loaded")
        cstage_full, cw2_loaded, ln3_loaded = sem("cstage_full"), sem("cw2_loaded"), sem("ln3_loaded")
        out_stored = sem("out_stored")
        ident_ready, vecs_turned, vecs_ready = sem("ident_ready"), sem("vecs_turned"), sem("vecs_ready")
        pos_step, red_ready, trig_ready = sem("pos_step"), sem("red_ready"), sem("trig_ready")
        in_turned, in_full, in_hi, in_ready = sem("in_turned"), sem("in_full"), sem("in_hi"), sem("in_ready")
        stat_step, aggr_ready, std_ready, rstd_ready, z_ready = (
            sem("stat_step"), sem("aggr_ready"), sem("std_ready"), sem("rstd_ready"), sem("z_ready"))
        resid_step, resid_ready = sem("resid_step"), sem("resid_ready")
        silu_ready, gated_ready, hid_turned, hT_hi_ready, hT_ready = (
            sem("silu_ready"), sem("gated_ready"), sem("hid_turned"), sem("hT_hi_ready"), sem("hT_ready"))
        down_added, out_added = sem("down_added"), sem("out_added")
        proj_copied_a, proj_copied_v, wg_hi_ready, wg_ready, gate_summed, gate_biased, gates_ready = (
            sem("proj_copied_a"), sem("proj_copied_v"), sem("wg_hi_ready"), sem("wg_ready"), sem("gate_summed"), sem("gate_biased"),
            sem("gates_ready"))
        tok_turned, tok_copied, flat_step, flat_ready = (
            sem("tok_turned"), sem("tok_copied"), sem("flat_step"), sem("flat_ready"))
        c_hi_ready, c_lo_ready, c_used, hid_copied = (
            sem("c_hi_ready"), sem("c_lo_ready"), sem("c_used"), sem("hid_copied"))
        rope_step, roped = sem("rope_step"), sem("roped")
        qk_turned, qk_even, qk_odd = sem("qk_turned"), sem("qk_even"), sem("qk_odd")
        hid_step, hid_sum_ready, hidT_ready, kvc_summed, kvc_step, kvc_ready = (
            sem("hid_step"), sem("hid_sum_ready"), sem("hidT_ready"), sem("kvc_summed"), sem("kvc_step"),
            sem("kvc_ready"))
        kc_turned, kcT_ready, cmp_scored, cmp_step, cmp_shifted, cmp_exp, cmp_ready = (
            sem("kc_turned"), sem("kcT_ready"), sem("cmp_scored"), sem("cmp_step"), sem("cmp_shifted"),
            sem("cmp_exp"), sem("cmp_ready"))
        scored, masked_ready, negmax_ready, exp_ready, inv_ready, probs_ready = (
            sem("scored"), sem("masked_ready"), sem("negmax_ready"), sem("exp_ready"), sem("inv_ready"),
            sem("probs_ready"))
        probs_turned, probsT_ready, cmpT_ready, valued = (
            sem("probs_turned"), sem("probsT_ready"), sem("cmpT_ready"), sem("valued"))
        head_done, mix_hi_ready, mix_ready = sem("head_done"), sem("mix_hi_ready"), sem("mix_ready")
        final_g, final_b = sem("final_g"), sem("final_b")

        block = ctx.enter_context(nc.Block())

        def rows(w, kt, n):
            return w[kt * P:(kt + n) * P, :].rearrange("(k p) n -> p k n", p=P)

        @block.sync
        def _(sp):
            def slot_free(q, s):
                if not (isinstance(q, int) and q == 0):
                    sp.wait_ge(lo_ready, 4 * q + s - 3)

            def load_up(w1, w3, q, c):
                for s in range(STAGES):
                    slot_free(q, s)
                    for half, w in enumerate((w1, w3)):
                        sp.dma_start(stage[:, s, :, half * UP_COLS:(half + 1) * UP_COLS],
                                     rows(w, s * BK, BK)[:, :, bass.ds(c * UP_COLS, UP_COLS)]
                                     ).then_inc(stage_full[s], 16)

            def load_block(w, q, s, kt, n, col):
                slot_free(q, s)
                for a, b in ((0, 2), (2, n)):
                    sp.dma_start(stage[:, s, a:b, :], rows(w, kt + a, b - a)[:, :, bass.ds(col, BN)]
                                 ).then_inc(stage_full[s], 16)

            def load_down(w2, q0):
                with sp.Fori(0, DOWN_CHUNKS) as n:
                    for b, k in enumerate(DOWN_K):
                        load_block(w2, q0 + n * (DOWN_BLOCKS // STAGES) + b // STAGES, b % STAGES,
                                   sum(DOWN_K[:b]), k, n * BN)

            for q in range(4):
                sp.dma_start(resid[:, :, q * BN:(q + 1) * BN],
                             x[0].rearrange("(t p) n -> p t n", p=P)[:, :, q * BN:(q + 1) * BN]
                             ).then_inc(x_loaded[q], 16)
            load_up(ffn1_w1[0], ffn1_w3[0], 0, 0)
            with sp.Fori(1, UP_CHUNKS) as c:
                load_up(ffn1_w1[0], ffn1_w3[0], Q_UP1 + c, c)
            load_down(ffn1_w2[0], Q_DOWN1)
            for p in range(PROJ_CHUNKS):
                for s in range(STAGES):
                    load_block(w_in[0], Q_PROJ + p, s, s * BK, BK, PROJ_FROM[p])
                    if s == 1 and p >= 2:
                        cb = p - 2
                        if cb == 0:
                            sp.wait_ge(flat_ready, 2)
                        else:
                            sp.wait_ge(c_lo_ready, cb)
                        sp.dma_start(cstage[:, :, :],
                                     cmp_w1[0, cb // 4][(cb % 4) * CMP_K * P:(cb % 4 + 1) * CMP_K * P, :]
                                     .rearrange("(k p) n -> p k n", p=P)).then_inc(cstage_full, 16)
            with sp.Fori(0, OUT_CHUNKS) as n:
                for s in range(STAGES):
                    load_block(w_out[0], Q_OUT + n, s, s * BK, BK, n * BN)
            with sp.Fori(0, UP_CHUNKS) as c:
                load_up(ffn2_w1[0], ffn2_w3[0], Q_UP2 + c, c)
            load_down(ffn2_w2[0], Q_DOWN2)
            for q in range(4):
                for t in range(NT):
                    sp.wait_ge(final_b, q * NT + t + 1)
                    sp.dma_start(out[0, t * P:(t + 1) * P, q * BN:(q + 1) * BN],
                                 resid[:, t, q * BN:(q + 1) * BN]).then_inc(out_stored, 16)
            sp.wait_ge(out_stored, 16 * 4 * NT)

        @block.tensor
        def _(pe):
            def product(acc, a, b, start, stop):
                pe.matmul(acc, a[0], b[0], start=start, stop=False)
                pe.matmul(acc, a[0], b[1], start=False, stop=False)
                return pe.matmul(acc, a[1], b[0], start=False, stop=stop)

            def split_block(accs, src, q, s, kt, n, first, last):
                pe.wait_ge(lo_ready, 4 * q + s + 1)
                for k in range(n):
                    for t in range(NT):
                        col = slice(t * P, (t + 1) * P)
                        mm = product(accs[t][:, :], (src[0][:, kt + k, col], src[1][:, kt + k, col]),
                                     (w_hi[:, s % 2, k, :], w_lo[:, s % 2, k, :]),
                                     first and k == 0, last and k == n - 1)
                mm.then_inc(block_used, 1)

            xT, hT = (xT_hi, xT_lo), (hT_hi, hT_lo)
            A, B = bank[0:2], bank[2:4]
            T = bank[4]

            def turn_input(n0, src_ready):
                for j in range(KT // 2):
                    n = n0 + j
                    if j % 2 == 0:
                        src_ready(j // 2)
                    if n >= 2:
                        pe.wait_ge(in_full, n - 1)
                    for k in range(2):
                        for t in range(NT):
                            mm = pe.transpose(bank[5 + n % 2][:, k * SEQ + t * P:k * SEQ + (t + 1) * P],
                                              resid[:, t, (2 * j + k) * P:(2 * j + k + 1) * P], ident[:, :])
                    mm.then_inc(in_turned, 1)

            def turn_hidden(m):
                pe.wait_ge(gated_ready, m + 1)
                pe.wait_ge(hT_ready, m + 1)
                for f in range(UP_F):
                    for t in range(NT):
                        mm = pe.transpose(T[:, f * SEQ + t * P:f * SEQ + (t + 1) * P],
                                          gated[:, t, f * P:(f + 1) * P], ident[:, :])
                mm.then_inc(hid_turned, 1)

            def up_chunk(q, accs, m, n0=None):
                for s in range(STAGES):
                    if n0 is not None:
                        pe.wait_ge(in_ready, n0 + 2 * (s + 1))
                    split_block(accs, xT, q, s, s * BK, BK, s == 0, s == STAGES - 1)
                    if s == 0 and n0 is None:
                        turn_hidden(m - 1)

            def up(q0, m0, n0):
                up_chunk(q0, A, m0, n0)
                with pe.Fori(0, (UP_CHUNKS - 2) // 2) as i:
                    up_chunk(q0 + 1 + 2 * i, B, m0 + 1 + 2 * i)
                    up_chunk(q0 + 2 + 2 * i, A, m0 + 2 + 2 * i)
                up_chunk(q0 + UP_CHUNKS - 1, B, m0 + UP_CHUNKS - 1)
                turn_hidden(m0 + UP_CHUNKS - 1)

            def down(q0, m0, d0):
                with pe.Fori(0, DOWN_CHUNKS // 2) as i:
                    for j, accs in enumerate((A, B)):
                        if j == 1:
                            pe.wait_ge(down_added, d0 + 2 * i + 1)
                        for b, k in enumerate(DOWN_K):
                            if j == 0 and b == DOWN_BLOCKS - 1:
                                pe.wait_ge(hT_ready, m0 + UP_CHUNKS + 1)
                            split_block(accs, hT, q0 + (2 * i + j) * (DOWN_BLOCKS // STAGES) + b // STAGES,
                                        b % STAGES, sum(DOWN_K[:b]), k, b == 0, b == DOWN_BLOCKS - 1)
                    pe.wait_ge(down_added, d0 + 2 * i + 2)

            pe.sem_inc(c_used, 1)
            pe.wait_ge(ident_ready, 2)
            pe.wait_ge(vecs_loaded, 16 * 6)
            pe.transpose(bank[7][:, 0:P], vecs[:, :], ident[:, :])
            pe.transpose(bank[7][:, P:P + 4], b1rows[:, :], ident[0:4, 0:4]).then_inc(vecs_turned, 1)
            turn_input(0, lambda q: pe.wait_ge(x_loaded[q], 16))
            up(Q_UP1, 0, 0)
            down(Q_DOWN1, 0, 0)
            turn_input(8, lambda q: pe.wait_ge(z_ready, q + 1))

            def proj_chunk(p, accs, n0=None):
                for s in range(STAGES):
                    if n0 is not None:
                        pe.wait_ge(in_ready, n0 + 2 * (s + 1))
                    split_block(accs, xT, Q_PROJ + p, s, s * BK, BK, s == 0, s == STAGES - 1)

            def compress(cb):
                pe.wait_ge(c_lo_ready, cb + 1)
                pe.wait_ge(hid_copied, cb + 1)
                for half in range(2):
                    hcol = slice(half * P, (half + 1) * P)
                    acc = bank[7][:, half * 32:half * 32 + ROWS_CMP]
                    for k in range(CMP_K):
                        f = (slice(None), bass.ds(cb * CMP_K + k, 1), slice(None))
                        mm = product(acc, (c_hi[:, k, hcol], c_lo[:, k, hcol]),
                                     (flat_hi[f].rearrange("p a n -> p (a n)"),
                                      flat_lo[f].rearrange("p a n -> p (a n)")), k == 0, k == CMP_K - 1)
                mm.then_inc(c_used, 1)

            proj_chunk(0, A, 8)
            split_block(B, xT, Q_PROJ + 1, 0, 0, BK, True, False)
            pe.wait_ge(proj_copied_a, 1)
            pe.wait_ge(proj_copied_v, 1)
            for a in range(4):
                for t in range(NT):
                    mm = pe.transpose(bank[5 + a // 2][:, (a % 2) * SEQ + t * P:(a % 2) * SEQ + (t + 1) * P],
                                      proj[:, t, a * HD:(a + 1) * HD], ident[:, :])
            mm.then_inc(tok_turned, 1)
            split_block(B, xT, Q_PROJ + 1, 1, BK, BK, False, False)
            pe.wait_ge(wg_ready, 1)
            for t in range(NT):
                col = slice(t * P, (t + 1) * P)
                for k in range(KT):
                    mm = product(bank[7][:, t * 32:t * 32 + N_GATE], (xT_hi[:, k, col], xT_lo[:, k, col]),
                                 (wg_hi[:, k, :], wg_lo[:, k, :]), k == 0, k == KT - 1)
            mm.then_inc(gate_summed, 1)
            split_block(B, xT, Q_PROJ + 1, 2, 2 * BK, BK, False, False)
            split_block(B, xT, Q_PROJ + 1, 3, 3 * BK, BK, False, True)
            pe.wait_ge(gate_biased, 1)
            pe.wait_ge(flat_ready, 2)
            with pe.Fori(0, (PROJ_CHUNKS - 2) // 2) as i:
                for j, accs in enumerate((A, B)):
                    pe.wait_ge(proj_copied_a, 2 * i + j + 1)
                    pe.wait_ge(proj_copied_v, 2 * i + j + 1)
                    proj_chunk(2 * i + j + 2, accs)
                    compress(2 * i + j)

            pe.wait_ge(roped, len(ROPE_RUNS))
            pe.wait_ge(hid_copied, CMP_BLOCKS + 1)
            for n in range(len(TURNED) // 2):
                if n >= 2:
                    pe.wait_ge(qk_odd if n % 2 else qk_even, n // 2)
                for a in range(2):
                    for t in range(NT):
                        col = TURNED[2 * n + a]
                        mm = pe.transpose(bank[6 + n % 2][:, a * SEQ + t * P:a * SEQ + (t + 1) * P],
                                          proj[:, t, col:col + HD], ident[:, :])
                mm.then_inc(qk_turned, 1)
            pe.wait_ge(qk_even, 7)
            pe.wait_ge(qk_odd, 6)
            pe.wait_ge(proj_copied_a, PROJ_CHUNKS)
            pe.wait_ge(proj_copied_v, PROJ_CHUNKS)

            def q_slot(h):
                return T_QA + h if h < N_DIL else T_QN + h - N_DIL

            def scores(u):
                h, t, br = UNITS[u]
                k = {"dil": T_KA + h, "slc": T_KS + (h - N_DIL) // NSA_GROUP,
                     "win": T_KW + (h - N_DIL) // NSA_GROUP}[br]
                if u >= 2:
                    pe.wait_ge(masked_ready, u - 1)
                n = (t + 1) * P
                pe.matmul(bank[u % 2][:, 0:n], qkT[:, q_slot(h), t * P:(t + 1) * P], qkT[:, k, 0:n],
                          start=True, stop=True).then_inc(scored, 1)

            def turn_probs(u):
                h, t, br = UNITS[u]
                pe.wait_ge(probs_ready, u + 1)
                if u >= 2:
                    pe.wait_ge(probsT_ready, u - 1)
                for k in range(t + 1):
                    mm = pe.transpose(bank[2 + u % 2][:, k * P:(k + 1) * P],
                                      probs[:, u % E_RING, k * P:(k + 1) * P], ident[:, :])
                if br == "slc":
                    pe.wait_ge(cmp_ready, 1)
                    mm = pe.transpose(bank[2 + u % 2][0:N_CMP, 2 * P:3 * P], cpr[:, t, h - N_DIL, :],
                                      ident[:, :])
                mm.then_inc(probs_turned, 1)

            def values(u):
                h, t, br = UNITS[u]
                if t == 0 and br != "win" and h >= 2:
                    pe.wait_ge(mix_ready, h - 1)
                pe.wait_ge(probsT_ready, u + 1)
                g = (h - N_DIL) // NSA_GROUP
                o = bank[4 + h % 2][:, t * P:(t + 1) * P]
                col = {"dil": COL_VA + h * HD if h < 4 else COL_VA_TAIL + (h - 4) * HD,
                       "slc": COL_VS + g * HD, "win": COL_VW + g * HD}[br]
                if br == "slc":
                    pe.wait_ge(cmpT_ready, 2 * (h - N_DIL) + t + 1)
                    pe.matmul(o, kvc[:, 2 + g, :], cprT[:, t, :], start=True, stop=False)
                for k in range(t + 1):
                    mm = pe.matmul(o, proj[:, k, col:col + HD], probsT[:, u % 2, k, :],
                                   start=(br == "dil" and k == 0), stop=(br != "slc" and k == t))
                mm.then_inc(valued, 1)

            for step in range(NU + LAG_PV):
                if step < NU:
                    scores(step)
                if step == STEP_CMP_OUT:
                    pe.wait_ge(hidT_ready, 4)
                    pe.wait_ge(cw2_loaded, 32)
                    for a in range(4):
                        j, g = a // 2, a % 2
                        for half in range(2):
                            mm = pe.matmul(bank[6][0:N_CMP, a * HD:(a + 1) * HD],
                                           hidT[:, j, half, g * N_CMP:(g + 1) * N_CMP],
                                           cw2[:, 2 * j + half, :], start=(half == 0), stop=(half == 1))
                    mm.then_inc(kvc_summed, 1)
                if step == STEP_CMP_TURN:
                    pe.wait_ge(kvc_ready, 1)
                    for g in range(KV_GROUPS):
                        mm = pe.transpose(bank[7][:, g * N_CMP:(g + 1) * N_CMP], kvc[:, g, :],
                                          ident[0:N_CMP, 0:N_CMP])
                    mm.then_inc(kc_turned, 1)
                if step == STEP_CMP_SCORE:
                    pe.wait_ge(kcT_ready, 1)
                    for t in range(NT):
                        for h in range(N_NSA):
                            c = (t * N_NSA + h) * N_CMP
                            mm = pe.matmul(bank[6][:, c:c + N_CMP], qkT[:, T_QN + h, t * P:(t + 1) * P],
                                           kcT[:, h // NSA_GROUP, :], start=True, stop=True)
                    mm.then_inc(cmp_scored, 1)
                if step >= LAG_TURN and step - LAG_TURN < NU:
                    turn_probs(step - LAG_TURN)
                if step >= LAG_PV:
                    values(step - LAG_PV)

            pe.wait_ge(mix_ready, N_DIL + N_NSA)
            with pe.Fori(0, OUT_CHUNKS // 2) as i:
                for j, accs in enumerate((A, B)):
                    if j == 1:
                        pe.wait_ge(out_added, 2 * i + 1)
                    for s in range(STAGES):
                        split_block(accs, xT, Q_OUT + 2 * i + j, s, s * BK, BK, s == 0, s == STAGES - 1)
                pe.wait_ge(out_added, 2 * i + 2)
            turn_input(16, lambda q: pe.wait_ge(z_ready, 4 + q + 1))
            up(Q_UP2, UP_CHUNKS, 16)
            down(Q_DOWN2, UP_CHUNKS, DOWN_CHUNKS)

        @block.scalar
        def _(act):
            def hi(q, s):
                act.wait_ge(stage_full[s], 32 * q + 32)
                if not (isinstance(q, int) and 4 * q + s < SPLITS):
                    act.wait_ge(block_used, 4 * q + s + 1 - SPLITS)
                act.activation(w_hi[:, s % SPLITS, :, :], stage[:, s, :, :], ACT.Copy).then_inc(hi_ready, 1)

            def full_input(n0, vec):
                for j in range(KT // 2):
                    n = n0 + j
                    act.wait_ge(in_turned, n + 1)
                    if n >= 2:
                        act.wait_ge(in_ready, n - 1)
                    if vec is None:
                        act.activation(turned_f32[:, n % 2, :], bank[5 + n % 2][:, :], ACT.Copy
                                       ).then_inc(in_full, 1)
                        continue
                    for k in range(2):
                        kt = 2 * j + k
                        a = act.activation(turned_f32[:, n % 2, k * SEQ:(k + 1) * SEQ],
                                           bank[5 + n % 2][:, k * SEQ:(k + 1) * SEQ], ACT.Identity,
                                           scale=vecsT[:, vec + kt:vec + kt + 1],
                                           bias=vecsT[:, vec + KT + kt:vec + KT + kt + 1])
                    a.then_inc(in_full, 1)

            def up_step(q, accs, m, m0, turn):
                hi(q, 1)
                hi(q, 2)
                if turn:
                    act.wait_ge(hid_turned, m)
                    act.activation(hT_hi[:, bass.ds(UP_F * (m - 1 - m0), UP_F), :],
                                   bank[4][:, :].rearrange("p (f n) -> p f n", f=UP_F), ACT.Copy
                                   ).then_inc(hT_hi_ready, 1)
                hi(q, 3)
                hi(q + 1, 0)
                act.wait_ge(block_used, 4 * q + 4)
                for t in range(NT):
                    act.activation(silu[:, t, :], accs[t][:, 0:UP_COLS], ACT.Silu).then_inc(silu_ready, 1)

            A, B = bank[0:2], bank[2:4]

            def up(q0, m0):
                up_step(q0, A, m0, m0, False)
                with act.Fori(0, (UP_CHUNKS - 2) // 2) as i:
                    up_step(q0 + 1 + 2 * i, B, m0 + 1 + 2 * i, m0, True)
                    up_step(q0 + 2 + 2 * i, A, m0 + 2 + 2 * i, m0, True)
                m = m0 + UP_CHUNKS - 1
                up_step(q0 + UP_CHUNKS - 1, B, m, m0, True)
                act.wait_ge(hid_turned, m + 1)
                act.activation(hT_hi[:, FT - UP_F:FT, :], bank[4][:, :].rearrange("p (f n) -> p f n", f=UP_F),
                               ACT.Copy).then_inc(hT_hi_ready, 1)

            def std_of(l):
                act.wait_ge(aggr_ready, l + 1)
                act.activation(std[:, :], mv[:, :, 1], ACT.Sqrt, bias=eps_t[:, :]).then_inc(std_ready, 1)

            for t in range(NT):
                act.dma_start(pos_i[:, t:t + 1], positions[0, t * P:(t + 1) * P].rearrange("(p a) -> p a", a=1)
                              ).then_inc(pos_loaded, 16)
            for a, start in enumerate((0, CMP_BLOCK - CMP_STRIDE)):
                tok = positions[0, start:start + N_CMP * CMP_STRIDE].rearrange("(n c) -> n c", c=CMP_STRIDE)
                col = (0, CMP_STRIDE - 1)[a]
                act.dma_start(pos_i[0:N_CMP, NT + a:NT + a + 1], tok[:, col:col + 1],
                              allow_slow_non_contiguous=True).then_inc(pos_loaded, 16)
            act.dma_start(invf_bc[:, :], inv_freq[0:1, :].broadcast_to([P, HD // 2])).then_inc(pos_loaded, 16)
            for r, v in enumerate((ln1_g, ln1_b, ln2_g, ln2_b)):
                act.dma_start(vecs[r * KT:(r + 1) * KT, :], v[0].rearrange("(k p) -> k p", p=P)
                              ).then_inc(vecs_loaded, 16)
            act.dma_start(vecs[4 * KT:P, :], cmp_pe[0].rearrange("j c d -> (j c) d")).then_inc(vecs_loaded, 16)
            act.dma_start(b1rows[:, :], cmp_b1[0].rearrange("j (h p) -> (j h) p", p=P)).then_inc(vecs_loaded, 16)
            act.wait_ge(red_ready, 1)
            act.activation(sin_t[:, :, :], red[:, 0, 0:NT, :], ACT.Sin)
            act.activation(cos_t[:, :, :], red[:, 1, 0:NT, :], ACT.Sin)
            act.activation(cos_c[:, 1, :], red[:, 0, NT, :], ACT.Sin)
            act.activation(cos_c[:, 0, :], red[:, 1, NT, :], ACT.Sin).then_inc(trig_ready, 1)
            full_input(0, None)
            hi(0, 0)

            up(Q_UP1, 0)
            with act.Fori(0, DOWN_CHUNKS) as n:
                for b in range(1, DOWN_BLOCKS + 1):
                    hi(Q_DOWN1 + (DOWN_BLOCKS // STAGES) * n + b // STAGES, b % STAGES)
            std_of(0)
            full_input(8, 0)

            def compress_hi(cb):
                act.wait_ge(cstage_full, 16 * cb + 16)
                act.wait_ge(c_used, cb + 1)
                act.activation(c_hi[:, :, :], cstage[:, :, :], ACT.Copy).then_inc(c_hi_ready, 1)

            def proj_step(p, accs, cb=None):
                hi(Q_PROJ + p, 1)
                hi(Q_PROJ + p, 2)
                if cb is not None:
                    compress_hi(cb)
                hi(Q_PROJ + p, 3)
                hi(Q_PROJ + p + 1, 0)
                act.wait_ge(block_used, 4 * (Q_PROJ + p) + 4)
                act.activation(proj[:, 0, bass.ds(p * BN, BN)], accs[0][:, :], ACT.Copy
                               ).then_inc(proj_copied_a, 1)

            proj_step(0, A)
            proj_step(1, B)
            act.wait_ge(gate_biased, 1)
            act.activation(gates[:, :, :], gates[:, :, :], ACT.Sigmoid).then_inc(gates_ready, 1)
            with act.Fori(0, (PROJ_CHUNKS - 2) // 2) as i:
                proj_step(2 * i + 2, A, 2 * i)
                proj_step(2 * i + 3, B, 2 * i + 1)

            act.wait_ge(hid_sum_ready, 1)
            for j in range(2):
                for half in range(2):
                    act.activation(hidT[:, j, half, :], hid_sum[:, j, half, :], ACT.Gelu_apprx_tanh,
                                   bias=b1T[:, 2 * j + half:2 * j + half + 1]).then_inc(hidT_ready, 1)
            for n in range(1, len(TURNED) // 2, 2):
                act.wait_ge(qk_turned, n + 1)
                act.activation(qkT[:, 2 * n:2 * n + 2, :], bank[7][:, :].rearrange("p (a n) -> p a n", a=2),
                               ACT.Copy).then_inc(qk_odd, 1)

            def exps(u):
                h, t, br = UNITS[u]
                n = (t + 1) * P
                act.wait_ge(negmax_ready, u + 1)
                if u >= E_RING:
                    act.wait_ge(probs_turned, u - E_RING + 1)
                act.activation(probs[:, u % E_RING, 0:n], masked[:, u % 2, 0:n], ACT.Exp,
                               bias=negmax[:, u:u + 1], scale=SCALE, accum_out=rowsum[:, u:u + 1]
                               ).then_inc(exp_ready, 1)

            def take_turned(u):
                h, t, br = UNITS[u]
                act.wait_ge(probs_turned, u + 1)
                if u >= 2:
                    act.wait_ge(valued, u - 1)
                if br == "slc":
                    act.activation(cprT[:, t, :], bank[2 + u % 2][0:N_CMP, 2 * P:3 * P], ACT.Copy
                                   ).then_inc(cmpT_ready, 1)
                act.activation(probsT[:, u % 2, 0:t + 1, :],
                               bank[2 + u % 2][:, 0:(t + 1) * P].rearrange("p (k n) -> p k n", n=P), ACT.Copy
                               ).then_inc(probsT_ready, 1)

            def mix_hi(h):
                act.wait_ge(valued, HEAD_LAST[h] + 1)
                act.activation(xT_hi[:, h, :], bank[4 + h % 2][:, 0:SEQ], ACT.Copy).then_inc(mix_hi_ready, 1)

            for step in range(NU + LAG_PV):
                if step < NU:
                    exps(step)
                if step == STEP_CMP_SCORE + 2:
                    act.wait_ge(cmp_shifted, 1)
                    act.activation(cex[:, :, :, :], csc[:, :, :, :], ACT.Exp, scale=SCALE).then_inc(cmp_exp, 1)
                if step >= LAG_TURN and step - LAG_TURN < NU:
                    take_turned(step - LAG_TURN)
                for h in HEAD_LAST:
                    if HEAD_LAST[h] == step - LAG_PV:
                        mix_hi(h)

            with act.Fori(0, OUT_CHUNKS) as n:
                hi(Q_OUT + n, 1)
                hi(Q_OUT + n, 2)
                hi(Q_OUT + n, 3)
                hi(Q_OUT + n + 1, 0)
            std_of(1)
            full_input(16, 2 * KT)

            up(Q_UP2, UP_CHUNKS)
            for b in range(1, DOWN_CHUNKS * DOWN_BLOCKS):
                hi(Q_DOWN2 + b // STAGES, b % STAGES)
            std_of(2)
            act.wait_ge(rstd_ready, 3)
            for q in range(4):
                for t in range(NT):
                    piece = resid[:, t, q * BN:(q + 1) * BN]
                    act.activation(piece, piece, ACT.Identity, scale=rstd[:, t:t + 1], bias=nmr[:, t:t + 1]
                                   ).then_inc(z_ready, 1)

        @block.vector
        def _(dve):
            A, B = bank[0:2], bank[2:4]

            def lo(q, s):
                dve.wait_ge(hi_ready, 4 * q + s + 1)
                dve.tensor_tensor(w_lo[:, s % SPLITS, :, :], stage[:, s, :, :], w_hi[:, s % SPLITS, :, :],
                                  ALU.subtract).then_inc(lo_ready, 1)

            def split_input(n0):
                for j in range(KT // 2):
                    n = n0 + j
                    src = turned_f32[:, n % 2, :].rearrange("p (k n) -> p k n", k=2)
                    dve.wait_ge(in_full, n + 1)
                    dve.tensor_copy(xT_hi[:, 2 * j:2 * j + 2, :], src).then_inc(in_hi, 1)
                    dve.wait_ge(in_hi, n + 1)
                    dve.tensor_tensor(xT_lo[:, 2 * j:2 * j + 2, :], src, xT_hi[:, 2 * j:2 * j + 2, :],
                                      ALU.subtract).then_inc(in_ready, 1)

            def hidden_lo(m, f):
                dve.wait_ge(hT_hi_ready, m + 1)
                part = (slice(None), bass.ds(f, UP_F), slice(None))
                dve.tensor_tensor(hT_lo[part], bank[4][:, :].rearrange("p (f n) -> p f n", f=UP_F),
                                  hT_hi[part], ALU.subtract).then_inc(hT_ready, 1)

            def up_step(q, accs, m, m0, turn):
                lo(q, 1)
                lo(q, 2)
                if turn:
                    hidden_lo(m - 1, UP_F * (m - 1 - m0))
                lo(q, 3)
                lo(q + 1, 0)
                for t in range(NT):
                    dve.wait_ge(silu_ready, 2 * m + t + 1)
                    g = dve.tensor_tensor(gated[:, t, :], silu[:, t, :], accs[t][:, UP_COLS:BN], ALU.mult)
                g.then_inc(gated_ready, 1)

            def up(q0, m0, r):
                up_step(q0, A, m0, m0, False)
                with dve.Fori(0, (UP_CHUNKS - 2) // 2) as i:
                    up_step(q0 + 1 + 2 * i, B, m0 + 1 + 2 * i, m0, True)
                    up_step(q0 + 2 + 2 * i, A, m0 + 2 + 2 * i, m0, True)
                dve.wait_ge(resid_ready, r)
                m = m0 + UP_CHUNKS - 1
                up_step(q0 + UP_CHUNKS - 1, B, m, m0, True)
                hidden_lo(m, FT - UP_F)

            def add(accs, q_end, n, factor, added, a0, s0):
                dve.wait_ge(block_used, 4 * q_end)
                cols = bass.ds(n * BN, BN)
                for t in range(NT):
                    a = dve.scalar_tensor_tensor(out=resid[:, t, cols], in0=accs[t][:, :], scalar=factor,
                                                 in1=resid[:, t, cols], op0=ALU.mult, op1=ALU.add)
                a.then_inc(added, 1)
                dve.wait_ge(added, a0 + n + 2)
                for t in range(NT):
                    a = dve.bn_stats(bn[:, t, bass.ds(n, 1), :].rearrange("p a s -> p (a s)"), resid[:, t, cols])
                a.then_inc(stat_step, 1)

            def down_step(q0, n, accs, last=False):
                per = DOWN_BLOCKS // STAGES
                for b in range(1, DOWN_BLOCKS + (not last)):
                    lo(q0 + per * n + b // STAGES, b % STAGES)

            def norm(l, s_end):
                dve.wait_ge(stat_step, s_end)
                for t in range(NT):
                    a = dve.bn_aggr(mv[:, t, :], bn[:, t, :, :].rearrange("p c s -> p (c s)"))
                a.then_inc(aggr_ready, 1)
                dve.wait_ge(std_ready, l + 1)
                if l < 2:
                    dve.reciprocal(rstd[:, :], std[:, :]).then_inc(rstd_ready, 1)
                    dve.wait_ge(rstd_ready, l + 1)
                    for q in range(4):
                        for t in range(NT):
                            piece = resid[:, t, q * BN:(q + 1) * BN]
                            a = dve.tensor_scalar(piece, piece, mv[:, t, 0:1], rstd[:, t:t + 1],
                                                  ALU.subtract, ALU.mult)
                        a.then_inc(z_ready, 1)

            steps = [0]

            def step(ins):
                ins.then_inc(pos_step, 1)
                steps[0] += 1
                dve.wait_ge(pos_step, steps[0])

            for counter in (hT_ready, down_added, out_added, hid_copied):
                dve.sem_inc(counter, 1)
            dve.memset(ang[:, :, :], 0.0)
            dve.wait_ge(pos_loaded, 16 * 5)
            dve.tensor_copy(pos_f[:, 0:NT], pos_i[:, 0:NT])
            step(dve.tensor_tensor(pos_f[0:N_CMP, NT:NT + 1], pos_i[0:N_CMP, NT:NT + 1],
                                   pos_i[0:N_CMP, NT + 1:NT + 2], ALU.add))
            for t in range(NT):
                dve.tensor_scalar(ang[:, t, :], invf_bc[:, :], pos_f[:, t:t + 1], None, ALU.mult)
            step(dve.tensor_scalar(ang[0:N_CMP, NT, :], invf_bc[0:N_CMP, :], pos_f[0:N_CMP, NT:NT + 1], 0.5,
                                   ALU.mult, ALU.mult))
            step(dve.tensor_scalar(turns[:, :, :], ang[:, :, :], 0.15915494309189535, MAGIC, ALU.mult, ALU.add))
            step(dve.tensor_scalar(turns[:, :, :], turns[:, :, :], MAGIC, None, ALU.subtract))
            for part in (TWO_PI_1, TWO_PI_2, TWO_PI_3):
                step(dve.scalar_tensor_tensor(out=ang[:, :, :], in0=turns[:, :, :], scalar=-part, in1=ang[:, :, :],
                                              op0=ALU.mult, op1=ALU.add))
            step(dve.tensor_scalar(red[:, 0], ang[:, :, :], PI, -PI, ALU.min, ALU.max))
            step(dve.tensor_scalar(ang[:, :, :], red[:, 0], PI / 2, None, ALU.add))
            step(dve.tensor_scalar(turns[:, :, :], ang[:, :, :], PI, -2 * 3.141592653589793, ALU.is_gt, ALU.mult))
            step(dve.tensor_tensor(ang[:, :, :], ang[:, :, :], turns[:, :, :], ALU.add))
            dve.tensor_scalar(red[:, 1], ang[:, :, :], PI, -PI, ALU.min, ALU.max).then_inc(red_ready, 1)
            dve.wait_ge(vecs_turned, 1)
            dve.tensor_copy(vecsT[:, :], bank[7][:, 0:P])
            dve.tensor_copy(b1T[:, :], bank[7][:, P:P + 4]).then_inc(vecs_ready, 1)
            split_input(0)
            lo(0, 0)

            up(Q_UP1, 0, 1)
            with dve.Fori(0, DOWN_CHUNKS // 2) as i:
                for j, accs in enumerate((A, B)):
                    down_step(Q_DOWN1, 2 * i + j, accs)
                    add(accs, Q_DOWN1 + (DOWN_BLOCKS // STAGES) * (2 * i + j + 1), 2 * i + j, 0.5, down_added, 0, 0)
            norm(0, 4)
            split_input(8)

            def proj_step(p, accs, between=None, cb=None):
                lo(Q_PROJ + p, 1)
                if between:
                    between()
                lo(Q_PROJ + p, 2)
                if cb is not None:
                    dve.wait_ge(c_hi_ready, cb + 1)
                    dve.tensor_tensor(c_lo[:, :, :], cstage[:, :, :], c_hi[:, :, :], ALU.subtract
                                      ).then_inc(c_lo_ready, 1)
                lo(Q_PROJ + p, 3)
                lo(Q_PROJ + p + 1, 0)
                dve.wait_ge(block_used, 4 * (Q_PROJ + p) + 4)
                dve.tensor_copy(proj[:, 1, bass.ds(p * BN, BN)], accs[1][:, :]).then_inc(proj_copied_v, 1)
                if cb is not None:
                    dve.wait_ge(c_used, cb + 2)
                    dve.tensor_copy(hid_part[:, bass.ds(cb, 1), :, :].rearrange("p a h r -> p (a h) r"),
                                    bank[7][:, 0:64].rearrange("p (h r) -> p h r", r=32)[:, :, 0:ROWS_CMP]
                                    ).then_inc(hid_copied, 1)

            def take_tokens():
                dve.wait_ge(tok_turned, 1)
                for a in range(2):
                    c = dve.tensor_copy(tokT[:, 2 * a:2 * a + 2, :],
                                        bank[5 + a][:, :].rearrange("p (a n) -> p a n", a=2))
                c.then_inc(tok_copied, 1)

            proj_step(0, A)
            proj_step(1, B, take_tokens)
            dve.wait_ge(gate_summed, 1)
            dve.wait_ge(attn_loaded, 16 * 4)
            for t in range(NT):
                a = dve.tensor_tensor(gates[:, t, :], bank[7][:, t * 32:t * 32 + N_GATE], gate_b_bc[:, :], ALU.add)
            a.then_inc(gate_biased, 1)
            dve.wait_ge(resid_ready, 2)
            with dve.Fori(0, (PROJ_CHUNKS - 2) // 2) as i:
                proj_step(2 * i + 2, A, None, 2 * i)
                proj_step(2 * i + 3, B, None, 2 * i + 1)

            parts = hid_part[:, :, :, :].rearrange("p (j c) h r -> p c j (h r)", c=CMP_BLOCKS // 2)
            total = hid_sum[:, :, :, :].rearrange("p j h r -> p j (h r)")
            dve.wait_ge(hid_copied, CMP_BLOCKS + 1)
            dve.tensor_tensor(total, parts[:, 0], parts[:, 1], ALU.add).then_inc(hid_step, 1)
            for c in (2, 3):
                dve.wait_ge(hid_step, c - 1)
                a = dve.tensor_tensor(total, total, parts[:, c], ALU.add)
                a.then_inc(hid_step if c == 2 else hid_sum_ready, 1)
            for n in range(0, len(TURNED) // 2, 2):
                dve.wait_ge(qk_turned, n + 1)
                dve.tensor_copy(qkT[:, 2 * n:2 * n + 2, :], bank[6][:, :].rearrange("p (a n) -> p a n", a=2)
                                ).then_inc(qk_even, 1)

            def mask_scores(u):
                h, t, br = UNITS[u]
                n = (t + 1) * P
                m = dmask if br == "dil" else cmask
                dve.wait_ge(scored, u + 1)
                if u >= 2:
                    dve.wait_ge(exp_ready, u - 1)
                dve.tensor_tensor_reduce(masked[:, u % 2, 0:n], bank[u % 2][:, 0:n], m[:, SEQ - n:SEQ], 1.0, -3e38,
                                         ALU.add, ALU.max, rowmax[:, u:u + 1]).then_inc(masked_ready, 1)
                dve.wait_ge(masked_ready, u + 1)
                dve.tensor_scalar(negmax[:, u:u + 1], rowmax[:, u:u + 1], -SCALE, None, ALU.mult
                                  ).then_inc(negmax_ready, 1)

            def weigh(u):
                h, t, br = UNITS[u]
                e = probs[:, u % E_RING, 0:(t + 1) * P]
                dve.wait_ge(exp_ready, u + 1)
                dve.reciprocal(rinv[:, u:u + 1], rowsum[:, u:u + 1]).then_inc(inv_ready, 1)
                dve.wait_ge(inv_ready, u + 1)
                if br == "dil":
                    w = dve.tensor_scalar(e, e, rinv[:, u:u + 1], None, ALU.mult)
                else:
                    c = (h - N_DIL) * N_BRANCH + (1 if br == "slc" else 2)
                    w = dve.tensor_scalar(e, e, rinv[:, u:u + 1], gates[:, t, c:c + 1], ALU.mult, ALU.mult)
                w.then_inc(probs_ready, 1)

            def mix_lo(h):
                dve.wait_ge(mix_hi_ready, h + 1)
                dve.tensor_tensor(xT_lo[:, h, :], bank[4 + h % 2][:, 0:SEQ], xT_hi[:, h, :], ALU.subtract
                                  ).then_inc(mix_ready, 1)

            def chain(sem_, count):
                def go(ins):
                    ins.then_inc(sem_, 1)
                    count[0] += 1
                    dve.wait_ge(sem_, count[0])
                return go

            def compressed_kv():
                go = chain(kvc_step, [0])
                dve.wait_ge(kvc_summed, 1)
                go(dve.tensor_tensor(kvc[:, :, :].rearrange("p (j g) d -> p j g d", j=2),
                                     bank[6][0:N_CMP, :].rearrange("p (j g d) -> p j g d", j=2, g=2),
                                     b2_bc[:, :, :].unsqueeze(2).broadcast_to([N_CMP, 2, KV_GROUPS, HD]), ALU.add))
                k = kvc[:, 0:KV_GROUPS, :].rearrange("p g (x d) -> p g x d", x=2)
                cos = cos_c[0:N_CMP, 0, :].unsqueeze(1).unsqueeze(1).broadcast_to([N_CMP, KV_GROUPS, 2, HD // 2])
                sin = cos_c[0:N_CMP, 1, :].unsqueeze(1).unsqueeze(1).broadcast_to([N_CMP, KV_GROUPS, 2, HD // 2])
                dve.tensor_tensor(crt[:, 0], k, cos, ALU.mult)
                go(dve.tensor_tensor(crt[:, 1], k, sin, ALU.mult))
                dve.tensor_tensor(k[:, :, 0, :], crt[:, 0, :, 0, :], crt[:, 1, :, 1, :], ALU.subtract)
                dve.tensor_tensor(k[:, :, 1, :], crt[:, 0, :, 1, :], crt[:, 1, :, 0, :], ALU.add
                                  ).then_inc(kvc_ready, 1)

            def compressed_softmax_a():
                go = chain(cmp_step, [0])
                dve.wait_ge(cmp_scored, 1)
                for t in range(NT):
                    a = dve.tensor_tensor(
                        csc[:, t], bank[6][:, t * N_NSA * N_CMP:(t + 1) * N_NSA * N_CMP].rearrange(
                            "p (h n) -> p h n", n=N_CMP),
                        cmpm[:, 0, t, :].unsqueeze(1).broadcast_to([P, N_NSA, N_CMP]), ALU.add)
                go(a)
                go(dve.tensor_reduce(cst[:, 0], csc[:, :, :, :], AX.X, ALU.max))
                dve.tensor_tensor(csc[:, :, :, :], csc[:, :, :, :],
                                  cst[:, 0].unsqueeze(3).broadcast_to([P, NT, N_NSA, N_CMP]), ALU.subtract
                                  ).then_inc(cmp_shifted, 1)

            def compressed_softmax_b():
                go = chain(cmp_step, [2])
                dve.wait_ge(cmp_exp, 1)
                for t in range(NT):
                    a = dve.tensor_tensor(cex[:, t], cex[:, t],
                                          cmpm[:, 1, t, :].unsqueeze(1).broadcast_to([P, N_NSA, N_CMP]), ALU.mult)
                go(a)
                go(dve.tensor_reduce(cst[:, 1], cex[:, :, :, :], AX.X, ALU.add))
                go(dve.tensor_scalar(cst[:, 2], cst[:, 1], 1e-30, None, ALU.max))
                go(dve.reciprocal(cst[:, 1], cst[:, 2]))
                go(dve.tensor_tensor(cst[:, 3], cst[:, 1],
                                     gates[:, :, :].rearrange("p t (h b) -> p t h b", b=N_BRANCH)[:, :, :, 0],
                                     ALU.mult))
                dve.tensor_tensor(cpr[:, :, :, :], cex[:, :, :, :],
                                  cst[:, 3].unsqueeze(3).broadcast_to([P, NT, N_NSA, N_CMP]), ALU.mult
                                  ).then_inc(cmp_ready, 1)

            dve.wait_ge(gates_ready, 1)
            for s in range(NU + LAG_PV):
                if s < NU:
                    mask_scores(s)
                if s == STEP_CMP_OUT + 2:
                    compressed_kv()
                if s == STEP_CMP_TURN + 1:
                    dve.wait_ge(kc_turned, 1)
                    dve.tensor_copy(kcT[:, :, :], bank[7][:, 0:ROWS_CMP].rearrange("p (g n) -> p g n", g=KV_GROUPS)
                                    ).then_inc(kcT_ready, 1)
                if s == STEP_CMP_SCORE + 1:
                    compressed_softmax_a()
                if s == STEP_CMP_SCORE + 3:
                    compressed_softmax_b()
                if 1 <= s <= NU:
                    weigh(s - 1)
                for h in HEAD_LAST:
                    if HEAD_LAST[h] == s - LAG_PV:
                        mix_lo(h)

            with dve.Fori(0, OUT_CHUNKS // 2) as i:
                for j, accs in enumerate((A, B)):
                    q = Q_OUT + 2 * i + j
                    lo(q, 1)
                    lo(q, 2)
                    lo(q, 3)
                    lo(q + 1, 0)
                    add(accs, q + 1, 2 * i + j, 1.0, out_added, 0, 4)
            norm(1, 8)
            split_input(16)

            up(Q_UP2, UP_CHUNKS, 3)
            for n in range(DOWN_CHUNKS):
                accs = (A, B)[n % 2]
                down_step(Q_DOWN2, n, accs, n == DOWN_CHUNKS - 1)
                add(accs, Q_DOWN2 + (DOWN_BLOCKS // STAGES) * (n + 1), n, 0.5, down_added, DOWN_CHUNKS, 8)
            norm(2, 12)
            dve.reciprocal(rstd[:, :], std[:, :]).then_inc(inv_ready, 1)
            dve.wait_ge(inv_ready, NU + 1)
            dve.scalar_tensor_tensor(out=nmr[:, :], in0=mv[:, :, 0], scalar=-1.0, in1=rstd[:, :],
                                     op0=ALU.mult, op1=ALU.mult).then_inc(rstd_ready, 1)
            dve.wait_ge(ln3_loaded, 32)
            for q in range(4):
                for t in range(NT):
                    piece = resid[:, t, q * BN:(q + 1) * BN]
                    dve.wait_ge(z_ready, 8 + q * NT + t + 1)
                    dve.tensor_tensor(piece, piece, ln3_g_bc[:, q * BN:(q + 1) * BN], ALU.mult
                                      ).then_inc(final_g, 1)

        @block.gpsimd
        def _(pool):
            pool.memset(eps_t[:, :], EPS)
            pool.memset(ident[:, :], 0.0).then_inc(ident_ready, 1)
            pool.wait_ge(ident_ready, 1)
            pool.affine_select(out=ident[:, :], in_=ident[:, :], compare_op=ALU.not_equal, fill=1.0, base=0,
                               pattern=[[-1, P]], channel_multiplier=1).then_inc(ident_ready, 1)
            pool.wait_ge(in_turned, KT // 2)
            for t in range(NT):
                r = pool.tensor_scalar(resid[:, t, :], resid[:, t, :], ALPHA, None, ALU.mult)
            r.then_inc(resid_ready, 1)

            def scale_resid(g, b, bc, turned, n_before):
                pool.wait_ge(in_turned, turned)
                for q in range(4):
                    n = 3 * (n_before + q)
                    if q:
                        pool.wait_ge(resid_step, n)
                    cols = slice(q * BN, (q + 1) * BN)
                    for a, v in enumerate((g, b)):
                        pool.dma_start(bc[:, a, :], v[0:1, cols].broadcast_to([P, BN])).then_inc(bc_loaded, 16)
                    pool.wait_ge(bc_loaded, 32 * (n_before + q + 1))
                    pool.tensor_scalar(bc[:, :, :], bc[:, :, :], ALPHA, None, ALU.mult).then_inc(resid_step, 1)
                    for i, op in enumerate((ALU.mult, ALU.add)):
                        pool.wait_ge(resid_step, n + i + 1)
                        for t in range(NT):
                            r = pool.tensor_tensor(resid[:, t, cols], resid[:, t, cols], bc[:, i, :], op)
                        r.then_inc(resid_step, 1)
                pool.wait_ge(resid_step, 3 * (n_before + 4))
                pool.sem_inc(resid_ready, 1)

            pool.wait_ge(block_used, 4 * Q_PROJ)
            pool.dma_start(wg[:, :, :], w_in[0][:, GATE_COL:IN_COLS].rearrange("(k p) n -> p k n", p=P)
                           ).then_inc(wg_loaded, 16)
            pool.wait_ge(in_ready, KT)
            pool.dma_start(dmask[:, :], dil_mask).then_inc(attn_loaded, 16)
            pool.dma_start(cmask[:, :], causal_mask).then_inc(attn_loaded, 16)
            pool.dma_start(cmpm[:, :, :, :], cmp_mask).then_inc(attn_loaded, 16)
            pool.dma_start(gate_b_bc[:, :], gate_b[0:1, :].broadcast_to([P, N_GATE])).then_inc(attn_loaded, 16)
            pool.wait_ge(wg_loaded, 16)
            pool.tensor_copy(wg_hi[:, :, :], wg[:, :, :]).then_inc(wg_hi_ready, 1)
            pool.wait_ge(wg_hi_ready, 1)
            pool.tensor_tensor(wg_lo[:, :, :], wg[:, :, :], wg_hi[:, :, :], ALU.subtract).then_inc(wg_ready, 1)
            scale_resid(ln1_g, ln1_b, bc1, KT, 0)

            pool.wait_ge(tok_copied, 1)
            pool.wait_ge(vecs_ready, 1)
            for j in range(2):
                tok = tokT[:, 2 * j:2 * j + 2, :].rearrange("p g (n c) -> p c g n", c=CMP_STRIDE)
                for half in range(2):
                    pe_col = 4 * KT + j * CMP_BLOCK + half * CMP_STRIDE
                    for g in range(KV_GROUPS):
                        f = pool.tensor_tensor(
                            flat[:, half * CMP_STRIDE:(half + 1) * CMP_STRIDE, g * N_CMP:(g + 1) * N_CMP],
                            tok[:, :, g, half:half + N_CMP],
                            vecsT[:, pe_col:pe_col + CMP_STRIDE].unsqueeze(2).broadcast_to([P, CMP_STRIDE, N_CMP]),
                            ALU.add)
                f.then_inc(flat_step, 1)
                pool.wait_ge(flat_step, 2 * j + 1)
                part = slice(j * CMP_BLOCK, (j + 1) * CMP_BLOCK)
                pool.tensor_copy(flat_hi[:, part, :], flat[:, :, :]).then_inc(flat_step, 1)
                pool.wait_ge(flat_step, 2 * j + 2)
                pool.tensor_tensor(flat_lo[:, part, :], flat[:, :, :], flat_hi[:, part, :], ALU.subtract
                                   ).then_inc(flat_ready, 1)
                pool.wait_ge(flat_ready, j + 1)

            pool.wait_ge(trig_ready, 1)
            n = 0
            for p, col, heads in ROPE_RUNS:
                pool.wait_ge(proj_copied_a, p + 1)
                pool.wait_ge(proj_copied_v, p + 1)
                for t in range(NT):
                    cos = cos_t[:, t, :].unsqueeze(1).unsqueeze(1).broadcast_to([P, 2, 2, HD // 2])
                    sin = sin_t[:, t, :].unsqueeze(1).unsqueeze(1).broadcast_to([P, 2, 2, HD // 2])
                    for h in range(0, heads, 2):
                        v = proj[:, t, col + h * HD:col + (h + 2) * HD].rearrange("p (h x d) -> p h x d", h=2, x=2)
                        if n:
                            pool.wait_ge(rope_step, 2 * n)
                        pool.tensor_tensor(rt[:, 0], v, cos, ALU.mult)
                        pool.tensor_tensor(rt[:, 1], v, sin, ALU.mult).then_inc(rope_step, 1)
                        pool.wait_ge(rope_step, 2 * n + 1)
                        pool.tensor_tensor(v[:, :, 0, :], rt[:, 0, :, 0, :], rt[:, 1, :, 1, :], ALU.subtract)
                        pool.tensor_tensor(v[:, :, 1, :], rt[:, 0, :, 1, :], rt[:, 1, :, 0, :], ALU.add
                                           ).then_inc(rope_step, 1)
                        n += 1
                pool.wait_ge(rope_step, 2 * n)
                pool.sem_inc(roped, 1)

            pool.wait_ge(c_used, CMP_BLOCKS + 1)
            pool.dma_start(cw2[:, :, :], cmp_w2[0].rearrange("j (h p) d -> p (j h) d", p=P)).then_inc(cw2_loaded, 16)
            pool.dma_start(b2_bc[:, :, :], cmp_b2[0:1].broadcast_to([N_CMP, 2, HD])).then_inc(cw2_loaded, 16)

            scale_resid(ln2_g, ln2_b, bc2, 3 * KT // 2, 4)
            pool.wait_ge(block_used, 4 * Q_DOWN2)
            pool.dma_start(ln3_g_bc[:, :], ln3_g[0:1, :].broadcast_to([P, DM])).then_inc(ln3_loaded, 16)
            pool.dma_start(ln3_b_bc[:, :], ln3_b[0:1, :].broadcast_to([P, DM])).then_inc(ln3_loaded, 16)
            pool.wait_ge(ln3_loaded, 32)
            for q in range(4):
                for t in range(NT):
                    piece = resid[:, t, q * BN:(q + 1) * BN]
                    pool.wait_ge(final_g, q * NT + t + 1)
                    pool.tensor_tensor(piece, piece, ln3_b_bc[:, q * BN:(q + 1) * BN], ALU.add
                                       ).then_inc(final_b, 1)


_INS = ["x", "positions", "ln1_g", "ln1_b", "ffn1_w1", "ffn1_w3", "ffn1_w2", "w_in", "gate_b", "cmp_pe", "cmp_w1",
        "cmp_b1", "cmp_w2", "cmp_b2", "w_out", "ln2_g", "ln2_b", "ffn2_w1", "ffn2_w3", "ffn2_w2", "ln3_g", "ln3_b"]


def _constants():
    import numpy as np

    f = np.float32
    inv_freq = (f(10000.0) ** (-np.arange(0, HD, 2, dtype=f) / f(HD))).astype(f)[None, :]
    d = (P + np.arange(P)[:, None]) - np.arange(SEQ)[None, :]
    causal = np.where(d >= 0, 0.0, -1e30).astype(f)
    count = (d <= 128) * 1 + (d % 4 == 0) * 1 + (d % 16 == 0) * 1
    dil = np.where((d >= 0) & (count > 0), np.log(np.maximum(count, 1)) / SCALE, -1e30).astype(f)
    token = np.arange(SEQ).reshape(NT, P).T[:, :, None]
    seen = np.arange(N_CMP) * CMP_STRIDE + CMP_BLOCK - 1 <= token
    cmp = np.stack([np.where(seen, 0.0, -1e30), seen * 1.0], axis=1).astype(f)
    return {"inv_freq": inv_freq, "dil_mask": dil, "causal_mask": causal, "cmp_mask": cmp}


def kernel(**inputs):
    import numpy as _np
    import concourse.bacc as _bacc
    from concourse import mybir as _mybir
    from concourse.bass_utils import run_bass_kernel_spmd as _run

    nc = _bacc.Bacc("TRN2", target_bir_lowering=False, num_devices=1)
    arrays, args = {}, []
    given = {name: _np.ascontiguousarray(inputs[name]) for name in _INS}
    for name, a in {**given, **_constants()}.items():
        arrays[f"in_{name}"] = a
        args.append(nc.dram_tensor(f"in_{name}", a.shape, _mybir.dt.from_np(a.dtype), kind="ExternalInput").ap())
    args.append(nc.dram_tensor("out_0", (1, SEQ, DM), F32, kind="ExternalOutput").ap())
    layer(nc, *args)
    r = _run(nc, [arrays], core_ids=[0])
    return r.results[0]["out_0"]
```

```python
from contextlib import ExitStack

import concourse.bass as bass
from concourse import mybir

F32 = mybir.dt.float32
F32R = mybir.dt.float32r
I32 = mybir.dt.int32
ALU = mybir.AluOpType
ACT = mybir.ActivationFunctionType
AX = mybir.AxisListType

P = 128
SEQ = 256
NT = SEQ // P
DM = 2048
KT = DM // P
DFF = 5632
FT = DFF // P
HD = 128
N_DIL = 6
N_NSA = 10
KV_GROUPS = 2
NSA_GROUP = N_NSA // KV_GROUPS
N_BRANCH = 3
N_GATE = N_NSA * N_BRANCH
CMP_BLOCK = 32
CMP_STRIDE = 16
CMP_HIDDEN = 256
N_CMP = (SEQ - CMP_BLOCK) // CMP_STRIDE + 1
ROWS_CMP = KV_GROUPS * N_CMP
IN_COLS = 5150
GATE_COL = IN_COLS - N_GATE
SCALE = float(HD) ** -0.5
ALPHA = 2.0 ** 0.25
EPS = 1e-5

BK = 4
BN = 512
STAGES = 4
SPLITS = 2
BC = 256
UP_COLS = BN // 2
UP_CHUNKS = DFF // UP_COLS
UP_F = UP_COLS // P
DOWN_CHUNKS = DM // BN
PROJ_CHUNKS = 10
OUT_CHUNKS = DM // BN
DOWN_K = [4] * 8 + [3] * 4
DOWN_BLOCKS = len(DOWN_K)
assert sum(DOWN_K) == FT and DOWN_BLOCKS % STAGES == 0 and KT // BK == STAGES

Q_UP1 = 0
Q_DOWN1 = Q_UP1 + UP_CHUNKS
Q_PROJ = Q_DOWN1 + DOWN_CHUNKS * DOWN_BLOCKS // STAGES
Q_OUT = Q_PROJ + PROJ_CHUNKS
Q_UP2 = Q_OUT + OUT_CHUNKS
Q_DOWN2 = Q_UP2 + UP_CHUNKS
Q_END = Q_DOWN2 + DOWN_CHUNKS * DOWN_BLOCKS // STAGES

PROJ_FROM = [3584, 4096, 4608, 2048, 2560, 3072, 0, 512, 1024, 1536]
COL_KC, COL_VC, COL_KS, COL_VS, COL_KW, COL_VW = range(0, 1536, 256)
COL_VA_TAIL, COL_QN, COL_QA, COL_KA, COL_VA = 1536, 1792, 3072, 3840, 4608
PROJ_COLS = PROJ_CHUNKS * BN
ROPE_RUNS = [(1, COL_KS, 2), (2, COL_KW, 2), (3, COL_QN, 2), (4, 2048, 4), (5, 2560, 4),
             (6, 3072, 4), (7, 3584, 4), (8, 4096, 4)]
TURNED = [COL_KS, COL_KS + HD, COL_KW, COL_KW + HD] + list(range(COL_QN, COL_VA, HD))
T_KS, T_KW, T_QN, T_QA, T_KA = 0, 2, 4, 14, 20
CMP_K = 8
CMP_BLOCKS = 2 * CMP_BLOCK // CMP_K

TWO_PI_1, TWO_PI_2 = 6.28125, 0.0019350051879882812
TWO_PI_3 = 6.283185307179586 - TWO_PI_1 - TWO_PI_2
PI = 3.1415925
MAGIC = 12582912.0

UNITS = [(h, t, "dil") for h in range(N_DIL) for t in range(NT)]
UNITS += [(N_DIL + h, t, b) for h in range(N_NSA) for t in range(NT) for b in ("slc", "win")]
NU = len(UNITS)
HEAD_LAST = {h: max(u for u in range(NU) if UNITS[u][0] == h) for h in range(N_DIL + N_NSA)}
LAG_TURN, LAG_PV = 4, 5
E_RING, MASKED_RING = 6, 3
STEP_CMP_OUT, STEP_CMP_TURN, STEP_CMP_SCORE = 1, 5, 7


def layer(nc, x, positions, ln1_g, ln1_b, ffn1_w1, ffn1_w3, ffn1_w2, w_in, gate_b, cmp_pe, cmp_w1,
          cmp_b1, cmp_w2, cmp_b2, w_out, ln2_g, ln2_b, ffn2_w1, ffn2_w3, ffn2_w2, ln3_g, ln3_b,
          inv_freq, dil_mask, causal_mask, cmp_mask, out):
    base = (nc.sbuf_base + 63) // 64 * 64

    def at(name, shape, dt, offset):
        return nc.alloc_sbuf_tensor_at(name, shape, dt, offset=base + offset)

    o = 0
    resid = at("resid", [P, NT, DM], F32, o)
    o += NT * DM * 4
    xT_hi = at("xT_hi", [P, KT, SEQ], F32R, o)
    xT_lo = at("xT_lo", [P, KT, SEQ], F32R, o + KT * SEQ * 4)
    ln3_g_bc = at("ln3_g_bc", [P, DM], F32, o)
    ln3_b_bc = at("ln3_b_bc", [P, DM], F32, o + DM * 4)
    o += 2 * KT * SEQ * 4
    HT = o
    hT_hi = at("hT_hi", [P, FT, SEQ], F32R, HT)
    hT_lo = at("hT_lo", [P, FT, SEQ], F32R, HT + FT * SEQ * 4)
    o += 2 * FT * SEQ * 4
    LN_BC2 = o - 2 * BC * 4
    stage = at("stage", [P, STAGES, BK, BN], F32, o)
    o += STAGES * BK * BN * 4
    w_hi = at("w_hi", [P, SPLITS, BK, BN], F32R, o)
    o += SPLITS * BK * BN * 4
    w_lo = at("w_lo", [P, SPLITS, BK, BN], F32R, o)
    o += SPLITS * BK * BN * 4
    SMALL = o
    silu = at("silu", [P, NT, UP_COLS], F32, o)
    gated = at("gated", [P, NT, UP_COLS], F32, o + 2048)
    turned_f32 = at("turned_f32", [P, 2, BN], F32, o)
    dmask = at("dmask", [P, SEQ], F32, o)
    cmask = at("cmask", [P, SEQ], F32, o + 1024)
    cmpm = at("cmpm", [P, 2, NT, N_CMP], F32, o + 2048)
    gates = at("gates", [P, NT, N_GATE], F32, o + 2304)
    negmax = at("negmax", [P, NU], F32, o + 2912)
    rowsum = at("rowsum", [P, NU], F32, o + 3136)
    rinv = at("rinv", [P, NU], F32, o + 3360)
    gate_bT = at("gate_bT", [N_GATE, 1], F32, o + 3584)
    o += 4096
    ident = at("ident", [P, P], F32, o)
    o += 512
    vecs = at("vecs", [P, P], F32, o)
    vecsT = at("vecsT", [P, P], F32, o + 512)
    o += 1024
    cos_t = at("cos_t", [P, NT, HD // 2], F32, o)
    sin_t = at("sin_t", [P, NT, HD // 2], F32, o + 512)
    o += 1024
    cos_c = at("cos_c", [P, 2, HD // 2], F32, o)
    o += 512
    bn = at("bn", [P, NT, DM // BN, 6], F32, o)
    o += 192
    mv = at("mv", [P, NT, 2], F32, o)
    std = at("std", [P, NT], F32, o + 32)
    rstd = at("rstd", [P, NT], F32, o + 64)
    nmr = at("nmr", [P, NT], F32, o + 96)
    eps_t = at("eps_t", [P, 1], F32, o + 128)
    b1T = at("b1T", [P, 4], F32, o + 160)
    warm = at("warm", [P, 3], F32, o + 192)
    o += 224
    assert base + o <= nc.sbuf_usable_end

    o = HT
    proj = at("proj", [P, NT, PROJ_COLS], F32, o)
    o += NT * PROJ_COLS * 4
    FREE = o
    cstage = at("cstage", [P, CMP_K, CMP_HIDDEN], F32, o)
    c_hi = at("c_hi", [P, CMP_K, CMP_HIDDEN], F32R, o + 8192)
    c_lo = at("c_lo", [P, CMP_K, CMP_HIDDEN], F32R, o + 16384)
    wg = at("wg", [P, KT, N_GATE], F32, o)
    wg_hi = at("wg_hi", [P, KT, N_GATE], F32R, o + 8192)
    wg_lo = at("wg_lo", [P, KT, N_GATE], F32R, o + 16384)
    o += 24576
    tokT = at("tokT", [P, 4, SEQ], F32, o)
    o += 4096
    flat_hi = at("flat_hi", [P, 2 * CMP_BLOCK, ROWS_CMP], F32R, o)
    flat_lo = at("flat_lo", [P, 2 * CMP_BLOCK, ROWS_CMP], F32R, o + 7680)
    o += 15360
    flat = at("flat", [P, CMP_BLOCK, ROWS_CMP], F32, FREE)
    bc1 = at("bc1", [P, 2, BC], F32, o)
    rt = at("rt", [P, 2, 2, 2, HD // 2], F32, o)
    hid_sum = at("hid_sum", [ROWS_CMP, 2, CMP_HIDDEN], F32, o + 2048)
    gatesT = at("gatesT", [N_GATE, SEQ], F32, o + 4096)
    flat_now_hi = at("flat_now_hi", [P, CMP_K, ROWS_CMP], F32R, FREE + 24576)
    flat_now_lo = at("flat_now_lo", [P, CMP_K, ROWS_CMP], F32R, FREE + 24576 + 1024)
    o += 5120
    assert o <= HT + 2 * FT * SEQ * 4
    o = FREE
    qkT = at("qkT", [P, len(TURNED), SEQ], F32, o)
    o += len(TURNED) * SEQ * 4
    masked = at("masked", [P, MASKED_RING, SEQ], F32, o)
    o += MASKED_RING * SEQ * 4
    probs = at("probs", [P, E_RING, SEQ], F32, o)
    o += E_RING * SEQ * 4
    probsT = at("probsT", [P, 2, NT, P], F32, o)
    o += 2048
    csc = at("csc", [P, NT, N_NSA, N_CMP], F32, o)
    cex = at("cex", [P, NT, N_NSA, N_CMP], F32, o + 1216)
    crt = at("crt", [N_CMP, 2, KV_GROUPS, 2, HD // 2], F32, o)
    cpr = at("cpr", [P, NT, N_NSA, N_CMP], F32, o + 2432)
    cst = at("cst", [P, 4, NT, N_NSA], F32, o + 3648)
    o += 3968
    hidT = at("hidT", [P, 2, 2, ROWS_CMP], F32, o)
    o += 512
    kcT = at("kcT", [P, KV_GROUPS, N_CMP], F32, o)
    o += 128
    cw2 = at("cw2", [P, 4, HD], F32, o)
    o += 2048
    cprT = at("cprT", [N_CMP, 2, P], F32, o)
    o += 1024
    assert o <= FREE + 44032 + 2048
    kvc = at("kvc", [N_CMP, 4, HD], F32, o)
    b2_bc = at("b2_bc", [N_CMP, 2, HD], F32, FREE + 48128)
    assert o + 2048 <= FREE + 48128
    bc2 = at("bc2", [P, 2, BC], F32, LN_BC2)
    pos_i = at("pos_i", [P, NT + 2], I32, HT)
    pos_f = at("pos_f", [P, NT + 2], F32, HT + 32)
    invf_bc = at("invf_bc", [P, HD // 2], F32, HT + 64)
    ang = at("ang", [P, 3, HD // 2], F32, HT + 1024)
    turns = at("turns", [P, 3, HD // 2], F32, HT + 2048)
    red = at("red", [P, 2, 3, HD // 2], F32, HT + 3072)
    b1rows = at("b1rows", [4, P], F32, HT + 5120)

    with ExitStack() as ctx:
        bank = [ctx.enter_context(nc.psum_tensor(f"bank{i}", [P, 512], F32)) for i in range(8)]

        def sem(name):
            return ctx.enter_context(nc.semaphore(name))

        stage_full = [sem(f"stage_full{s}") for s in range(STAGES)]
        hi_ready, lo_ready, block_used = sem("hi_ready"), sem("lo_ready"), sem("block_used")
        x_loaded = [sem(f"x_loaded{q}") for q in range(4)]
        vecs_loaded, pos_loaded = sem("vecs_loaded"), sem("pos_loaded")
        attn_loaded, wg_loaded, bc_loaded = sem("attn_loaded"), sem("wg_loaded"), sem("bc_loaded")
        cstage_full, cw2_loaded, ln3_loaded = sem("cstage_full"), sem("cw2_loaded"), sem("ln3_loaded")
        out_stored = sem("out_stored")
        ident_ready, vecs_turned, vecs_ready = sem("ident_ready"), sem("vecs_turned"), sem("vecs_ready")
        pos_step, red_ready, trig_ready = sem("pos_step"), sem("red_ready"), sem("trig_ready")
        in_turned, in_full, in_hi, in_ready = sem("in_turned"), sem("in_full"), sem("in_hi"), sem("in_ready")
        stat_step, aggr_ready, std_ready, rstd_ready, z_ready = (
            sem("stat_step"), sem("aggr_ready"), sem("std_ready"), sem("rstd_ready"), sem("z_ready"))
        resid_step, resid_ready = sem("resid_step"), sem("resid_ready")
        silu_ready, gated_ready, hid_turned, hT_hi_ready, hT_ready = (
            sem("silu_ready"), sem("gated_ready"), sem("hid_turned"), sem("hT_hi_ready"), sem("hT_ready"))
        down_added, out_added = sem("down_added"), sem("out_added")
        proj_copied_a, proj_copied_v, wg_hi_ready, wg_ready = (
            sem("proj_copied_a"), sem("proj_copied_v"), sem("wg_hi_ready"), sem("wg_ready"))
        gate_summed, gatesT_ready, gates_turned, gates_ready = (
            sem("gate_summed"), sem("gatesT_ready"), sem("gates_turned"), sem("gates_ready"))
        tok_turned, tok_copied, flat_step, flat_ready = (
            sem("tok_turned"), sem("tok_copied"), sem("flat_step"), sem("flat_ready"))
        c_hi_ready, c_lo_ready, c_used, hid_added = (
            sem("c_hi_ready"), sem("c_lo_ready"), sem("c_used"), sem("hid_added"))
        rope_step, roped = sem("rope_step"), sem("roped")
        qk_turned, qk_even, qk_odd = sem("qk_turned"), sem("qk_even"), sem("qk_odd")
        sums_turned, hidT_ready, kvc_summed, kvc_step, kvc_ready = (
            sem("sums_turned"), sem("hidT_ready"), sem("kvc_summed"), sem("kvc_step"), sem("kvc_ready"))
        kc_turned, kcT_ready, cmp_scored, cmp_step, cmp_shifted, cmp_exp, cmp_ready = (
            sem("kc_turned"), sem("kcT_ready"), sem("cmp_scored"), sem("cmp_step"), sem("cmp_shifted"),
            sem("cmp_exp"), sem("cmp_ready"))
        scored, masked_ready, exp_ready, inv_ready, probs_ready = (
            sem("scored"), sem("masked_ready"), sem("exp_ready"), sem("inv_ready"),
            sem("probs_ready"))
        probs_turned, probsT_ready, valued = (
            sem("probs_turned"), [sem("probsT_ready0"), sem("probsT_ready1")], sem("valued"))
        mix_hi_ready, mix_ready = sem("mix_hi_ready"), sem("mix_ready")
        final_step, final_g = sem("final_step"), sem("final_g")
        final_ready = [sem("final_ready0"), sem("final_ready1")]

        def flat_rows(i, j):
            return bass.ds(CMP_K * i + j * CMP_BLOCK, CMP_K)

        def taken(u):
            t = UNITS[u][1]
            return probsT_ready[t], sum(UNITS[v][1] == t for v in range(u + 1))

        block = ctx.enter_context(nc.Block())

        def rows(w, kt, n):
            return w[kt * P:(kt + n) * P, :].rearrange("(k p) n -> p k n", p=P)

        @block.sync
        def _(sp):
            def slot_free(q, s):
                if not (isinstance(q, int) and q == 0):
                    sp.wait_ge(lo_ready, 4 * q + s - 3)

            def load_up_block(w1, w3, q, c, s):
                slot_free(q, s)
                for half, w in enumerate((w1, w3)):
                    sp.dma_start(stage[:, s, :, half * UP_COLS:(half + 1) * UP_COLS],
                                 rows(w, s * BK, BK)[:, :, bass.ds(c * UP_COLS, UP_COLS)]
                                 ).then_inc(stage_full[s], 16)

            def load_up(w1, w3, q, c):
                for s in range(STAGES):
                    load_up_block(w1, w3, q, c, s)

            def load_block(w, q, s, kt, n, col):
                slot_free(q, s)
                for a, b in ((0, 2), (2, n)):
                    sp.dma_start(stage[:, s, a:b, :], rows(w, kt + a, b - a)[:, :, bass.ds(col, BN)]
                                 ).then_inc(stage_full[s], 16)

            def load_down(w2, q0):
                with sp.Fori(0, DOWN_CHUNKS) as n:
                    for b, k in enumerate(DOWN_K):
                        load_block(w2, q0 + n * (DOWN_BLOCKS // STAGES) + b // STAGES, b % STAGES,
                                   sum(DOWN_K[:b]), k, n * BN)

            def load_x(q):
                sp.dma_start(resid[:, :, q * BN:(q + 1) * BN],
                             x[0].rearrange("(t p) n -> p t n", p=P)[:, :, q * BN:(q + 1) * BN]
                             ).then_inc(x_loaded[q], 16)

            load_x(0)
            for s in range(STAGES):
                if s:
                    load_x(s)
                load_up_block(ffn1_w1[0], ffn1_w3[0], 0, 0, s)
            with sp.Fori(1, UP_CHUNKS) as c:
                load_up(ffn1_w1[0], ffn1_w3[0], Q_UP1 + c, c)
            load_down(ffn1_w2[0], Q_DOWN1)
            for p in range(PROJ_CHUNKS):
                for s in range(STAGES):
                    load_block(w_in[0], Q_PROJ + p, s, s * BK, BK, PROJ_FROM[p])
            with sp.Fori(0, OUT_CHUNKS) as n:
                for s in range(STAGES):
                    load_block(w_out[0], Q_OUT + n, s, s * BK, BK, n * BN)
            with sp.Fori(0, UP_CHUNKS) as c:
                load_up(ffn2_w1[0], ffn2_w3[0], Q_UP2 + c, c)
            load_down(ffn2_w2[0], Q_DOWN2)
            for q in range(4):
                for t in range(NT):
                    sp.wait_ge(final_ready[t], q + 1)
                    sp.dma_start(out[0, t * P:(t + 1) * P, q * BN:(q + 1) * BN],
                                 resid[:, t, q * BN:(q + 1) * BN]).then_inc(out_stored, 16)
            sp.wait_ge(out_stored, 16 * 4 * NT)

        @block.tensor
        def _(pe):
            def product(acc, a, b, start, stop):
                pe.matmul(acc, a[0], b[0], start=start, stop=False)
                pe.matmul(acc, a[0], b[1], start=False, stop=False)
                return pe.matmul(acc, a[1], b[0], start=False, stop=stop)

            def split_block(accs, src, q, s, kt, n, first, last):
                pe.wait_ge(lo_ready, 4 * q + s + 1)
                for k in range(n):
                    for t in range(NT):
                        col = slice(t * P, (t + 1) * P)
                        mm = product(accs[t][:, :], (src[0][:, kt + k, col], src[1][:, kt + k, col]),
                                     (w_hi[:, s % 2, k, :], w_lo[:, s % 2, k, :]),
                                     first and k == 0, last and k == n - 1)
                mm.then_inc(block_used, 1)

            xT, hT = (xT_hi, xT_lo), (hT_hi, hT_lo)
            A, B = bank[0:2], bank[2:4]
            T = bank[4]

            def turn_quarter(n0, q, src_ready):
                src_ready(q)
                for j in (2 * q, 2 * q + 1):
                    n = n0 + j
                    if n >= 2:
                        pe.wait_ge(in_full, n - 1)
                    for k in range(2):
                        for t in range(NT):
                            mm = pe.transpose(bank[5 + n % 2][:, k * SEQ + t * P:k * SEQ + (t + 1) * P],
                                              resid[:, t, (2 * j + k) * P:(2 * j + k + 1) * P], ident[:, :])
                    mm.then_inc(in_turned, 1)

            def turn_hidden(m):
                pe.wait_ge(gated_ready, m + 1)
                pe.wait_ge(hT_ready, m + 1)
                for f in range(UP_F):
                    for t in range(NT):
                        mm = pe.transpose(T[:, f * SEQ + t * P:f * SEQ + (t + 1) * P],
                                          gated[:, t, f * P:(f + 1) * P], ident[:, :])
                mm.then_inc(hid_turned, 1)

            def up_chunk(q, accs, m):
                for s in range(STAGES):
                    split_block(accs, xT, q, s, s * BK, BK, s == 0, s == STAGES - 1)
                    if s == 0:
                        turn_hidden(m - 1)

            def first_chunk(q, n0, src_ready):
                turn_quarter(n0, 0, src_ready)
                for s in range(STAGES):
                    if s + 1 < STAGES:
                        turn_quarter(n0, s + 1, src_ready)
                    pe.wait_ge(in_ready, n0 + 2 * (s + 1))
                    split_block(A, xT, q, s, s * BK, BK, s == 0, s == STAGES - 1)

            def up(q0, m0):
                with pe.Fori(0, (UP_CHUNKS - 2) // 2) as i:
                    up_chunk(q0 + 1 + 2 * i, B, m0 + 1 + 2 * i)
                    up_chunk(q0 + 2 + 2 * i, A, m0 + 2 + 2 * i)
                up_chunk(q0 + UP_CHUNKS - 1, B, m0 + UP_CHUNKS - 1)
                turn_hidden(m0 + UP_CHUNKS - 1)

            def down(q0, m0, d0):
                with pe.Fori(0, DOWN_CHUNKS // 2) as i:
                    for j, accs in enumerate((A, B)):
                        if j == 1:
                            pe.wait_ge(down_added, d0 + 2 * i + 1)
                        for b, k in enumerate(DOWN_K):
                            if j == 0 and b == DOWN_BLOCKS - 1:
                                pe.wait_ge(hT_ready, m0 + UP_CHUNKS + 1)
                            split_block(accs, hT, q0 + (2 * i + j) * (DOWN_BLOCKS // STAGES) + b // STAGES,
                                        b % STAGES, sum(DOWN_K[:b]), k, b == 0, b == DOWN_BLOCKS - 1)
                    pe.wait_ge(down_added, d0 + 2 * i + 2)

            pe.sem_inc(c_used, 1)
            pe.wait_ge(ident_ready, 2)
            first_chunk(Q_UP1, 0, lambda q: pe.wait_ge(x_loaded[q], 16))
            pe.wait_ge(vecs_loaded, 16 * 6)
            pe.transpose(bank[7][:, 0:P], vecs[:, :], ident[:, :])
            pe.transpose(bank[7][:, P:P + 4], b1rows[:, :], ident[0:4, 0:4]).then_inc(vecs_turned, 1)
            up(Q_UP1, 0)
            down(Q_DOWN1, 0, 0)

            def proj_chunk(p, accs):
                for s in range(STAGES):
                    split_block(accs, xT, Q_PROJ + p, s, s * BK, BK, s == 0, s == STAGES - 1)

            def compress(cb):
                pe.wait_ge(c_lo_ready, cb + 1)
                pe.wait_ge(hid_added, cb + 1)
                for k in range(CMP_K):
                    mm = product(bank[7][0:ROWS_CMP, 0:CMP_HIDDEN], (flat_now_hi[:, k, :], flat_now_lo[:, k, :]),
                                 (c_hi[:, k, :], c_lo[:, k, :]), k == 0, k == CMP_K - 1)
                mm.then_inc(c_used, 1)

            first_chunk(Q_PROJ, KT // 2, lambda q: pe.wait_ge(z_ready, q + 1))
            split_block(B, xT, Q_PROJ + 1, 0, 0, BK, True, False)
            pe.wait_ge(proj_copied_a, 1)
            pe.wait_ge(proj_copied_v, 1)
            for a in range(4):
                for t in range(NT):
                    mm = pe.transpose(bank[5 + a // 2][:, (a % 2) * SEQ + t * P:(a % 2) * SEQ + (t + 1) * P],
                                      proj[:, t, a * HD:(a + 1) * HD], ident[:, :])
            mm.then_inc(tok_turned, 1)
            split_block(B, xT, Q_PROJ + 1, 1, BK, BK, False, False)
            pe.wait_ge(wg_ready, 1)
            for k in range(KT):
                mm = product(T[0:N_GATE, 0:SEQ], (wg_hi[:, k, :], wg_lo[:, k, :]),
                             (xT_hi[:, k, :], xT_lo[:, k, :]), k == 0, k == KT - 1)
            mm.then_inc(gate_summed, 1)
            split_block(B, xT, Q_PROJ + 1, 2, 2 * BK, BK, False, False)
            split_block(B, xT, Q_PROJ + 1, 3, 3 * BK, BK, False, True)
            pe.wait_ge(gatesT_ready, 1)
            for t in range(NT):
                mm = pe.transpose(T[:, SEQ + t * 32:SEQ + t * 32 + N_GATE], gatesT[:, t * P:(t + 1) * P],
                                  ident[0:N_GATE, 0:N_GATE])
            mm.then_inc(gates_turned, 1)
            with pe.Fori(0, (PROJ_CHUNKS - 2) // 2) as i:
                for j, accs in enumerate((A, B)):
                    pe.wait_ge(proj_copied_a, 2 * i + j + 1)
                    pe.wait_ge(proj_copied_v, 2 * i + j + 1)
                    proj_chunk(2 * i + j + 2, accs)
                    compress(2 * i + j)

            pe.wait_ge(roped, len(ROPE_RUNS))
            pe.wait_ge(hid_added, CMP_BLOCKS + 1)
            for a in range(4):
                mm = pe.transpose(bank[5][:, a * 32:a * 32 + ROWS_CMP],
                                  hid_sum[:, a // 2, (a % 2) * P:(a % 2 + 1) * P],
                                  ident[0:ROWS_CMP, 0:ROWS_CMP])
            mm.then_inc(sums_turned, 1)
            for n in range(len(TURNED) // 2):
                if n >= 2:
                    pe.wait_ge(qk_odd if n % 2 else qk_even, n // 2)
                for a in range(2):
                    for t in range(NT):
                        col = TURNED[2 * n + a]
                        mm = pe.transpose(bank[6 + n % 2][:, a * SEQ + t * P:a * SEQ + (t + 1) * P],
                                          proj[:, t, col:col + HD], ident[:, :])
                mm.then_inc(qk_turned, 1)
            pe.wait_ge(qk_even, 7)
            pe.wait_ge(qk_odd, 6)
            pe.wait_ge(gates_ready, 1)
            pe.wait_ge(proj_copied_a, PROJ_CHUNKS)
            pe.wait_ge(proj_copied_v, PROJ_CHUNKS)

            def q_slot(h):
                return T_QA + h if h < N_DIL else T_QN + h - N_DIL

            def scores(u):
                h, t, br = UNITS[u]
                k = {"dil": T_KA + h, "slc": T_KS + (h - N_DIL) // NSA_GROUP,
                     "win": T_KW + (h - N_DIL) // NSA_GROUP}[br]
                if u >= 2:
                    pe.wait_ge(masked_ready, u - 1)
                n = (t + 1) * P
                pe.matmul(bank[u % 2][:, 0:n], qkT[:, q_slot(h), t * P:(t + 1) * P], qkT[:, k, 0:n],
                          start=True, stop=True).then_inc(scored, 1)

            def turn_probs(u):
                h, t, br = UNITS[u]
                pe.wait_ge(probs_ready, u + 1)
                if u >= 2:
                    pe.wait_ge(*taken(u - 2))
                for k in range(t + 1):
                    mm = pe.transpose(bank[2 + u % 2][:, k * P:(k + 1) * P],
                                      probs[:, u % E_RING, k * P:(k + 1) * P], ident[:, :])
                if br == "slc":
                    pe.wait_ge(cmp_ready, 1)
                    mm = pe.transpose(bank[2 + u % 2][0:N_CMP, 2 * P:3 * P], cpr[:, t, h - N_DIL, :],
                                      ident[:, :])
                mm.then_inc(probs_turned, 1)

            def values(u):
                h, t, br = UNITS[u]
                if t == 0 and br != "win" and h >= 2:
                    pe.wait_ge(mix_ready, h - 1)
                pe.wait_ge(*taken(u))
                g = (h - N_DIL) // NSA_GROUP
                o = bank[4 + h % 2][:, t * P:(t + 1) * P]
                col = {"dil": COL_VA + h * HD if h < 4 else COL_VA_TAIL + (h - 4) * HD,
                       "slc": COL_VS + g * HD, "win": COL_VW + g * HD}[br]
                if br == "slc":
                    pe.matmul(o, kvc[:, 2 + g, :], cprT[:, t, :], start=True, stop=False)
                for k in range(t + 1):
                    mm = pe.matmul(o, proj[:, k, col:col + HD], probsT[:, u % 2, k, :],
                                   start=(br == "dil" and k == 0), stop=(br != "slc" and k == t))
                mm.then_inc(valued, 1)

            for step in range(NU + LAG_PV):
                if step < NU:
                    scores(step)
                if step == STEP_CMP_OUT:
                    pe.wait_ge(hidT_ready, 4)
                    pe.wait_ge(cw2_loaded, 32)
                    for a in range(4):
                        j, g = a // 2, a % 2
                        for half in range(2):
                            mm = pe.matmul(bank[6][0:N_CMP, a * HD:(a + 1) * HD],
                                           hidT[:, j, half, g * N_CMP:(g + 1) * N_CMP],
                                           cw2[:, 2 * j + half, :], start=(half == 0), stop=(half == 1))
                    mm.then_inc(kvc_summed, 1)
                if step == STEP_CMP_TURN:
                    pe.wait_ge(kvc_ready, 1)
                    for g in range(KV_GROUPS):
                        mm = pe.transpose(bank[7][:, g * N_CMP:(g + 1) * N_CMP], kvc[:, g, :],
                                          ident[0:N_CMP, 0:N_CMP])
                    mm.then_inc(kc_turned, 1)
                if step == STEP_CMP_SCORE:
                    pe.wait_ge(kcT_ready, 1)
                    for t in range(NT):
                        for h in range(N_NSA):
                            c = (t * N_NSA + h) * N_CMP
                            mm = pe.matmul(bank[6][:, c:c + N_CMP], qkT[:, T_QN + h, t * P:(t + 1) * P],
                                           kcT[:, h // NSA_GROUP, :], start=True, stop=True)
                    mm.then_inc(cmp_scored, 1)
                if step >= LAG_TURN and step - LAG_TURN < NU:
                    turn_probs(step - LAG_TURN)
                if step >= LAG_PV:
                    values(step - LAG_PV)

            pe.wait_ge(mix_ready, N_DIL + N_NSA)
            with pe.Fori(0, OUT_CHUNKS // 2) as i:
                for j, accs in enumerate((A, B)):
                    if j == 1:
                        pe.wait_ge(out_added, 2 * i + 1)
                    for s in range(STAGES):
                        split_block(accs, xT, Q_OUT + 2 * i + j, s, s * BK, BK, s == 0, s == STAGES - 1)
                pe.wait_ge(out_added, 2 * i + 2)
            first_chunk(Q_UP2, KT, lambda q: pe.wait_ge(z_ready, 4 + q + 1))
            up(Q_UP2, UP_CHUNKS)
            down(Q_DOWN2, UP_CHUNKS, DOWN_CHUNKS)

        @block.scalar
        def _(act):
            def hi(q, s):
                act.wait_ge(stage_full[s], 32 * q + 32)
                if not (isinstance(q, int) and 4 * q + s < SPLITS):
                    act.wait_ge(block_used, 4 * q + s + 1 - SPLITS)
                act.activation(w_hi[:, s % SPLITS, :, :], stage[:, s, :, :], ACT.Copy).then_inc(hi_ready, 1)

            def full_quarter(n0, q, vec):
                for j in (2 * q, 2 * q + 1):
                    n = n0 + j
                    act.wait_ge(in_turned, n + 1)
                    if n >= 2:
                        act.wait_ge(in_ready, n - 1)
                    if vec is None:
                        act.activation(turned_f32[:, n % 2, :], bank[5 + n % 2][:, :], ACT.Copy
                                       ).then_inc(in_full, 1)
                        continue
                    for k in range(2):
                        kt = 2 * j + k
                        a = act.activation(turned_f32[:, n % 2, k * SEQ:(k + 1) * SEQ],
                                           bank[5 + n % 2][:, k * SEQ:(k + 1) * SEQ], ACT.Identity,
                                           scale=vecsT[:, vec + kt:vec + kt + 1],
                                           bias=vecsT[:, vec + KT + kt:vec + KT + kt + 1])
                    a.then_inc(in_full, 1)

            def first_blocks(q, n0, vec):
                full_quarter(n0, 0, vec)
                if vec is None:
                    hi(q, 0)
                full_quarter(n0, 1, vec)
                if vec is None:
                    hi(q, 1)
                full_quarter(n0, 2, vec)
                hi(q, 2)
                full_quarter(n0, 3, vec)
                hi(q, 3)
                hi(q + 1, 0)

            def up_step(q, accs, m, m0, turn):
                if turn:
                    hi(q, 1)
                    hi(q, 2)
                    act.wait_ge(hid_turned, m)
                    act.activation(hT_hi[:, bass.ds(UP_F * (m - 1 - m0), UP_F), :],
                                   bank[4][:, :].rearrange("p (f n) -> p f n", f=UP_F), ACT.Copy
                                   ).then_inc(hT_hi_ready, 1)
                    hi(q, 3)
                    hi(q + 1, 0)
                act.wait_ge(block_used, 4 * q + 4)
                for t in range(NT):
                    act.activation(silu[:, t, :], accs[t][:, 0:UP_COLS], ACT.Silu).then_inc(silu_ready, 1)

            A, B = bank[0:2], bank[2:4]

            def up(q0, m0):
                up_step(q0, A, m0, m0, False)
                with act.Fori(0, (UP_CHUNKS - 2) // 2) as i:
                    up_step(q0 + 1 + 2 * i, B, m0 + 1 + 2 * i, m0, True)
                    up_step(q0 + 2 + 2 * i, A, m0 + 2 + 2 * i, m0, True)
                m = m0 + UP_CHUNKS - 1
                up_step(q0 + UP_CHUNKS - 1, B, m, m0, True)
                act.wait_ge(hid_turned, m + 1)
                act.activation(hT_hi[:, FT - UP_F:FT, :], bank[4][:, :].rearrange("p (f n) -> p f n", f=UP_F),
                               ACT.Copy).then_inc(hT_hi_ready, 1)

            def std_of(l):
                act.activation(warm[:, l:l + 1], eps_t[:, :], ACT.Sqrt)
                act.wait_ge(aggr_ready, l + 1)
                act.activation(std[:, :], mv[:, :, 1], ACT.Sqrt, bias=eps_t[:, :]).then_inc(std_ready, 1)

            for t in range(NT):
                act.dma_start(pos_i[:, t:t + 1], positions[0, t * P:(t + 1) * P].rearrange("(p a) -> p a", a=1)
                              ).then_inc(pos_loaded, 16)
            for a, start in enumerate((0, CMP_BLOCK - CMP_STRIDE)):
                tok = positions[0, start:start + N_CMP * CMP_STRIDE].rearrange("(n c) -> n c", c=CMP_STRIDE)
                col = (0, CMP_STRIDE - 1)[a]
                act.dma_start(pos_i[0:N_CMP, NT + a:NT + a + 1], tok[:, col:col + 1],
                              allow_slow_non_contiguous=True).then_inc(pos_loaded, 16)
            act.dma_start(invf_bc[:, :], inv_freq[0:1, :].broadcast_to([P, HD // 2])).then_inc(pos_loaded, 16)
            for r, v in enumerate((ln1_g, ln1_b, ln2_g, ln2_b)):
                act.dma_start(vecs[r * KT:(r + 1) * KT, :], v[0].rearrange("(k p) -> k p", p=P)
                              ).then_inc(vecs_loaded, 16)
            act.dma_start(vecs[4 * KT:P, :], cmp_pe[0].rearrange("j c d -> (j c) d")).then_inc(vecs_loaded, 16)
            act.dma_start(b1rows[:, :], cmp_b1[0].rearrange("j (h p) -> (j h) p", p=P)).then_inc(vecs_loaded, 16)
            first_blocks(Q_UP1, 0, None)
            act.wait_ge(red_ready, 1)
            act.activation(sin_t[:, :, :], red[:, 0, 0:NT, :], ACT.Sin)
            act.activation(cos_t[:, :, :], red[:, 1, 0:NT, :], ACT.Sin)
            act.activation(cos_c[:, 1, :], red[:, 0, NT, :], ACT.Sin)
            act.activation(cos_c[:, 0, :], red[:, 1, NT, :], ACT.Sin).then_inc(trig_ready, 1)
            up(Q_UP1, 0)
            hi(Q_DOWN1, 1)
            with act.Fori(0, DOWN_CHUNKS) as n:
                for b in range(2, DOWN_BLOCKS + 2):
                    hi(Q_DOWN1 + (DOWN_BLOCKS // STAGES) * n + b // STAGES, b % STAGES)
            std_of(0)

            def compress_hi(i, j):
                cb = 2 * i + j
                act.wait_ge(cstage_full, 16 * cb + 16)
                act.wait_ge(c_used, cb + 1)
                act.activation(flat_now_hi[:, :, :], flat_hi[:, flat_rows(i, j), :], ACT.Copy)
                act.activation(c_hi[:, :, :], cstage[:, :, :], ACT.Copy).then_inc(c_hi_ready, 1)

            def load_compress(i, j):
                act.dma_start(cstage[:, :, :], cmp_w1[0][j].rearrange("(b k p) n -> p b k n", k=CMP_K, p=P)[
                    :, bass.ds(i, 1), :, :].rearrange("p a k n -> p (a k) n")).then_inc(cstage_full, 16)

            def proj_step(p, accs, cmp=None):
                if isinstance(p, int) and p == 0:
                    first_blocks(Q_PROJ, KT // 2, 0)
                else:
                    hi(Q_PROJ + p, 1)
                    hi(Q_PROJ + p, 2)
                    if cmp is not None:
                        compress_hi(*cmp)
                    hi(Q_PROJ + p, 3)
                    hi(Q_PROJ + p + 1, 0)
                if isinstance(p, int) and p == 1:
                    act.wait_ge(gate_summed, 1)
                    act.wait_ge(attn_loaded, 16 * 4)
                    act.activation(gatesT[:, :], bank[4][0:N_GATE, 0:SEQ], ACT.Sigmoid, bias=gate_bT[:, :]
                                   ).then_inc(gatesT_ready, 1)
                act.wait_ge(block_used, 4 * (Q_PROJ + p) + 4)
                act.activation(proj[:, 0, bass.ds(p * BN, BN)], accs[0][:, :], ACT.Copy
                               ).then_inc(proj_copied_a, 1)

            proj_step(0, A)
            proj_step(1, B)
            act.wait_ge(flat_ready, 2)
            load_compress(0, 0)
            with act.Fori(0, (PROJ_CHUNKS - 4) // 2) as i:
                proj_step(2 * i + 2, A, (i, 0))
                act.wait_ge(c_lo_ready, 2 * i + 1)
                load_compress(i, 1)
                proj_step(2 * i + 3, B, (i, 1))
                act.wait_ge(c_lo_ready, 2 * i + 2)
                load_compress(i + 1, 0)
            last = CMP_BLOCKS // 2 - 1
            proj_step(PROJ_CHUNKS - 2, A, (last, 0))
            act.wait_ge(c_lo_ready, CMP_BLOCKS - 1)
            load_compress(last, 1)
            proj_step(PROJ_CHUNKS - 1, B, (last, 1))

            act.wait_ge(sums_turned, 1)
            for j in range(2):
                for half in range(2):
                    a = 2 * j + half
                    act.activation(hidT[:, j, half, :], bank[5][:, a * 32:a * 32 + ROWS_CMP], ACT.Gelu_apprx_tanh,
                                   bias=b1T[:, 2 * j + half:2 * j + half + 1]).then_inc(hidT_ready, 1)
            for n in range(1, len(TURNED) // 2, 2):
                act.wait_ge(qk_turned, n + 1)
                act.activation(qkT[:, 2 * n:2 * n + 2, :], bank[7][:, :].rearrange("p (a n) -> p a n", a=2),
                               ACT.Copy).then_inc(qk_odd, 1)

            def exps(u):
                h, t, br = UNITS[u]
                n = (t + 1) * P
                act.wait_ge(masked_ready, u + 1)
                if u >= E_RING:
                    act.wait_ge(probs_turned, u - E_RING + 1)
                act.activation(probs[:, u % E_RING, 0:n], masked[:, u % MASKED_RING, 0:n], ACT.Exp,
                               bias=negmax[:, u:u + 1], scale=-1.0, accum_out=rowsum[:, u:u + 1]
                               ).then_inc(exp_ready, 1)

            def take_turned(u):
                h, t, br = UNITS[u]
                act.wait_ge(probs_turned, u + 1)
                if u >= 2:
                    act.wait_ge(valued, u - 1)
                if br == "slc":
                    act.activation(cprT[:, t, :], bank[2 + u % 2][0:N_CMP, 2 * P:3 * P], ACT.Copy)
                act.activation(probsT[:, u % 2, 0:t + 1, :],
                               bank[2 + u % 2][:, 0:(t + 1) * P].rearrange("p (k n) -> p k n", n=P), ACT.Copy
                               ).then_inc(probsT_ready[t], 1)

            def mix_hi(h):
                act.wait_ge(valued, HEAD_LAST[h] + 1)
                act.activation(xT_hi[:, h, :], bank[4 + h % 2][:, 0:SEQ], ACT.Copy).then_inc(mix_hi_ready, 1)

            for step in range(NU + LAG_PV):
                if step < NU:
                    exps(step)
                if step == STEP_CMP_SCORE + 2:
                    act.wait_ge(cmp_shifted, 1)
                    act.activation(cex[:, :, :, :], csc[:, :, :, :], ACT.Exp, scale=SCALE).then_inc(cmp_exp, 1)
                if step >= LAG_TURN and step - LAG_TURN < NU and UNITS[step - LAG_TURN][1] == 1:
                    take_turned(step - LAG_TURN)
                if step == NU + 1:
                    hi(Q_OUT, 1)
                for h in HEAD_LAST:
                    if HEAD_LAST[h] == step - LAG_PV:
                        mix_hi(h)

            with act.Fori(0, OUT_CHUNKS) as n:
                for b in range(2, STAGES + 2):
                    hi(Q_OUT + n + b // STAGES, b % STAGES)
            std_of(1)

            first_blocks(Q_UP2, KT, 2 * KT)
            up(Q_UP2, UP_CHUNKS)
            for b in range(1, DOWN_CHUNKS * DOWN_BLOCKS):
                hi(Q_DOWN2 + b // STAGES, b % STAGES)
            std_of(2)
            act.wait_ge(rstd_ready, 3)
            for q in range(4):
                piece = resid[:, 1, q * BN:(q + 1) * BN]
                act.activation(piece, piece, ACT.Identity, scale=rstd[:, 1:2], bias=nmr[:, 1:2]
                               ).then_inc(z_ready, 1)

        @block.vector
        def _(dve):
            A, B = bank[0:2], bank[2:4]

            def lo(q, s):
                dve.wait_ge(hi_ready, 4 * q + s + 1)
                dve.tensor_tensor(w_lo[:, s % SPLITS, :, :], stage[:, s, :, :], w_hi[:, s % SPLITS, :, :],
                                  ALU.subtract).then_inc(lo_ready, 1)

            def split_quarter(n0, q):
                for j in (2 * q, 2 * q + 1):
                    n = n0 + j
                    src = turned_f32[:, n % 2, :].rearrange("p (k n) -> p k n", k=2)
                    dve.wait_ge(in_full, n + 1)
                    dve.tensor_copy(xT_hi[:, 2 * j:2 * j + 2, :], src).then_inc(in_hi, 1)
                    dve.wait_ge(in_hi, n + 1)
                    dve.tensor_tensor(xT_lo[:, 2 * j:2 * j + 2, :], src, xT_hi[:, 2 * j:2 * j + 2, :],
                                      ALU.subtract).then_inc(in_ready, 1)

            def hidden_lo(m, f):
                dve.wait_ge(hT_hi_ready, m + 1)
                part = (slice(None), bass.ds(f, UP_F), slice(None))
                dve.tensor_tensor(hT_lo[part], bank[4][:, :].rearrange("p (f n) -> p f n", f=UP_F),
                                  hT_hi[part], ALU.subtract).then_inc(hT_ready, 1)

            def first_blocks(q, n0, vec=0, between=()):
                split_quarter(n0, 0)
                if vec is None:
                    lo(q, 0)
                split_quarter(n0, 1)
                if vec is None:
                    lo(q, 1)
                split_quarter(n0, 2)
                lo(q, 2)
                split_quarter(n0, 3)
                for work in between[:1]:
                    work()
                lo(q, 3)
                for work in between[1:]:
                    work()
                lo(q + 1, 0)

            def up_step(q, accs, m, m0, turn):
                if turn:
                    lo(q, 1)
                    lo(q, 2)
                    hidden_lo(m - 1, UP_F * (m - 1 - m0))
                    lo(q, 3)
                    lo(q + 1, 0)
                for t in range(NT):
                    dve.wait_ge(silu_ready, 2 * m + t + 1)
                    g = dve.tensor_tensor(gated[:, t, :], silu[:, t, :], accs[t][:, UP_COLS:BN], ALU.mult)
                g.then_inc(gated_ready, 1)

            def up(q0, m0, r):
                up_step(q0, A, m0, m0, False)
                with dve.Fori(0, (UP_CHUNKS - 2) // 2) as i:
                    up_step(q0 + 1 + 2 * i, B, m0 + 1 + 2 * i, m0, True)
                    up_step(q0 + 2 + 2 * i, A, m0 + 2 + 2 * i, m0, True)
                dve.wait_ge(resid_ready, r)
                m = m0 + UP_CHUNKS - 1
                up_step(q0 + UP_CHUNKS - 1, B, m, m0, True)
                hidden_lo(m, FT - UP_F)

            def add(accs, q_end, n, factor, added):
                dve.wait_ge(block_used, 4 * q_end)
                cols = bass.ds(n * BN, BN)
                for t in range(NT):
                    a = dve.scalar_tensor_tensor(out=resid[:, t, cols], in0=accs[t][:, :], scalar=factor,
                                                 in1=resid[:, t, cols], op0=ALU.mult, op1=ALU.add)
                a.then_inc(added, 1)

            def stats(n, added, a0):
                cols = bass.ds(n * BN, BN)
                dve.wait_ge(added, a0 + n + 2)
                for t in range(NT):
                    a = dve.bn_stats(bn[:, t, bass.ds(n, 1), :].rearrange("p a s -> p (a s)"), resid[:, t, cols])
                a.then_inc(stat_step, 1)

            def down_step(q0, n, accs, a0, last=False):
                per = DOWN_BLOCKS // STAGES
                for b in range(2, DOWN_BLOCKS + (not last)):
                    lo(q0 + per * n + b // STAGES, b % STAGES)
                add(accs, q0 + per * (n + 1), n, 0.5, down_added)
                if not last:
                    lo(q0 + per * (n + 1), 1)
                stats(n, down_added, a0)

            def norm(l, s_end):
                dve.wait_ge(stat_step, s_end)
                for t in range(NT):
                    a = dve.bn_aggr(mv[:, t, :], bn[:, t, :, :].rearrange("p c s -> p (c s)"))
                a.then_inc(aggr_ready, 1)
                dve.wait_ge(std_ready, l + 1)
                if l < 2:
                    dve.reciprocal(rstd[:, :], std[:, :]).then_inc(rstd_ready, 1)
                    dve.wait_ge(rstd_ready, l + 1)
                    for q in range(4):
                        for t in range(NT):
                            piece = resid[:, t, q * BN:(q + 1) * BN]
                            a = dve.tensor_scalar(piece, piece, mv[:, t, 0:1], rstd[:, t:t + 1],
                                                  ALU.subtract, ALU.mult)
                        a.then_inc(z_ready, 1)

            steps = [0]

            def step(ins):
                ins.then_inc(pos_step, 1)
                steps[0] += 1
                dve.wait_ge(pos_step, steps[0])

            for counter in (hT_ready, down_added, out_added):
                dve.sem_inc(counter, 1)

            def angles():
                dve.memset(ang[:, :, :], 0.0)
                dve.wait_ge(pos_loaded, 16 * 5)
                dve.tensor_copy(pos_f[:, 0:NT], pos_i[:, 0:NT])
                step(dve.tensor_tensor(pos_f[0:N_CMP, NT:NT + 1], pos_i[0:N_CMP, NT:NT + 1],
                                       pos_i[0:N_CMP, NT + 1:NT + 2], ALU.add))
                for t in range(NT):
                    dve.tensor_scalar(ang[:, t, :], invf_bc[:, :], pos_f[:, t:t + 1], None, ALU.mult)
                step(dve.tensor_scalar(ang[0:N_CMP, NT, :], invf_bc[0:N_CMP, :], pos_f[0:N_CMP, NT:NT + 1], 0.5,
                                       ALU.mult, ALU.mult))
                step(dve.tensor_scalar(turns[:, :, :], ang[:, :, :], 0.15915494309189535, MAGIC, ALU.mult, ALU.add))
                step(dve.tensor_scalar(turns[:, :, :], turns[:, :, :], MAGIC, None, ALU.subtract))

            def reduced_angles():
                for part in (TWO_PI_1, TWO_PI_2, TWO_PI_3):
                    step(dve.scalar_tensor_tensor(out=ang[:, :, :], in0=turns[:, :, :], scalar=-part, in1=ang[:, :, :],
                                                  op0=ALU.mult, op1=ALU.add))
                step(dve.tensor_scalar(red[:, 0], ang[:, :, :], PI, -PI, ALU.min, ALU.max))
                step(dve.tensor_scalar(ang[:, :, :], red[:, 0], PI / 2, None, ALU.add))
                step(dve.tensor_scalar(turns[:, :, :], ang[:, :, :], PI, -2 * 3.141592653589793, ALU.is_gt, ALU.mult))
                step(dve.tensor_tensor(ang[:, :, :], ang[:, :, :], turns[:, :, :], ALU.add))
                dve.tensor_scalar(red[:, 1], ang[:, :, :], PI, -PI, ALU.min, ALU.max).then_inc(red_ready, 1)

            first_blocks(Q_UP1, 0, None, (angles, reduced_angles))
            dve.wait_ge(vecs_turned, 1)
            dve.tensor_copy(vecsT[:, :], bank[7][:, 0:P])
            dve.tensor_copy(b1T[:, :], bank[7][:, P:P + 4]).then_inc(vecs_ready, 1)
            up(Q_UP1, 0, 1)
            lo(Q_DOWN1, 1)
            with dve.Fori(0, DOWN_CHUNKS // 2) as i:
                for j, accs in enumerate((A, B)):
                    down_step(Q_DOWN1, 2 * i + j, accs, 0)
            norm(0, 4)

            def proj_step(p, accs, between=None, cmp=None):
                if isinstance(p, int) and p == 0:
                    first_blocks(Q_PROJ, KT // 2)
                else:
                    proj_blocks(p, between, cmp)
                dve.wait_ge(block_used, 4 * (Q_PROJ + p) + 4)
                dve.tensor_copy(proj[:, 1, bass.ds(p * BN, BN)], accs[1][:, :]).then_inc(proj_copied_v, 1)
                if cmp is not None:
                    i, j = cmp
                    dve.wait_ge(c_used, 2 * i + j + 2)
                    dve.wait_ge(hid_added, 2 * i + j + 1)
                    dve.tensor_tensor(hid_sum[:, j, :], bank[7][0:ROWS_CMP, 0:CMP_HIDDEN], hid_sum[:, j, :],
                                      ALU.add).then_inc(hid_added, 1)

            def proj_blocks(p, between, cmp):
                lo(Q_PROJ + p, 1)
                if between:
                    between()
                lo(Q_PROJ + p, 2)
                if cmp is not None:
                    i, j = cmp
                    dve.wait_ge(c_hi_ready, 2 * i + j + 1)
                    dve.tensor_copy(flat_now_lo[:, :, :], flat_lo[:, flat_rows(i, j), :])
                    dve.tensor_tensor(c_lo[:, :, :], cstage[:, :, :], c_hi[:, :, :], ALU.subtract
                                      ).then_inc(c_lo_ready, 1)
                lo(Q_PROJ + p, 3)
                lo(Q_PROJ + p + 1, 0)

            def take_tokens():
                dve.wait_ge(tok_turned, 1)
                for a in range(2):
                    c = dve.tensor_copy(tokT[:, 2 * a:2 * a + 2, :],
                                        bank[5 + a][:, :].rearrange("p (a n) -> p a n", a=2))
                c.then_inc(tok_copied, 1)

            proj_step(0, A)
            proj_step(1, B, take_tokens)
            dve.memset(hid_sum[:, :, :], 0.0).then_inc(hid_added, 1)
            dve.wait_ge(gates_turned, 1)
            dve.tensor_copy(gates[:, :, :], bank[4][:, SEQ:SEQ + 64].rearrange("p (t n) -> p t n", n=32)[
                :, :, 0:N_GATE]).then_inc(gates_ready, 1)
            with dve.Fori(0, (PROJ_CHUNKS - 2) // 2) as i:
                proj_step(2 * i + 2, A, None, (i, 0))
                proj_step(2 * i + 3, B, None, (i, 1))

            for n in range(0, len(TURNED) // 2, 2):
                dve.wait_ge(qk_turned, n + 1)
                dve.tensor_copy(qkT[:, 2 * n:2 * n + 2, :], bank[6][:, :].rearrange("p (a n) -> p a n", a=2)
                                ).then_inc(qk_even, 1)

            def mask_scores(u):
                h, t, br = UNITS[u]
                n = (t + 1) * P
                m = dmask if br == "dil" else cmask
                dve.wait_ge(scored, u + 1)
                if u >= MASKED_RING:
                    dve.wait_ge(exp_ready, u - MASKED_RING + 1)
                dve.tensor_tensor_reduce(masked[:, u % MASKED_RING, 0:n], bank[u % 2][:, 0:n], m[:, SEQ - n:SEQ],
                                         -SCALE, 3e38, ALU.add, ALU.min, negmax[:, u:u + 1]
                                         ).then_inc(masked_ready, 1)

            def invert(u):
                dve.wait_ge(exp_ready, u + 1)
                dve.reciprocal(rinv[:, u:u + 1], rowsum[:, u:u + 1]).then_inc(inv_ready, 1)

            def take_turned(u):
                h, t, br = UNITS[u]
                dve.wait_ge(probs_turned, u + 1)
                if u >= 2:
                    dve.wait_ge(valued, u - 1)
                if br == "slc":
                    dve.tensor_copy(cprT[:, t, :], bank[2 + u % 2][0:N_CMP, 2 * P:3 * P])
                dve.tensor_copy(probsT[:, u % 2, 0:t + 1, :],
                                bank[2 + u % 2][:, 0:(t + 1) * P].rearrange("p (k n) -> p k n", n=P)
                                ).then_inc(probsT_ready[t], 1)

            def mix_lo(h):
                dve.wait_ge(mix_hi_ready, h + 1)
                dve.tensor_tensor(xT_lo[:, h, :], bank[4 + h % 2][:, 0:SEQ], xT_hi[:, h, :], ALU.subtract
                                  ).then_inc(mix_ready, 1)

            def chain(sem_, count):
                def go(ins):
                    ins.then_inc(sem_, 1)
                    count[0] += 1
                    dve.wait_ge(sem_, count[0])
                return go

            def compressed_kv():
                go = chain(kvc_step, [0])
                dve.wait_ge(kvc_summed, 1)
                go(dve.tensor_tensor(kvc[:, :, :].rearrange("p (j g) d -> p j g d", j=2),
                                     bank[6][0:N_CMP, :].rearrange("p (j g d) -> p j g d", j=2, g=2),
                                     b2_bc[:, :, :].unsqueeze(2).broadcast_to([N_CMP, 2, KV_GROUPS, HD]), ALU.add))
                k = kvc[:, 0:KV_GROUPS, :].rearrange("p g (x d) -> p g x d", x=2)
                cos = cos_c[0:N_CMP, 0, :].unsqueeze(1).unsqueeze(1).broadcast_to([N_CMP, KV_GROUPS, 2, HD // 2])
                sin = cos_c[0:N_CMP, 1, :].unsqueeze(1).unsqueeze(1).broadcast_to([N_CMP, KV_GROUPS, 2, HD // 2])
                dve.tensor_tensor(crt[:, 0], k, cos, ALU.mult)
                go(dve.tensor_tensor(crt[:, 1], k, sin, ALU.mult))
                dve.tensor_tensor(k[:, :, 0, :], crt[:, 0, :, 0, :], crt[:, 1, :, 1, :], ALU.subtract)
                dve.tensor_tensor(k[:, :, 1, :], crt[:, 0, :, 1, :], crt[:, 1, :, 0, :], ALU.add
                                  ).then_inc(kvc_ready, 1)

            def compressed_softmax_a():
                go = chain(cmp_step, [0])
                dve.wait_ge(cmp_scored, 1)
                for t in range(NT):
                    a = dve.tensor_tensor(
                        csc[:, t], bank[6][:, t * N_NSA * N_CMP:(t + 1) * N_NSA * N_CMP].rearrange(
                            "p (h n) -> p h n", n=N_CMP),
                        cmpm[:, 0, t, :].unsqueeze(1).broadcast_to([P, N_NSA, N_CMP]), ALU.add)
                go(a)
                go(dve.tensor_reduce(cst[:, 0], csc[:, :, :, :], AX.X, ALU.max))
                dve.tensor_tensor(csc[:, :, :, :], csc[:, :, :, :],
                                  cst[:, 0].unsqueeze(3).broadcast_to([P, NT, N_NSA, N_CMP]), ALU.subtract
                                  ).then_inc(cmp_shifted, 1)

            def compressed_softmax_b():
                go = chain(cmp_step, [2])
                dve.wait_ge(cmp_exp, 1)
                for t in range(NT):
                    a = dve.tensor_tensor(cex[:, t], cex[:, t],
                                          cmpm[:, 1, t, :].unsqueeze(1).broadcast_to([P, N_NSA, N_CMP]), ALU.mult)
                go(a)
                go(dve.tensor_reduce(cst[:, 1], cex[:, :, :, :], AX.X, ALU.add))
                go(dve.tensor_scalar(cst[:, 2], cst[:, 1], 1e-30, None, ALU.max))
                go(dve.reciprocal(cst[:, 1], cst[:, 2]))
                go(dve.tensor_tensor(cst[:, 3], cst[:, 1],
                                     gates[:, :, :].rearrange("p t (h b) -> p t h b", b=N_BRANCH)[:, :, :, 0],
                                     ALU.mult))
                dve.tensor_tensor(cpr[:, :, :, :], cex[:, :, :, :],
                                  cst[:, 3].unsqueeze(3).broadcast_to([P, NT, N_NSA, N_CMP]), ALU.mult
                                  ).then_inc(cmp_ready, 1)

            dve.wait_ge(attn_loaded, 16 * 4)
            for s in range(NU + LAG_PV):
                if s < NU:
                    mask_scores(s)
                if s == STEP_CMP_OUT + 2:
                    compressed_kv()
                if s == STEP_CMP_TURN + 1:
                    dve.wait_ge(kc_turned, 1)
                    dve.tensor_copy(kcT[:, :, :], bank[7][:, 0:ROWS_CMP].rearrange("p (g n) -> p g n", g=KV_GROUPS)
                                    ).then_inc(kcT_ready, 1)
                if s == STEP_CMP_SCORE + 1:
                    compressed_softmax_a()
                if s == STEP_CMP_SCORE + 3:
                    compressed_softmax_b()
                if 1 <= s <= NU:
                    invert(s - 1)
                if s >= LAG_TURN and s - LAG_TURN < NU and UNITS[s - LAG_TURN][1] == 0:
                    take_turned(s - LAG_TURN)
                if s == NU + 1:
                    lo(Q_OUT, 1)
                for h in HEAD_LAST:
                    if HEAD_LAST[h] == s - LAG_PV:
                        mix_lo(h)

            with dve.Fori(0, OUT_CHUNKS // 2) as i:
                for j, accs in enumerate((A, B)):
                    q = Q_OUT + 2 * i + j
                    lo(q, 2)
                    lo(q, 3)
                    lo(q + 1, 0)
                    add(accs, q + 1, 2 * i + j, 1.0, out_added)
                    lo(q + 1, 1)
                    stats(2 * i + j, out_added, 0)
            norm(1, 8)

            first_blocks(Q_UP2, KT)
            up(Q_UP2, UP_CHUNKS, 3)
            lo(Q_DOWN2, 1)
            for n in range(DOWN_CHUNKS):
                down_step(Q_DOWN2, n, (A, B)[n % 2], DOWN_CHUNKS, n == DOWN_CHUNKS - 1)
            norm(2, 12)
            dve.reciprocal(rstd[:, :], std[:, :]).then_inc(inv_ready, 1)
            dve.wait_ge(inv_ready, NU + 1)
            dve.scalar_tensor_tensor(out=nmr[:, :], in0=mv[:, :, 0], scalar=-1.0, in1=rstd[:, :],
                                     op0=ALU.mult, op1=ALU.mult).then_inc(rstd_ready, 1)
            dve.wait_ge(ln3_loaded, 32)
            for q in range(4):
                cols = slice(q * BN, (q + 1) * BN)
                piece = resid[:, 0, cols]
                dve.scalar_tensor_tensor(out=piece, in0=piece, scalar=mv[:, 0, 0:1], in1=ln3_g_bc[:, cols],
                                         op0=ALU.subtract, op1=ALU.mult).then_inc(final_step, 1)
                dve.wait_ge(z_ready, 8 + q + 1)
                dve.tensor_tensor(resid[:, 1, cols], resid[:, 1, cols], ln3_g_bc[:, cols], ALU.mult
                                  ).then_inc(final_g, 1)
                dve.wait_ge(final_step, q + 1)
                dve.scalar_tensor_tensor(out=piece, in0=piece, scalar=rstd[:, 0:1], in1=ln3_b_bc[:, cols],
                                         op0=ALU.mult, op1=ALU.add).then_inc(final_ready[0], 1)

        @block.gpsimd
        def _(pool):
            pool.memset(eps_t[:, :], EPS)
            pool.memset(ident[:, :], 0.0).then_inc(ident_ready, 1)
            pool.wait_ge(ident_ready, 1)
            pool.affine_select(out=ident[:, :], in_=ident[:, :], compare_op=ALU.not_equal, fill=1.0, base=0,
                               pattern=[[-1, P]], channel_multiplier=1).then_inc(ident_ready, 1)
            pool.wait_ge(in_turned, KT // 2)
            for t in range(NT):
                r = pool.tensor_scalar(resid[:, t, :], resid[:, t, :], ALPHA, None, ALU.mult)
            r.then_inc(resid_ready, 1)

            def scale_resid(g, b, bc, turned, n_before):
                pool.wait_ge(in_turned, turned)
                for q in range(DM // BC):
                    n = 3 * (n_before + q)
                    if q:
                        pool.wait_ge(resid_step, n)
                    cols = slice(q * BC, (q + 1) * BC)
                    for a, v in enumerate((g, b)):
                        pool.dma_start(bc[:, a, :], v[0:1, cols].broadcast_to([P, BC])).then_inc(bc_loaded, 16)
                    pool.wait_ge(bc_loaded, 32 * (n_before + q + 1))
                    pool.tensor_scalar(bc[:, :, :], bc[:, :, :], ALPHA, None, ALU.mult).then_inc(resid_step, 1)
                    for i, op in enumerate((ALU.mult, ALU.add)):
                        pool.wait_ge(resid_step, n + i + 1)
                        for t in range(NT):
                            r = pool.tensor_tensor(resid[:, t, cols], resid[:, t, cols], bc[:, i, :], op)
                        r.then_inc(resid_step, 1)
                pool.wait_ge(resid_step, 3 * (n_before + DM // BC))
                pool.sem_inc(resid_ready, 1)

            pool.wait_ge(block_used, 4 * Q_PROJ)
            pool.dma_start(wg[:, :, :], w_in[0][:, GATE_COL:IN_COLS].rearrange("(k p) n -> p k n", p=P)
                           ).then_inc(wg_loaded, 16)
            pool.wait_ge(in_ready, KT)
            pool.dma_start(dmask[:, :], dil_mask).then_inc(attn_loaded, 16)
            pool.dma_start(cmask[:, :], causal_mask).then_inc(attn_loaded, 16)
            pool.dma_start(cmpm[:, :, :, :], cmp_mask).then_inc(attn_loaded, 16)
            pool.dma_start(gate_bT[:, :], gate_b[0].rearrange("(n a) -> n a", a=1)).then_inc(attn_loaded, 16)
            pool.wait_ge(wg_loaded, 16)
            pool.tensor_copy(wg_hi[:, :, :], wg[:, :, :]).then_inc(wg_hi_ready, 1)
            pool.wait_ge(wg_hi_ready, 1)
            pool.tensor_tensor(wg_lo[:, :, :], wg[:, :, :], wg_hi[:, :, :], ALU.subtract).then_inc(wg_ready, 1)

            pool.wait_ge(wg_ready, 1)
            pool.wait_ge(tok_copied, 1)
            pool.wait_ge(vecs_ready, 1)
            for j in range(2):
                tok = tokT[:, 2 * j:2 * j + 2, :].rearrange("p g (n c) -> p c g n", c=CMP_STRIDE)
                for half in range(2):
                    pe_col = 4 * KT + j * CMP_BLOCK + half * CMP_STRIDE
                    for g in range(KV_GROUPS):
                        f = pool.tensor_tensor(
                            flat[:, half * CMP_STRIDE:(half + 1) * CMP_STRIDE, g * N_CMP:(g + 1) * N_CMP],
                            tok[:, :, g, half:half + N_CMP],
                            vecsT[:, pe_col:pe_col + CMP_STRIDE].unsqueeze(2).broadcast_to([P, CMP_STRIDE, N_CMP]),
                            ALU.add)
                f.then_inc(flat_step, 1)
                pool.wait_ge(flat_step, 2 * j + 1)
                part = slice(j * CMP_BLOCK, (j + 1) * CMP_BLOCK)
                pool.tensor_copy(flat_hi[:, part, :], flat[:, :, :]).then_inc(flat_step, 1)
                pool.wait_ge(flat_step, 2 * j + 2)
                pool.tensor_tensor(flat_lo[:, part, :], flat[:, :, :], flat_hi[:, part, :], ALU.subtract
                                   ).then_inc(flat_ready, 1)
                pool.wait_ge(flat_ready, j + 1)

            scale_resid(ln1_g, ln1_b, bc1, KT, 0)

            pool.wait_ge(trig_ready, 1)
            n = 0
            for p, col, heads in ROPE_RUNS:
                pool.wait_ge(proj_copied_a, p + 1)
                pool.wait_ge(proj_copied_v, p + 1)
                for t in range(NT):
                    cos = cos_t[:, t, :].unsqueeze(1).unsqueeze(1).broadcast_to([P, 2, 2, HD // 2])
                    sin = sin_t[:, t, :].unsqueeze(1).unsqueeze(1).broadcast_to([P, 2, 2, HD // 2])
                    for h in range(0, heads, 2):
                        v = proj[:, t, col + h * HD:col + (h + 2) * HD].rearrange("p (h x d) -> p h x d", h=2, x=2)
                        if n:
                            pool.wait_ge(rope_step, 2 * n)
                        pool.tensor_tensor(rt[:, 0], v, cos, ALU.mult)
                        pool.tensor_tensor(rt[:, 1], v, sin, ALU.mult).then_inc(rope_step, 1)
                        pool.wait_ge(rope_step, 2 * n + 1)
                        pool.tensor_tensor(v[:, :, 0, :], rt[:, 0, :, 0, :], rt[:, 1, :, 1, :], ALU.subtract)
                        pool.tensor_tensor(v[:, :, 1, :], rt[:, 0, :, 1, :], rt[:, 1, :, 0, :], ALU.add
                                           ).then_inc(rope_step, 1)
                        n += 1
                pool.wait_ge(rope_step, 2 * n)
                pool.sem_inc(roped, 1)

            pool.wait_ge(c_used, CMP_BLOCKS + 1)
            pool.dma_start(cw2[:, :, :], cmp_w2[0].rearrange("j (h p) d -> p (j h) d", p=P)).then_inc(cw2_loaded, 16)
            pool.dma_start(b2_bc[:, :, :], cmp_b2[0:1].broadcast_to([N_CMP, 2, HD])).then_inc(cw2_loaded, 16)

            pool.wait_ge(gates_ready, 1)
            for u, (h, t, br) in enumerate(UNITS):
                e = probs[:, u % E_RING, 0:(t + 1) * P]
                pool.wait_ge(inv_ready, u + 1)
                if br == "dil":
                    w = pool.tensor_scalar(e, e, rinv[:, u:u + 1], None, ALU.mult)
                else:
                    c = (h - N_DIL) * N_BRANCH + (1 if br == "slc" else 2)
                    w = pool.tensor_scalar(e, e, rinv[:, u:u + 1], gates[:, t, c:c + 1], ALU.mult, ALU.mult)
                w.then_inc(probs_ready, 1)

            scale_resid(ln2_g, ln2_b, bc2, 3 * KT // 2, DM // BC)
            pool.wait_ge(block_used, 4 * Q_DOWN2)
            pool.dma_start(ln3_g_bc[:, :], ln3_g[0:1, :].broadcast_to([P, DM])).then_inc(ln3_loaded, 16)
            pool.dma_start(ln3_b_bc[:, :], ln3_b[0:1, :].broadcast_to([P, DM])).then_inc(ln3_loaded, 16)
            pool.wait_ge(ln3_loaded, 32)
            for q in range(4):
                piece = resid[:, 1, q * BN:(q + 1) * BN]
                pool.wait_ge(final_g, q + 1)
                pool.tensor_tensor(piece, piece, ln3_b_bc[:, q * BN:(q + 1) * BN], ALU.add
                                   ).then_inc(final_ready[1], 1)


_INS = ["x", "positions", "ln1_g", "ln1_b", "ffn1_w1", "ffn1_w3", "ffn1_w2", "w_in", "gate_b", "cmp_pe", "cmp_w1",
        "cmp_b1", "cmp_w2", "cmp_b2", "w_out", "ln2_g", "ln2_b", "ffn2_w1", "ffn2_w3", "ffn2_w2", "ln3_g", "ln3_b"]


def _constants():
    import numpy as np

    f = np.float32
    inv_freq = (f(10000.0) ** (-np.arange(0, HD, 2, dtype=f) / f(HD))).astype(f)[None, :]
    d = (P + np.arange(P)[:, None]) - np.arange(SEQ)[None, :]
    causal = np.where(d >= 0, 0.0, -1e30).astype(f)
    count = (d <= 128) * 1 + (d % 4 == 0) * 1 + (d % 16 == 0) * 1
    dil = np.where((d >= 0) & (count > 0), np.log(np.maximum(count, 1)) / SCALE, -1e30).astype(f)
    token = np.arange(SEQ).reshape(NT, P).T[:, :, None]
    seen = np.arange(N_CMP) * CMP_STRIDE + CMP_BLOCK - 1 <= token
    cmp = np.stack([np.where(seen, 0.0, -1e30), seen * 1.0], axis=1).astype(f)
    return {"inv_freq": inv_freq, "dil_mask": dil, "causal_mask": causal, "cmp_mask": cmp}


def kernel(**inputs):
    import numpy as _np
    import concourse.bacc as _bacc
    from concourse import mybir as _mybir
    from concourse.bass_utils import run_bass_kernel_spmd as _run

    nc = _bacc.Bacc("TRN2", target_bir_lowering=False, num_devices=1)
    arrays, args = {}, []
    given = {name: _np.ascontiguousarray(inputs[name]) for name in _INS}
    for name, a in {**given, **_constants()}.items():
        arrays[f"in_{name}"] = a
        args.append(nc.dram_tensor(f"in_{name}", a.shape, _mybir.dt.from_np(a.dtype), kind="ExternalInput").ap())
    args.append(nc.dram_tensor("out_0", (1, SEQ, DM), F32, kind="ExternalOutput").ap())
    layer(nc, *args)
    r = _run(nc, [arrays], core_ids=[0])
    return r.results[0]["out_0"]
```

```python
from contextlib import ExitStack

import concourse.bass as bass
from concourse import mybir

F32 = mybir.dt.float32
F32R = mybir.dt.float32r
I32 = mybir.dt.int32
ALU = mybir.AluOpType
ACT = mybir.ActivationFunctionType
AX = mybir.AxisListType

P = 128
SEQ = 256
NT = SEQ // P
DM = 2048
KT = DM // P
DFF = 5632
FT = DFF // P
HD = 128
N_DIL = 6
N_NSA = 10
KV_GROUPS = 2
NSA_GROUP = N_NSA // KV_GROUPS
N_BRANCH = 3
N_GATE = N_NSA * N_BRANCH
CMP_BLOCK = 32
CMP_STRIDE = 16
CMP_HIDDEN = 256
N_CMP = (SEQ - CMP_BLOCK) // CMP_STRIDE + 1
ROWS_CMP = KV_GROUPS * N_CMP
IN_COLS = 5150
GATE_COL = IN_COLS - N_GATE
SCALE = float(HD) ** -0.5
ALPHA = 2.0 ** 0.25
EPS = 1e-5

BK = 4
BN = 512
STAGES = 4
SPLITS = 2
BC = 256
UP_COLS = BN // 2
UP_CHUNKS = DFF // UP_COLS
UP_F = UP_COLS // P
DOWN_CHUNKS = DM // BN
PROJ_CHUNKS = 10
OUT_CHUNKS = DM // BN
DOWN_K = [4] * 8 + [3] * 4
DOWN_BLOCKS = len(DOWN_K)
assert sum(DOWN_K) == FT and DOWN_BLOCKS % STAGES == 0 and KT // BK == STAGES

Q_UP1 = 0
Q_DOWN1 = Q_UP1 + UP_CHUNKS
Q_PROJ = Q_DOWN1 + DOWN_CHUNKS * DOWN_BLOCKS // STAGES
Q_OUT = Q_PROJ + PROJ_CHUNKS
Q_UP2 = Q_OUT + OUT_CHUNKS
Q_DOWN2 = Q_UP2 + UP_CHUNKS

PROJ_FROM = [3584, 4096, 4608, 2048, 2560, 3072, 0, 512, 1024, 1536]
COL_KC, COL_VC, COL_KS, COL_VS, COL_KW, COL_VW = range(0, 1536, 256)
COL_VA_TAIL, COL_QN, COL_QA, COL_KA, COL_VA = 1536, 1792, 3072, 3840, 4608
PROJ_COLS = PROJ_CHUNKS * BN
ROPE_RUNS = [(1, COL_KS, 2), (2, COL_KW, 2), (3, COL_QN, 2), (4, 2048, 4), (5, 2560, 4),
             (6, 3072, 4), (7, 3584, 4), (8, 4096, 4)]
_DIL = [(COL_QA + h * HD, COL_KA + h * HD) for h in range(N_DIL)]
_NSA_Q = [(COL_QN + h * HD, COL_QN + (h + 1) * HD) for h in range(0, N_NSA, 2)]
_NSA_K = [(COL_KS, COL_KS + HD), (COL_KW, COL_KW + HD)]
PAIRS = [_DIL[0], _DIL[1], _DIL[2], _NSA_Q[0], _DIL[3], _NSA_Q[1], _DIL[4], _NSA_Q[2], _DIL[5], _NSA_Q[3],
         _NSA_Q[4], _NSA_K[0], _NSA_K[1]]
PAIRS_FIRST = (0, 2)
PAIRS_AT = {0: (2, 4), 1: (4, 6), 2: (6, 8), 3: (8, 11), 4: (11, 13)}
T_OF = {col: i for i, col in enumerate(c for pair in PAIRS for c in pair)}
CMP_K = 8
CMP_BLOCKS = 2 * CMP_BLOCK // CMP_K

TWO_PI_1, TWO_PI_2 = 6.28125, 0.0019350051879882812
TWO_PI_3 = 6.283185307179586 - TWO_PI_1 - TWO_PI_2
PI = 3.1415925
MAGIC = 12582912.0

UNITS = [(h, "dil") for h in range(N_DIL)]
UNITS += [(N_DIL + h, b) for h in range(N_NSA) for b in ("win", "slc")]
NU = len(UNITS)
HEAD_LAST = {h: max(u for u in range(NU) if UNITS[u][0] == h) for h in range(N_DIL + N_NSA)}
TRI = 3 * P
LAG_TURN, LAG_PV, LAG_MIX = 2, 3, 4
E_RING = 4
EARLY = 8
STEP_CMP_OUT, STEP_CMP_TURN, STEP_CMP_SCORE = 1, 3, (4, 5)


def layer(nc, x, positions, ln1_g, ln1_b, ffn1_w1, ffn1_w3, ffn1_w2, w_in, gate_b, cmp_pe, cmp_w1,
          cmp_b1, cmp_w2, cmp_b2, w_out, ln2_g, ln2_b, ffn2_w1, ffn2_w3, ffn2_w2, ln3_g, ln3_b,
          inv_freq, dil_mask, causal_mask, cmp_mask, out):
    base = (nc.sbuf_base + 63) // 64 * 64

    def at(name, shape, dt, offset):
        return nc.alloc_sbuf_tensor_at(name, shape, dt, offset=base + offset)

    o = 0
    resid = at("resid", [P, NT, DM], F32, o)
    o += NT * DM * 4
    xT_hi = at("xT_hi", [P, KT, SEQ], F32R, o)
    xT_lo = at("xT_lo", [P, KT, SEQ], F32R, o + KT * SEQ * 4)
    ln3_g_bc = at("ln3_g_bc", [P, DM], F32, o)
    ln3_b_bc = at("ln3_b_bc", [P, DM], F32, o + DM * 4)
    o += 2 * KT * SEQ * 4
    HT = o
    hT_hi = at("hT_hi", [P, FT, SEQ], F32R, HT)
    hT_lo = at("hT_lo", [P, FT, SEQ], F32R, HT + FT * SEQ * 4)
    o += 2 * FT * SEQ * 4
    BC2 = o - 2 * BC * 4
    stage = at("stage", [P, STAGES, BK, BN], F32, o)
    o += STAGES * BK * BN * 4
    w_hi = at("w_hi", [P, SPLITS, BK, BN], F32R, o)
    o += SPLITS * BK * BN * 4
    w_lo = at("w_lo", [P, SPLITS, BK, BN], F32R, o)
    o += SPLITS * BK * BN * 4
    silu = at("silu", [P, NT, UP_COLS], F32, o)
    gated = at("gated", [P, NT, UP_COLS], F32, o + 2048)
    turned_f32 = at("turned_f32", [P, 2, BN], F32, o)
    dmask = at("dmask", [P, SEQ], F32, o)
    cmask = at("cmask", [P, SEQ], F32, o + 1024)
    cmpm = at("cmpm", [P, 2, NT, N_CMP], F32, o + 2048)
    gates = at("gates", [P, NT, N_GATE], F32, o + 2304)
    negmax = at("negmax", [P, NU, NT], F32, o + 2912)
    rowsum = at("rowsum", [P, NU, NT], F32, o + 3136)
    rinv = at("rinv", [P, NU, NT], F32, o + 3360)
    gate_bT = at("gate_bT", [N_GATE, 1], F32, o + 3584)
    o += 4096
    ident = at("ident", [P, P], F32, o)
    o += 512
    vecs = at("vecs", [P, P], F32, o)
    vecsT = at("vecsT", [P, P], F32, o + 512)
    o += 1024
    cos_t = at("cos_t", [P, NT, HD // 2], F32, o)
    sin_t = at("sin_t", [P, NT, HD // 2], F32, o + 512)
    o += 1024
    cos_c = at("cos_c", [P, 2, HD // 2], F32, o)
    o += 512
    bn = at("bn", [P, NT, DM // BN, 6], F32, o)
    o += 192
    mv = at("mv", [P, NT, 2], F32, o)
    std = at("std", [P, NT], F32, o + 32)
    rstd = at("rstd", [P, NT], F32, o + 64)
    nmr = at("nmr", [P, NT], F32, o + 96)
    eps_t = at("eps_t", [P, 1], F32, o + 128)
    b1T = at("b1T", [P, 4], F32, o + 160)
    warm = at("warm", [P, 4], F32, o + 192)
    o += 224
    assert base + o <= nc.sbuf_usable_end

    o = HT
    proj = at("proj", [P, NT, PROJ_COLS], F32, o)
    o += NT * PROJ_COLS * 4
    FREE = o
    cstage = at("cstage", [P, CMP_K, CMP_HIDDEN], F32, o)
    c_hi = at("c_hi", [P, CMP_K, CMP_HIDDEN], F32R, o + 8192)
    c_lo = at("c_lo", [P, CMP_K, CMP_HIDDEN], F32R, o + 16384)
    wg = at("wg", [P, KT, N_GATE], F32, o)
    wg_hi = at("wg_hi", [P, KT, N_GATE], F32R, o + 8192)
    wg_lo = at("wg_lo", [P, KT, N_GATE], F32R, o + 16384)
    o += 24576
    tokT = at("tokT", [P, 4, SEQ], F32, o)
    o += 4096
    flat_hi = at("flat_hi", [P, 2 * CMP_BLOCK, ROWS_CMP], F32R, o)
    flat_lo = at("flat_lo", [P, 2 * CMP_BLOCK, ROWS_CMP], F32R, o + 7680)
    o += 15360
    flat = at("flat", [P, CMP_BLOCK, ROWS_CMP], F32, FREE)
    bc1 = at("bc1", [P, 2, BC], F32, o)
    rt = at("rt", [P, 2, 2, 2, HD // 2], F32, o)
    hid_sum = at("hid_sum", [ROWS_CMP, 2, CMP_HIDDEN], F32, o + 2048)
    gatesT = at("gatesT", [N_GATE, SEQ], F32, o + 4096)
    flat_now_hi = at("flat_now_hi", [P, CMP_K, ROWS_CMP], F32R, FREE + 24576)
    flat_now_lo = at("flat_now_lo", [P, CMP_K, ROWS_CMP], F32R, FREE + 24576 + 1024)
    o += 5120
    assert o <= HT + 2 * FT * SEQ * 4
    o = FREE
    qkT = at("qkT", [P, len(T_OF), SEQ], F32, o)
    o += len(T_OF) * SEQ * 4
    probs = at("probs", [P, E_RING, TRI], F32, o)
    o += E_RING * TRI * 4
    probsT = at("probsT", [P, 2, TRI], F32, o)
    o += 2 * TRI * 4
    csc = at("csc", [P, NT, N_NSA, N_CMP], F32, o)
    cex = at("cex", [P, NT, N_NSA, N_CMP], F32, o + 1216)
    crt = at("crt", [N_CMP, 2, KV_GROUPS, 2, HD // 2], F32, o)
    cpr = at("cpr", [P, NT, N_NSA, N_CMP], F32, o + 2432)
    cst = at("cst", [P, 4, NT, N_NSA], F32, o + 3648)
    o += 3968
    hidT = at("hidT", [P, 2, 2, ROWS_CMP], F32, o)
    o += 512
    kcT = at("kcT", [P, KV_GROUPS, N_CMP], F32, o)
    o += 128
    cw2 = at("cw2", [P, 4, HD], F32, o)
    o += 2048
    cprT = at("cprT", [N_CMP, 2, SEQ], F32, o)
    o += 2048
    kvc = at("kvc", [N_CMP, 4, HD], F32, o)
    b2_bc = at("b2_bc", [N_CMP, 2, HD], F32, FREE + 48128)
    assert o + 2048 <= FREE + 48128
    bc2 = at("bc2", [P, 2, BC], F32, BC2)
    pos_i = at("pos_i", [P, NT + 2], I32, HT)
    pos_f = at("pos_f", [P, NT + 2], F32, HT + 32)
    invf_bc = at("invf_bc", [P, HD // 2], F32, HT + 64)
    ang = at("ang", [P, 3, HD // 2], F32, HT + 1024)
    turns = at("turns", [P, 3, HD // 2], F32, HT + 2048)
    red = at("red", [P, 2, 3, HD // 2], F32, HT + 3072)
    b1rows = at("b1rows", [4, P], F32, HT + 5120)

    with ExitStack() as ctx:
        bank = [ctx.enter_context(nc.psum_tensor(f"bank{i}", [P, 512], F32)) for i in range(8)]

        def sem(name):
            return ctx.enter_context(nc.semaphore(name))

        stage_full = [sem(f"stage_full{s}") for s in range(STAGES)]
        hi_ready, lo_ready, block_used = sem("hi_ready"), sem("lo_ready"), sem("block_used")
        x_loaded = [sem(f"x_loaded{q}") for q in range(4)]
        vecs_loaded, pos_loaded = sem("vecs_loaded"), sem("pos_loaded")
        attn_loaded, wg_loaded, bc_loaded = sem("attn_loaded"), sem("wg_loaded"), sem("bc_loaded")
        cstage_full, cw2_loaded, ln3_loaded = sem("cstage_full"), sem("cw2_loaded"), sem("ln3_loaded")
        out_stored = sem("out_stored")
        ident_ready, vecs_turned, vecs_ready = sem("ident_ready"), sem("vecs_turned"), sem("vecs_ready")
        pos_step, red_ready, trig_ready = sem("pos_step"), sem("red_ready"), sem("trig_ready")
        in_turned, in_full, in_hi, in_ready = sem("in_turned"), sem("in_full"), sem("in_hi"), sem("in_ready")
        stat_step, aggr_ready, std_ready, rstd_ready, z_ready = (
            sem("stat_step"), sem("aggr_ready"), sem("std_ready"), sem("rstd_ready"), sem("z_ready"))
        resid_step, resid_ready = sem("resid_step"), sem("resid_ready")
        silu_ready, gated_ready, hid_turned, hT_hi_ready, hT_ready = (
            sem("silu_ready"), sem("gated_ready"), sem("hid_turned"), sem("hT_hi_ready"), sem("hT_ready"))
        down_added, out_added = sem("down_added"), sem("out_added")
        proj_copied_a, proj_copied_v, wg_hi_ready, wg_ready = (
            sem("proj_copied_a"), sem("proj_copied_v"), sem("wg_hi_ready"), sem("wg_ready"))
        gate_summed, gatesT_ready, gates_turned, gates_ready = (
            sem("gate_summed"), sem("gatesT_ready"), sem("gates_turned"), sem("gates_ready"))
        tok_turned, tok_copied, flat_step, flat_ready = (
            sem("tok_turned"), sem("tok_copied"), sem("flat_step"), sem("flat_ready"))
        c_hi_ready, c_lo_ready, c_used, hid_added = (
            sem("c_hi_ready"), sem("c_lo_ready"), sem("c_used"), sem("hid_added"))
        rope_step, roped = sem("rope_step"), sem("roped")
        qk_turned, qk_even, qk_odd = sem("qk_turned"), sem("qk_even"), sem("qk_odd")
        sums_turned, hidT_ready, kvc_summed, kvc_step, kvc_ready = (
            sem("sums_turned"), sem("hidT_ready"), sem("kvc_summed"), sem("kvc_step"), sem("kvc_ready"))
        kc_turned, kcT_ready, cmp_scored, cmp_step, cmp_shifted, cmp_exp, cmp_ready = (
            sem("kc_turned"), sem("kcT_ready"), sem("cmp_scored"), sem("cmp_step"), sem("cmp_shifted"),
            sem("cmp_exp"), sem("cmp_ready"))
        scored, masked_ready, exp_ready, inv_ready, probs_ready = (
            sem("scored"), sem("masked_ready"), sem("exp_ready"), sem("inv_ready"),
            sem("probs_ready"))
        probs_turned, probsT_even, probsT_odd, valued = (
            sem("probs_turned"), sem("probsT_even"), sem("probsT_odd"), sem("valued"))
        mix_hi_ready, mix_ready = sem("mix_hi_ready"), sem("mix_ready")
        final_step, final_g = sem("final_step"), sem("final_g")
        final_ready = [sem("final_ready0"), sem("final_ready1")]

        def flat_rows(i, j):
            return bass.ds(CMP_K * i + j * CMP_BLOCK, CMP_K)

        def taken(u):
            return (probsT_odd if u % 2 else probsT_even), u // 2 + 1

        def pair_copied(n):
            return (qk_odd if n % 2 else qk_even), n // 2 + 1

        block = ctx.enter_context(nc.Block())

        def rows(w, kt, n):
            return w[kt * P:(kt + n) * P, :].rearrange("(k p) n -> p k n", p=P)

        @block.sync
        def _(sp):
            def slot_free(q, s):
                if not (isinstance(q, int) and q == 0):
                    sp.wait_ge(lo_ready, 4 * q + s - 3)

            def load_up_block(w1, w3, q, c, s):
                slot_free(q, s)
                for half, w in enumerate((w1, w3)):
                    sp.dma_start(stage[:, s, :, half * UP_COLS:(half + 1) * UP_COLS],
                                 rows(w, s * BK, BK)[:, :, bass.ds(c * UP_COLS, UP_COLS)]
                                 ).then_inc(stage_full[s], 16)

            def load_up(w1, w3, q, c):
                for s in range(STAGES):
                    load_up_block(w1, w3, q, c, s)

            def load_block(w, q, s, kt, n, col):
                slot_free(q, s)
                for a, b in ((0, 2), (2, n)):
                    sp.dma_start(stage[:, s, a:b, :], rows(w, kt + a, b - a)[:, :, bass.ds(col, BN)]
                                 ).then_inc(stage_full[s], 16)

            def load_down(w2, q0):
                with sp.Fori(0, DOWN_CHUNKS) as n:
                    for b, k in enumerate(DOWN_K):
                        load_block(w2, q0 + n * (DOWN_BLOCKS // STAGES) + b // STAGES, b % STAGES,
                                   sum(DOWN_K[:b]), k, n * BN)

            def load_x(q):
                sp.dma_start(resid[:, :, q * BN:(q + 1) * BN],
                             x[0].rearrange("(t p) n -> p t n", p=P)[:, :, q * BN:(q + 1) * BN]
                             ).then_inc(x_loaded[q], 16)

            load_x(0)
            for s in range(STAGES):
                if s:
                    load_x(s)
                load_up_block(ffn1_w1[0], ffn1_w3[0], 0, 0, s)
            with sp.Fori(1, UP_CHUNKS) as c:
                load_up(ffn1_w1[0], ffn1_w3[0], Q_UP1 + c, c)
            load_down(ffn1_w2[0], Q_DOWN1)
            for p in range(PROJ_CHUNKS):
                for s in range(STAGES):
                    load_block(w_in[0], Q_PROJ + p, s, s * BK, BK, PROJ_FROM[p])
            with sp.Fori(0, OUT_CHUNKS) as n:
                for s in range(STAGES):
                    load_block(w_out[0], Q_OUT + n, s, s * BK, BK, n * BN)
            with sp.Fori(0, UP_CHUNKS) as c:
                load_up(ffn2_w1[0], ffn2_w3[0], Q_UP2 + c, c)
            load_down(ffn2_w2[0], Q_DOWN2)
            for q in range(4):
                for t in range(NT):
                    sp.wait_ge(final_ready[t], q + 1)
                    sp.dma_start(out[0, t * P:(t + 1) * P, q * BN:(q + 1) * BN],
                                 resid[:, t, q * BN:(q + 1) * BN]).then_inc(out_stored, 16)
            sp.wait_ge(out_stored, 16 * 4 * NT)

        @block.tensor
        def _(pe):
            def product(acc, a, b, start, stop):
                pe.matmul(acc, a[0], b[0], start=start, stop=False)
                pe.matmul(acc, a[0], b[1], start=False, stop=False)
                return pe.matmul(acc, a[1], b[0], start=False, stop=stop)

            def split_block(accs, src, q, s, kt, n, first, last):
                pe.wait_ge(lo_ready, 4 * q + s + 1)
                for k in range(n):
                    for t in range(NT):
                        col = slice(t * P, (t + 1) * P)
                        mm = product(accs[t][:, :], (src[0][:, kt + k, col], src[1][:, kt + k, col]),
                                     (w_hi[:, s % 2, k, :], w_lo[:, s % 2, k, :]),
                                     first and k == 0, last and k == n - 1)
                mm.then_inc(block_used, 1)

            xT, hT = (xT_hi, xT_lo), (hT_hi, hT_lo)
            A, B = bank[0:2], bank[2:4]
            T = bank[4]

            def turn_quarter(n0, q, src_ready):
                src_ready(q)
                for j in (2 * q, 2 * q + 1):
                    n = n0 + j
                    if n >= 2:
                        pe.wait_ge(in_full, n - 1)
                    for k in range(2):
                        for t in range(NT):
                            mm = pe.transpose(bank[5 + n % 2][:, k * SEQ + t * P:k * SEQ + (t + 1) * P],
                                              resid[:, t, (2 * j + k) * P:(2 * j + k + 1) * P], ident[:, :])
                    mm.then_inc(in_turned, 1)

            def turn_hidden(m):
                pe.wait_ge(gated_ready, m + 1)
                pe.wait_ge(hT_ready, m + 1)
                for f in range(UP_F):
                    for t in range(NT):
                        mm = pe.transpose(T[:, f * SEQ + t * P:f * SEQ + (t + 1) * P],
                                          gated[:, t, f * P:(f + 1) * P], ident[:, :])
                mm.then_inc(hid_turned, 1)

            def up_chunk(q, accs, m):
                for s in range(STAGES):
                    split_block(accs, xT, q, s, s * BK, BK, s == 0, s == STAGES - 1)
                    if s == 0:
                        turn_hidden(m - 1)

            def first_chunk(q, n0, src_ready):
                turn_quarter(n0, 0, src_ready)
                for s in range(STAGES):
                    if s + 1 < STAGES:
                        turn_quarter(n0, s + 1, src_ready)
                    pe.wait_ge(in_ready, n0 + 2 * (s + 1))
                    split_block(A, xT, q, s, s * BK, BK, s == 0, s == STAGES - 1)

            def up(q0, m0):
                with pe.Fori(0, (UP_CHUNKS - 2) // 2) as i:
                    up_chunk(q0 + 1 + 2 * i, B, m0 + 1 + 2 * i)
                    up_chunk(q0 + 2 + 2 * i, A, m0 + 2 + 2 * i)
                up_chunk(q0 + UP_CHUNKS - 1, B, m0 + UP_CHUNKS - 1)
                turn_hidden(m0 + UP_CHUNKS - 1)

            def down(q0, m0, d0):
                with pe.Fori(0, DOWN_CHUNKS // 2) as i:
                    for j, accs in enumerate((A, B)):
                        if j == 1:
                            pe.wait_ge(down_added, d0 + 2 * i + 1)
                        for b, k in enumerate(DOWN_K):
                            if j == 0 and b == DOWN_BLOCKS - 1:
                                pe.wait_ge(hT_ready, m0 + UP_CHUNKS + 1)
                            split_block(accs, hT, q0 + (2 * i + j) * (DOWN_BLOCKS // STAGES) + b // STAGES,
                                        b % STAGES, sum(DOWN_K[:b]), k, b == 0, b == DOWN_BLOCKS - 1)
                    pe.wait_ge(down_added, d0 + 2 * i + 2)

            pe.sem_inc(c_used, 1)
            pe.wait_ge(ident_ready, 2)
            first_chunk(Q_UP1, 0, lambda q: pe.wait_ge(x_loaded[q], 16))
            pe.wait_ge(vecs_loaded, 16 * 6)
            pe.transpose(bank[7][:, 0:P], vecs[:, :], ident[:, :])
            pe.transpose(bank[7][:, P:P + 4], b1rows[:, :], ident[0:4, 0:4]).then_inc(vecs_turned, 1)
            up(Q_UP1, 0)
            down(Q_DOWN1, 0, 0)

            def proj_chunk(p, accs):
                for s in range(STAGES):
                    split_block(accs, xT, Q_PROJ + p, s, s * BK, BK, s == 0, s == STAGES - 1)

            def compress(cb):
                pe.wait_ge(c_lo_ready, cb + 1)
                pe.wait_ge(hid_added, cb + 1)
                for k in range(CMP_K):
                    mm = product(bank[7][0:ROWS_CMP, 0:CMP_HIDDEN], (flat_now_hi[:, k, :], flat_now_lo[:, k, :]),
                                 (c_hi[:, k, :], c_lo[:, k, :]), k == 0, k == CMP_K - 1)
                mm.then_inc(c_used, 1)

            first_chunk(Q_PROJ, KT // 2, lambda q: pe.wait_ge(z_ready, q + 1))
            split_block(B, xT, Q_PROJ + 1, 0, 0, BK, True, False)
            pe.wait_ge(proj_copied_a, 1)
            pe.wait_ge(proj_copied_v, 1)
            for a in range(4):
                for t in range(NT):
                    mm = pe.transpose(bank[5 + a // 2][:, (a % 2) * SEQ + t * P:(a % 2) * SEQ + (t + 1) * P],
                                      proj[:, t, a * HD:(a + 1) * HD], ident[:, :])
            mm.then_inc(tok_turned, 1)
            split_block(B, xT, Q_PROJ + 1, 1, BK, BK, False, False)
            pe.wait_ge(wg_ready, 1)
            for k in range(KT):
                mm = product(T[0:N_GATE, 0:SEQ], (wg_hi[:, k, :], wg_lo[:, k, :]),
                             (xT_hi[:, k, :], xT_lo[:, k, :]), k == 0, k == KT - 1)
            mm.then_inc(gate_summed, 1)
            split_block(B, xT, Q_PROJ + 1, 2, 2 * BK, BK, False, False)
            split_block(B, xT, Q_PROJ + 1, 3, 3 * BK, BK, False, True)
            pe.wait_ge(gatesT_ready, 1)
            for t in range(NT):
                mm = pe.transpose(T[:, SEQ + t * 32:SEQ + t * 32 + N_GATE], gatesT[:, t * P:(t + 1) * P],
                                  ident[0:N_GATE, 0:N_GATE])
            mm.then_inc(gates_turned, 1)
            with pe.Fori(0, (PROJ_CHUNKS - 2) // 2) as i:
                for j, accs in enumerate((A, B)):
                    pe.wait_ge(proj_copied_a, 2 * i + j + 1)
                    pe.wait_ge(proj_copied_v, 2 * i + j + 1)
                    proj_chunk(2 * i + j + 2, accs)
                    compress(2 * i + j)

            pe.wait_ge(roped, len(ROPE_RUNS))
            pe.wait_ge(hid_added, CMP_BLOCKS + 1)
            for a in range(4):
                mm = pe.transpose(bank[5][:, a * 32:a * 32 + ROWS_CMP],
                                  hid_sum[:, a // 2, (a % 2) * P:(a % 2 + 1) * P],
                                  ident[0:ROWS_CMP, 0:ROWS_CMP])
            mm.then_inc(sums_turned, 1)

            def turn_pairs(first, end):
                for n in range(first, end):
                    if n >= 2:
                        pe.wait_ge(*pair_copied(n - 2))
                    for a in range(2):
                        for t in range(NT):
                            col = PAIRS[n][a]
                            mm = pe.transpose(bank[6 + n % 2][:, a * SEQ + t * P:a * SEQ + (t + 1) * P],
                                              proj[:, t, col:col + HD], ident[:, :])
                    mm.then_inc(qk_turned, 1)

            turn_pairs(*PAIRS_FIRST)
            pe.wait_ge(gates_ready, 1)
            pe.wait_ge(proj_copied_a, PROJ_CHUNKS)
            pe.wait_ge(proj_copied_v, PROJ_CHUNKS)

            def scores(u):
                h, br = UNITS[u]
                g = (h - N_DIL) // NSA_GROUP
                q = T_OF[COL_QA + h * HD if br == "dil" else COL_QN + (h - N_DIL) * HD]
                k = T_OF[{"dil": COL_KA + h * HD, "slc": COL_KS + g * HD, "win": COL_KW + g * HD}[br]]
                pe.wait_ge(*pair_copied(q // 2))
                pe.wait_ge(*pair_copied(k // 2))
                if u >= 2:
                    pe.wait_ge(masked_ready, NT * (u - 1))
                for t in range(NT):
                    mm = pe.matmul(bank[u % 2][:, t * P:(2 * t + 1) * P], qkT[:, q, t * P:(t + 1) * P],
                                   qkT[:, k, 0:(t + 1) * P], start=True, stop=True)
                mm.then_inc(scored, 1)

            def turn_probs(u):
                h, br = UNITS[u]
                pe.wait_ge(probs_ready, u + 1)
                if u >= 2:
                    pe.wait_ge(*taken(u - 2))
                if br == "slc":
                    if h == N_DIL:
                        pe.wait_ge(cmp_ready, 1)
                        pe.wait_ge(*pair_copied(len(PAIRS) - 1))
                        pe.wait_ge(*pair_copied(len(PAIRS) - 2))
                    if h >= N_DIL + 2:
                        pe.wait_ge(*taken(u - 4))
                    for t in range(NT):
                        pe.transpose(bank[6 + h % 2][0:N_CMP, t * P:(t + 1) * P], cpr[:, t, h - N_DIL, :],
                                     ident[:, :])
                for a in range(3):
                    mm = pe.transpose(bank[2 + u % 2][:, a * P:(a + 1) * P],
                                      probs[:, u % E_RING, a * P:(a + 1) * P], ident[:, :])
                mm.then_inc(probs_turned, 1)

            def values(u):
                h, br = UNITS[u]
                if br != "slc" and h >= 2:
                    pe.wait_ge(mix_ready, h - 1)
                if br == "dil" and h == 1:
                    pe.wait_ge(kcT_ready, 1)
                pe.wait_ge(*taken(u))
                g = (h - N_DIL) // NSA_GROUP
                o = bank[4 + h % 2]
                col = {"dil": COL_VA + h * HD if h < 4 else COL_VA_TAIL + (h - 4) * HD,
                       "slc": COL_VS + g * HD, "win": COL_VW + g * HD}[br]
                if br == "slc":
                    pe.matmul(o[:, 0:SEQ], kvc[:, 2 + g, :], cprT[:, h % 2, :], start=False, stop=False)
                pe.matmul(o[:, 0:SEQ], proj[:, 0, col:col + HD], probsT[:, u % 2, 0:SEQ],
                          start=(br != "slc"), stop=False)
                pe.matmul(o[:, P:SEQ], proj[:, 1, col:col + HD], probsT[:, u % 2, SEQ:TRI],
                          start=False, stop=(br != "win")).then_inc(valued, 1)

            for step in range(NU + LAG_PV):
                if step < NU:
                    scores(step)
                if step == STEP_CMP_OUT:
                    pe.wait_ge(hidT_ready, 4)
                    pe.wait_ge(cw2_loaded, 32)
                    for a in range(4):
                        j, g = a // 2, a % 2
                        for half in range(2):
                            mm = pe.matmul(bank[5][0:N_CMP, a * HD:(a + 1) * HD],
                                           hidT[:, j, half, g * N_CMP:(g + 1) * N_CMP],
                                           cw2[:, 2 * j + half, :], start=(half == 0), stop=(half == 1))
                    mm.then_inc(kvc_summed, 1)
                if step == STEP_CMP_TURN:
                    pe.wait_ge(kvc_ready, 1)
                    for g in range(KV_GROUPS):
                        mm = pe.transpose(bank[5][:, g * N_CMP:(g + 1) * N_CMP], kvc[:, g, :],
                                          ident[0:N_CMP, 0:N_CMP])
                    mm.then_inc(kc_turned, 1)
                if step in PAIRS_AT:
                    turn_pairs(*PAIRS_AT[step])
                if step >= LAG_TURN and step - LAG_TURN < NU:
                    turn_probs(step - LAG_TURN)
                if step >= LAG_PV:
                    values(step - LAG_PV)
                if step in STEP_CMP_SCORE:
                    t = STEP_CMP_SCORE.index(step)
                    pe.wait_ge(kcT_ready, 1)
                    pe.wait_ge(*pair_copied(11))
                    pe.wait_ge(*pair_copied(10))
                    for h in range(N_NSA):
                        c = (t * N_NSA + h) * N_CMP
                        mm = pe.matmul(bank[7][:, c:c + N_CMP], qkT[:, T_OF[COL_QN + h * HD], t * P:(t + 1) * P],
                                       kcT[:, h // NSA_GROUP, :], start=True, stop=True)
                    mm.then_inc(cmp_scored, 1)

            with pe.Fori(0, OUT_CHUNKS // 2) as i:
                for j, accs in enumerate((A, B)):
                    if j == 1:
                        pe.wait_ge(out_added, 2 * i + 1)
                    for s in range(STAGES):
                        if j == 0:
                            pe.wait_ge(mix_ready, BK * (s + 1))
                        split_block(accs, xT, Q_OUT + 2 * i + j, s, s * BK, BK, s == 0, s == STAGES - 1)
                pe.wait_ge(out_added, 2 * i + 2)
            first_chunk(Q_UP2, KT, lambda q: pe.wait_ge(z_ready, 4 + q + 1))
            up(Q_UP2, UP_CHUNKS)
            down(Q_DOWN2, UP_CHUNKS, DOWN_CHUNKS)

        @block.scalar
        def _(act):
            def hi(q, s, n=BK):
                act.wait_ge(stage_full[s], 32 * q + 32)
                if not (isinstance(q, int) and 4 * q + s < SPLITS):
                    act.wait_ge(block_used, 4 * q + s + 1 - SPLITS)
                act.activation(w_hi[:, s % SPLITS, 0:n, :], stage[:, s, 0:n, :], ACT.Copy).then_inc(hi_ready, 1)

            def full_quarter(n0, q, vec):
                for j in (2 * q, 2 * q + 1):
                    n = n0 + j
                    act.wait_ge(in_turned, n + 1)
                    if n >= 2:
                        act.wait_ge(in_ready, n - 1)
                    if vec is None:
                        act.activation(turned_f32[:, n % 2, :], bank[5 + n % 2][:, :], ACT.Copy
                                       ).then_inc(in_full, 1)
                        continue
                    for k in range(2):
                        kt = 2 * j + k
                        a = act.activation(turned_f32[:, n % 2, k * SEQ:(k + 1) * SEQ],
                                           bank[5 + n % 2][:, k * SEQ:(k + 1) * SEQ], ACT.Identity,
                                           scale=vecsT[:, vec + kt:vec + kt + 1],
                                           bias=vecsT[:, vec + KT + kt:vec + KT + kt + 1])
                    a.then_inc(in_full, 1)

            def first_blocks(q, n0, vec):
                full_quarter(n0, 0, vec)
                if vec is None:
                    hi(q, 0)
                full_quarter(n0, 1, vec)
                hi(q, 1)
                full_quarter(n0, 2, vec)
                hi(q, 2)
                full_quarter(n0, 3, vec)
                hi(q, 3)
                hi(q + 1, 0)

            def up_step(q, accs, m, m0, turn):
                if turn:
                    hi(q, 1)
                    hi(q, 2)
                    act.wait_ge(hid_turned, m)
                    act.activation(hT_hi[:, bass.ds(UP_F * (m - 1 - m0), UP_F), :],
                                   bank[4][:, :].rearrange("p (f n) -> p f n", f=UP_F), ACT.Copy
                                   ).then_inc(hT_hi_ready, 1)
                    hi(q, 3)
                    hi(q + 1, 0)
                act.wait_ge(block_used, 4 * q + 4)
                for t in range(NT):
                    act.activation(silu[:, t, :], accs[t][:, 0:UP_COLS], ACT.Silu).then_inc(silu_ready, 1)

            A, B = bank[0:2], bank[2:4]

            def up(q0, m0):
                up_step(q0, A, m0, m0, False)
                with act.Fori(0, (UP_CHUNKS - 2) // 2) as i:
                    up_step(q0 + 1 + 2 * i, B, m0 + 1 + 2 * i, m0, True)
                    up_step(q0 + 2 + 2 * i, A, m0 + 2 + 2 * i, m0, True)
                m = m0 + UP_CHUNKS - 1
                up_step(q0 + UP_CHUNKS - 1, B, m, m0, True)
                act.wait_ge(hid_turned, m + 1)
                act.activation(hT_hi[:, FT - UP_F:FT, :], bank[4][:, :].rearrange("p (f n) -> p f n", f=UP_F),
                               ACT.Copy).then_inc(hT_hi_ready, 1)

            def down_step(q0, n, last=False):
                for b in range(1, DOWN_BLOCKS + (not last)):
                    hi(q0 + (DOWN_BLOCKS // STAGES) * n + b // STAGES, b % STAGES, DOWN_K[b % DOWN_BLOCKS])

            def std_of(l):
                act.activation(warm[:, l:l + 1], eps_t[:, :], ACT.Sqrt)
                act.wait_ge(aggr_ready, l + 1)
                act.activation(std[:, :], mv[:, :, 1], ACT.Sqrt, bias=eps_t[:, :]).then_inc(std_ready, 1)

            act.wait_ge(ident_ready, 1)
            act.activation(warm[:, 3:4], eps_t[:, :], ACT.Copy)
            first_blocks(Q_UP1, 0, None)
            act.wait_ge(red_ready, 1)
            act.activation(sin_t[:, :, :], red[:, 0, 0:NT, :], ACT.Sin)
            act.activation(cos_t[:, :, :], red[:, 1, 0:NT, :], ACT.Sin)
            act.activation(cos_c[:, 1, :], red[:, 0, NT, :], ACT.Sin)
            act.activation(cos_c[:, 0, :], red[:, 1, NT, :], ACT.Sin).then_inc(trig_ready, 1)
            up(Q_UP1, 0)
            with act.Fori(0, DOWN_CHUNKS) as n:
                down_step(Q_DOWN1, n)
            std_of(0)

            def compress_hi(i, j):
                cb = 2 * i + j
                act.wait_ge(cstage_full, 16 * cb + 16)
                act.wait_ge(c_used, cb + 1)
                act.activation(flat_now_hi[:, :, :], flat_hi[:, flat_rows(i, j), :], ACT.Copy)
                act.activation(c_hi[:, :, :], cstage[:, :, :], ACT.Copy).then_inc(c_hi_ready, 1)

            def load_compress(i, j):
                act.dma_start(cstage[:, :, :], cmp_w1[0][j].rearrange("(b k p) n -> p b k n", k=CMP_K, p=P)[
                    :, bass.ds(i, 1), :, :].rearrange("p a k n -> p (a k) n")).then_inc(cstage_full, 16)

            def proj_step(p, accs, cmp=None):
                if isinstance(p, int) and p == 0:
                    first_blocks(Q_PROJ, KT // 2, 0)
                else:
                    hi(Q_PROJ + p, 1)
                    hi(Q_PROJ + p, 2)
                    if cmp is not None:
                        compress_hi(*cmp)
                    hi(Q_PROJ + p, 3)
                    hi(Q_PROJ + p + 1, 0)
                if isinstance(p, int) and p == 1:
                    act.wait_ge(gate_summed, 1)
                    act.wait_ge(attn_loaded, 16 * 4)
                    act.activation(gatesT[:, :], bank[4][0:N_GATE, 0:SEQ], ACT.Sigmoid, bias=gate_bT[:, :]
                                   ).then_inc(gatesT_ready, 1)
                act.wait_ge(block_used, 4 * (Q_PROJ + p) + 4)
                act.activation(proj[:, 0, bass.ds(p * BN, BN)], accs[0][:, :], ACT.Copy
                               ).then_inc(proj_copied_a, 1)

            proj_step(0, A)
            proj_step(1, B)
            act.wait_ge(flat_ready, 2)
            load_compress(0, 0)
            with act.Fori(0, (PROJ_CHUNKS - 4) // 2) as i:
                proj_step(2 * i + 2, A, (i, 0))
                act.wait_ge(c_lo_ready, 2 * i + 1)
                load_compress(i, 1)
                proj_step(2 * i + 3, B, (i, 1))
                act.wait_ge(c_lo_ready, 2 * i + 2)
                load_compress(i + 1, 0)
            last = CMP_BLOCKS // 2 - 1
            proj_step(PROJ_CHUNKS - 2, A, (last, 0))
            act.wait_ge(c_lo_ready, CMP_BLOCKS - 1)
            load_compress(last, 1)
            proj_step(PROJ_CHUNKS - 1, B, (last, 1))

            act.wait_ge(sums_turned, 1)
            for j in range(2):
                for half in range(2):
                    a = 2 * j + half
                    act.activation(hidT[:, j, half, :], bank[5][:, a * 32:a * 32 + ROWS_CMP], ACT.Gelu_apprx_tanh,
                                   bias=b1T[:, 2 * j + half:2 * j + half + 1]).then_inc(hidT_ready, 1)

            def copy_pairs(first, end):
                for n in range(first, end):
                    if n % 2:
                        act.wait_ge(qk_turned, n + 1)
                        act.activation(qkT[:, 2 * n:2 * n + 2, :],
                                       bank[7][:, :].rearrange("p (a n) -> p a n", a=2), ACT.Copy
                                       ).then_inc(qk_odd, 1)

            def exps(u):
                for t in range(NT):
                    act.wait_ge(masked_ready, NT * u + t + 1)
                    e = probs[:, u % E_RING, t * P:(2 * t + 1) * P]
                    act.activation(e, e, ACT.Exp, bias=negmax[:, u, t:t + 1], scale=-1.0,
                                   accum_out=rowsum[:, u, t:t + 1]).then_inc(exp_ready, 1)

            def take_turned(u):
                h, br = UNITS[u]
                act.wait_ge(probs_turned, u + 1)
                if u >= 2:
                    act.wait_ge(valued, u - 1)
                if br == "slc":
                    act.activation(cprT[:, h % 2, :], bank[6 + h % 2][0:N_CMP, 0:SEQ], ACT.Copy)
                act.activation(probsT[:, u % 2, :], bank[2 + u % 2][:, 0:TRI], ACT.Copy
                               ).then_inc(probsT_odd, 1)

            def mix_hi(h):
                act.wait_ge(valued, HEAD_LAST[h] + 1)
                act.activation(xT_hi[:, h, :], bank[4 + h % 2][:, 0:SEQ], ACT.Copy).then_inc(mix_hi_ready, 1)

            copy_pairs(*PAIRS_FIRST)
            for step in range(NU + LAG_MIX):
                if step < NU:
                    exps(step)
                if step in PAIRS_AT:
                    copy_pairs(*PAIRS_AT[step])
                if step == STEP_CMP_SCORE[1] + 2:
                    act.wait_ge(cmp_shifted, 1)
                    act.activation(cex[:, :, :, :], csc[:, :, :, :], ACT.Exp, scale=SCALE).then_inc(cmp_exp, 1)
                if LAG_TURN <= step < NU + LAG_TURN and (step - LAG_TURN) % 2:
                    take_turned(step - LAG_TURN)
                for h in HEAD_LAST:
                    if HEAD_LAST[h] == step - LAG_MIX:
                        mix_hi(h)

            with act.Fori(0, OUT_CHUNKS) as n:
                for b in range(1, STAGES + 1):
                    hi(Q_OUT + n + b // STAGES, b % STAGES)
            std_of(1)

            first_blocks(Q_UP2, KT, 2 * KT)
            up(Q_UP2, UP_CHUNKS)
            with act.Fori(0, DOWN_CHUNKS - 1) as n:
                down_step(Q_DOWN2, n)
            down_step(Q_DOWN2, DOWN_CHUNKS - 1, last=True)
            std_of(2)
            act.wait_ge(rstd_ready, 3)
            for q in range(4):
                piece = resid[:, 1, q * BN:(q + 1) * BN]
                act.activation(piece, piece, ACT.Identity, scale=rstd[:, 1:2], bias=nmr[:, 1:2]
                               ).then_inc(z_ready, 1)

        @block.vector
        def _(dve):
            A, B = bank[0:2], bank[2:4]

            def lo(q, s, n=BK):
                dve.wait_ge(hi_ready, 4 * q + s + 1)
                dve.tensor_tensor(w_lo[:, s % SPLITS, 0:n, :], stage[:, s, 0:n, :], w_hi[:, s % SPLITS, 0:n, :],
                                  ALU.subtract).then_inc(lo_ready, 1)

            def split_quarter(n0, q):
                for j in (2 * q, 2 * q + 1):
                    n = n0 + j
                    src = turned_f32[:, n % 2, :].rearrange("p (k n) -> p k n", k=2)
                    dve.wait_ge(in_full, n + 1)
                    dve.tensor_copy(xT_hi[:, 2 * j:2 * j + 2, :], src).then_inc(in_hi, 1)
                    dve.wait_ge(in_hi, n + 1)
                    dve.tensor_tensor(xT_lo[:, 2 * j:2 * j + 2, :], src, xT_hi[:, 2 * j:2 * j + 2, :],
                                      ALU.subtract).then_inc(in_ready, 1)

            def hidden_lo(m, f):
                dve.wait_ge(hT_hi_ready, m + 1)
                part = (slice(None), bass.ds(f, UP_F), slice(None))
                dve.tensor_tensor(hT_lo[part], bank[4][:, :].rearrange("p (f n) -> p f n", f=UP_F),
                                  hT_hi[part], ALU.subtract).then_inc(hT_ready, 1)

            def first_blocks(q, n0, vec=0, between=()):
                split_quarter(n0, 0)
                if vec is None:
                    lo(q, 0)
                else:
                    normalise(2)
                    normalise(3)
                split_quarter(n0, 1)
                lo(q, 1)
                split_quarter(n0, 2)
                lo(q, 2)
                split_quarter(n0, 3)
                for work in between[:1]:
                    work()
                lo(q, 3)
                for work in between[1:]:
                    work()
                lo(q + 1, 0)

            def up_step(q, accs, m, m0, turn):
                if turn:
                    lo(q, 1)
                    lo(q, 2)
                    hidden_lo(m - 1, UP_F * (m - 1 - m0))
                    lo(q, 3)
                    lo(q + 1, 0)
                for t in range(NT):
                    dve.wait_ge(silu_ready, 2 * m + t + 1)
                    g = dve.tensor_tensor(gated[:, t, :], silu[:, t, :], accs[t][:, UP_COLS:BN], ALU.mult)
                g.then_inc(gated_ready, 1)

            def up(q0, m0, r):
                up_step(q0, A, m0, m0, False)
                with dve.Fori(0, (UP_CHUNKS - 2) // 2) as i:
                    up_step(q0 + 1 + 2 * i, B, m0 + 1 + 2 * i, m0, True)
                    up_step(q0 + 2 + 2 * i, A, m0 + 2 + 2 * i, m0, True)
                dve.wait_ge(resid_ready, r)
                m = m0 + UP_CHUNKS - 1
                up_step(q0 + UP_CHUNKS - 1, B, m, m0, True)
                hidden_lo(m, FT - UP_F)

            def add(accs, q_end, n, factor, added):
                dve.wait_ge(block_used, 4 * q_end)
                cols = bass.ds(n * BN, BN)
                for t in range(NT):
                    a = dve.scalar_tensor_tensor(out=resid[:, t, cols], in0=accs[t][:, :], scalar=factor,
                                                 in1=resid[:, t, cols], op0=ALU.mult, op1=ALU.add)
                a.then_inc(added, 1)

            def stats(n, added, a0):
                cols = bass.ds(n * BN, BN)
                dve.wait_ge(added, a0 + n + 2)
                for t in range(NT):
                    a = dve.bn_stats(bn[:, t, bass.ds(n, 1), :].rearrange("p a s -> p (a s)"), resid[:, t, cols])
                a.then_inc(stat_step, 1)

            def down_step(q0, n, accs, a0, last=False):
                per = DOWN_BLOCKS // STAGES
                for b in range(1, DOWN_BLOCKS + (not last)):
                    lo(q0 + per * n + b // STAGES, b % STAGES, DOWN_K[b % DOWN_BLOCKS])
                add(accs, q0 + per * (n + 1), n, 0.5, down_added)
                stats(n, down_added, a0)

            def normalise(q):
                for t in range(NT):
                    piece = resid[:, t, q * BN:(q + 1) * BN]
                    a = dve.tensor_scalar(piece, piece, mv[:, t, 0:1], rstd[:, t:t + 1], ALU.subtract, ALU.mult)
                a.then_inc(z_ready, 1)

            def norm(l, s_end):
                dve.wait_ge(stat_step, s_end)
                for t in range(NT):
                    a = dve.bn_aggr(mv[:, t, :], bn[:, t, :, :].rearrange("p c s -> p (c s)"))
                a.then_inc(aggr_ready, 1)
                dve.wait_ge(std_ready, l + 1)
                if l < 2:
                    dve.reciprocal(rstd[:, :], std[:, :]).then_inc(rstd_ready, 1)
                    dve.wait_ge(rstd_ready, l + 1)
                    normalise(0)
                    normalise(1)

            steps = [0]

            def step(ins):
                ins.then_inc(pos_step, 1)
                steps[0] += 1
                dve.wait_ge(pos_step, steps[0])

            for counter in (hT_ready, down_added, out_added):
                dve.sem_inc(counter, 1)

            def angles():
                dve.memset(ang[:, :, :], 0.0)
                dve.wait_ge(pos_loaded, 16 * 5)
                dve.tensor_copy(pos_f[:, 0:NT], pos_i[:, 0:NT])
                step(dve.tensor_tensor(pos_f[0:N_CMP, NT:NT + 1], pos_i[0:N_CMP, NT:NT + 1],
                                       pos_i[0:N_CMP, NT + 1:NT + 2], ALU.add))
                for t in range(NT):
                    dve.tensor_scalar(ang[:, t, :], invf_bc[:, :], pos_f[:, t:t + 1], None, ALU.mult)
                step(dve.tensor_scalar(ang[0:N_CMP, NT, :], invf_bc[0:N_CMP, :], pos_f[0:N_CMP, NT:NT + 1], 0.5,
                                       ALU.mult, ALU.mult))
                step(dve.tensor_scalar(turns[:, :, :], ang[:, :, :], 0.15915494309189535, MAGIC, ALU.mult, ALU.add))
                step(dve.tensor_scalar(turns[:, :, :], turns[:, :, :], MAGIC, None, ALU.subtract))

            def reduced_angles():
                for part in (TWO_PI_1, TWO_PI_2, TWO_PI_3):
                    step(dve.scalar_tensor_tensor(out=ang[:, :, :], in0=turns[:, :, :], scalar=-part, in1=ang[:, :, :],
                                                  op0=ALU.mult, op1=ALU.add))
                step(dve.tensor_scalar(red[:, 0], ang[:, :, :], PI, -PI, ALU.min, ALU.max))
                step(dve.tensor_scalar(ang[:, :, :], red[:, 0], PI / 2, None, ALU.add))
                step(dve.tensor_scalar(turns[:, :, :], ang[:, :, :], PI, -2 * 3.141592653589793, ALU.is_gt, ALU.mult))
                step(dve.tensor_tensor(ang[:, :, :], ang[:, :, :], turns[:, :, :], ALU.add))
                dve.tensor_scalar(red[:, 1], ang[:, :, :], PI, -PI, ALU.min, ALU.max).then_inc(red_ready, 1)

            first_blocks(Q_UP1, 0, None, (angles, reduced_angles))
            dve.wait_ge(vecs_turned, 1)
            dve.tensor_copy(vecsT[:, :], bank[7][:, 0:P])
            dve.tensor_copy(b1T[:, :], bank[7][:, P:P + 4]).then_inc(vecs_ready, 1)
            up(Q_UP1, 0, 1)
            with dve.Fori(0, DOWN_CHUNKS // 2) as i:
                for j, accs in enumerate((A, B)):
                    down_step(Q_DOWN1, 2 * i + j, accs, 0)
            norm(0, 4)

            def proj_step(p, accs, between=None, cmp=None):
                if isinstance(p, int) and p == 0:
                    first_blocks(Q_PROJ, KT // 2)
                else:
                    proj_blocks(p, between, cmp)
                dve.wait_ge(block_used, 4 * (Q_PROJ + p) + 4)
                dve.tensor_copy(proj[:, 1, bass.ds(p * BN, BN)], accs[1][:, :]).then_inc(proj_copied_v, 1)
                if cmp is not None:
                    i, j = cmp
                    dve.wait_ge(c_used, 2 * i + j + 2)
                    dve.wait_ge(hid_added, 2 * i + j + 1)
                    dve.tensor_tensor(hid_sum[:, j, :], bank[7][0:ROWS_CMP, 0:CMP_HIDDEN], hid_sum[:, j, :],
                                      ALU.add).then_inc(hid_added, 1)

            def proj_blocks(p, between, cmp):
                lo(Q_PROJ + p, 1)
                if between:
                    between()
                lo(Q_PROJ + p, 2)
                if cmp is not None:
                    i, j = cmp
                    dve.wait_ge(c_hi_ready, 2 * i + j + 1)
                    dve.tensor_copy(flat_now_lo[:, :, :], flat_lo[:, flat_rows(i, j), :])
                    dve.tensor_tensor(c_lo[:, :, :], cstage[:, :, :], c_hi[:, :, :], ALU.subtract
                                      ).then_inc(c_lo_ready, 1)
                lo(Q_PROJ + p, 3)
                lo(Q_PROJ + p + 1, 0)

            def take_tokens():
                dve.wait_ge(tok_turned, 1)
                for a in range(2):
                    c = dve.tensor_copy(tokT[:, 2 * a:2 * a + 2, :],
                                        bank[5 + a][:, :].rearrange("p (a n) -> p a n", a=2))
                c.then_inc(tok_copied, 1)

            proj_step(0, A)
            proj_step(1, B, take_tokens)
            dve.memset(hid_sum[:, :, :], 0.0).then_inc(hid_added, 1)
            dve.wait_ge(gates_turned, 1)
            dve.tensor_copy(gates[:, :, :], bank[4][:, SEQ:SEQ + 64].rearrange("p (t n) -> p t n", n=32)[
                :, :, 0:N_GATE]).then_inc(gates_ready, 1)
            with dve.Fori(0, (PROJ_CHUNKS - 2) // 2) as i:
                proj_step(2 * i + 2, A, None, (i, 0))
                proj_step(2 * i + 3, B, None, (i, 1))


            def copy_pairs(first, end):
                for n in range(first, end):
                    if n % 2 == 0:
                        dve.wait_ge(qk_turned, n + 1)
                        dve.tensor_copy(qkT[:, 2 * n:2 * n + 2, :],
                                        bank[6][:, :].rearrange("p (a n) -> p a n", a=2)).then_inc(qk_even, 1)

            def mask_scores(u):
                h, br = UNITS[u]
                m = dmask if br == "dil" else cmask
                if u >= E_RING:
                    dve.wait_ge(probs_turned, u - E_RING + 1)
                dve.wait_ge(scored, u + 1)
                for t in range(NT):
                    n = (t + 1) * P
                    dve.tensor_tensor_reduce(probs[:, u % E_RING, t * P:(2 * t + 1) * P],
                                             bank[u % 2][:, t * P:(2 * t + 1) * P], m[:, SEQ - n:SEQ],
                                             -SCALE, 3e38, ALU.add, ALU.min, negmax[:, u, t:t + 1]
                                             ).then_inc(masked_ready, 1)

            def invert(u):
                dve.wait_ge(exp_ready, NT * (u + 1))
                dve.reciprocal(rinv[:, u, :], rowsum[:, u, :]).then_inc(inv_ready, 1)

            def take_turned(u):
                dve.wait_ge(probs_turned, u + 1)
                if u >= 2:
                    dve.wait_ge(valued, u - 1)
                dve.tensor_copy(probsT[:, u % 2, :], bank[2 + u % 2][:, 0:TRI]).then_inc(probsT_even, 1)

            def mix_lo(h):
                dve.wait_ge(mix_hi_ready, h + 1)
                dve.tensor_tensor(xT_lo[:, h, :], bank[4 + h % 2][:, 0:SEQ], xT_hi[:, h, :], ALU.subtract
                                  ).then_inc(mix_ready, 1)

            def chain(sem_, count):
                def go(ins):
                    ins.then_inc(sem_, 1)
                    count[0] += 1
                    dve.wait_ge(sem_, count[0])
                return go

            def compressed_kv():
                go = chain(kvc_step, [0])
                dve.wait_ge(kvc_summed, 1)
                go(dve.tensor_tensor(kvc[:, :, :].rearrange("p (j g) d -> p j g d", j=2),
                                     bank[5][0:N_CMP, :].rearrange("p (j g d) -> p j g d", j=2, g=2),
                                     b2_bc[:, :, :].unsqueeze(2).broadcast_to([N_CMP, 2, KV_GROUPS, HD]), ALU.add))
                k = kvc[:, 0:KV_GROUPS, :].rearrange("p g (x d) -> p g x d", x=2)
                cos = cos_c[0:N_CMP, 0, :].unsqueeze(1).unsqueeze(1).broadcast_to([N_CMP, KV_GROUPS, 2, HD // 2])
                sin = cos_c[0:N_CMP, 1, :].unsqueeze(1).unsqueeze(1).broadcast_to([N_CMP, KV_GROUPS, 2, HD // 2])
                dve.tensor_tensor(crt[:, 0], k, cos, ALU.mult)
                go(dve.tensor_tensor(crt[:, 1], k, sin, ALU.mult))
                dve.tensor_tensor(k[:, :, 0, :], crt[:, 0, :, 0, :], crt[:, 1, :, 1, :], ALU.subtract)
                dve.tensor_tensor(k[:, :, 1, :], crt[:, 0, :, 1, :], crt[:, 1, :, 0, :], ALU.add
                                  ).then_inc(kvc_ready, 1)

            def compressed_softmax_a():
                go = chain(cmp_step, [0])
                dve.wait_ge(cmp_scored, NT)
                for t in range(NT):
                    a = dve.tensor_tensor(
                        csc[:, t], bank[7][:, t * N_NSA * N_CMP:(t + 1) * N_NSA * N_CMP].rearrange(
                            "p (h n) -> p h n", n=N_CMP),
                        cmpm[:, 0, t, :].unsqueeze(1).broadcast_to([P, N_NSA, N_CMP]), ALU.add)
                go(a)
                go(dve.tensor_reduce(cst[:, 0], csc[:, :, :, :], AX.X, ALU.max))
                dve.tensor_tensor(csc[:, :, :, :], csc[:, :, :, :],
                                  cst[:, 0].unsqueeze(3).broadcast_to([P, NT, N_NSA, N_CMP]), ALU.subtract
                                  ).then_inc(cmp_shifted, 1)

            def compressed_softmax_b():
                go = chain(cmp_step, [2])
                dve.wait_ge(cmp_exp, 1)
                for t in range(NT):
                    a = dve.tensor_tensor(cex[:, t], cex[:, t],
                                          cmpm[:, 1, t, :].unsqueeze(1).broadcast_to([P, N_NSA, N_CMP]), ALU.mult)
                go(a)
                go(dve.tensor_reduce(cst[:, 1], cex[:, :, :, :], AX.X, ALU.add))
                go(dve.tensor_scalar(cst[:, 2], cst[:, 1], 1e-30, None, ALU.max))
                go(dve.reciprocal(cst[:, 1], cst[:, 2]))
                go(dve.tensor_tensor(cst[:, 3], cst[:, 1],
                                     gates[:, :, :].rearrange("p t (h b) -> p t h b", b=N_BRANCH)[:, :, :, 0],
                                     ALU.mult))
                dve.tensor_tensor(cpr[:, :, :, :], cex[:, :, :, :],
                                  cst[:, 3].unsqueeze(3).broadcast_to([P, NT, N_NSA, N_CMP]), ALU.mult
                                  ).then_inc(cmp_ready, 1)

            dve.wait_ge(attn_loaded, 16 * 4)
            copy_pairs(*PAIRS_FIRST)
            for s in range(NU + LAG_MIX):
                if s < NU:
                    mask_scores(s)
                if s in PAIRS_AT:
                    copy_pairs(*PAIRS_AT[s])
                if s < EARLY:
                    invert(s)
                if s == STEP_CMP_OUT + 1:
                    compressed_kv()
                if s == STEP_CMP_TURN:
                    dve.wait_ge(kc_turned, 1)
                    dve.tensor_copy(kcT[:, :, :], bank[5][:, 0:ROWS_CMP].rearrange("p (g n) -> p g n", g=KV_GROUPS)
                                    ).then_inc(kcT_ready, 1)
                if s == STEP_CMP_SCORE[1] + 1:
                    compressed_softmax_a()
                if s > EARLY and s <= NU:
                    invert(s - 1)
                if s == STEP_CMP_SCORE[1] + 2:
                    compressed_softmax_b()
                if LAG_TURN <= s < NU + LAG_TURN and (s - LAG_TURN) % 2 == 0:
                    take_turned(s - LAG_TURN)
                for h in HEAD_LAST:
                    if HEAD_LAST[h] == s - LAG_MIX:
                        mix_lo(h)

            with dve.Fori(0, OUT_CHUNKS // 2) as i:
                for j, accs in enumerate((A, B)):
                    q = Q_OUT + 2 * i + j
                    for b in range(1, STAGES):
                        lo(q, b)
                    lo(q + 1, 0)
                    add(accs, q + 1, 2 * i + j, 1.0, out_added)
                    stats(2 * i + j, out_added, 0)
            norm(1, 8)

            first_blocks(Q_UP2, KT)
            up(Q_UP2, UP_CHUNKS, 3)
            for n in range(DOWN_CHUNKS):
                down_step(Q_DOWN2, n, (A, B)[n % 2], DOWN_CHUNKS, n == DOWN_CHUNKS - 1)
            norm(2, 12)
            dve.reciprocal(rstd[:, :], std[:, :]).then_inc(inv_ready, 1)
            dve.wait_ge(inv_ready, NU + 1)
            dve.scalar_tensor_tensor(out=nmr[:, :], in0=mv[:, :, 0], scalar=-1.0, in1=rstd[:, :],
                                     op0=ALU.mult, op1=ALU.mult).then_inc(rstd_ready, 1)
            dve.wait_ge(ln3_loaded, 32)
            for q in range(4):
                cols = slice(q * BN, (q + 1) * BN)
                piece = resid[:, 0, cols]
                dve.scalar_tensor_tensor(out=piece, in0=piece, scalar=mv[:, 0, 0:1], in1=ln3_g_bc[:, cols],
                                         op0=ALU.subtract, op1=ALU.mult).then_inc(final_step, 1)
                dve.wait_ge(z_ready, 8 + q + 1)
                dve.tensor_tensor(resid[:, 1, cols], resid[:, 1, cols], ln3_g_bc[:, cols], ALU.mult
                                  ).then_inc(final_g, 1)
                dve.wait_ge(final_step, q + 1)
                dve.scalar_tensor_tensor(out=piece, in0=piece, scalar=rstd[:, 0:1], in1=ln3_b_bc[:, cols],
                                         op0=ALU.mult, op1=ALU.add).then_inc(final_ready[0], 1)

        @block.gpsimd
        def _(pool):
            pool.memset(eps_t[:, :], EPS)
            pool.memset(ident[:, :], 0.0).then_inc(ident_ready, 1)
            pool.wait_ge(ident_ready, 1)
            pool.affine_select(out=ident[:, :], in_=ident[:, :], compare_op=ALU.not_equal, fill=1.0, base=0,
                               pattern=[[-1, P]], channel_multiplier=1).then_inc(ident_ready, 1)
            for t in range(NT):
                pool.dma_start(pos_i[:, t:t + 1], positions[0, t * P:(t + 1) * P].rearrange("(p a) -> p a", a=1)
                              ).then_inc(pos_loaded, 16)
            for a, start in enumerate((0, CMP_BLOCK - CMP_STRIDE)):
                tok = positions[0, start:start + N_CMP * CMP_STRIDE].rearrange("(n c) -> n c", c=CMP_STRIDE)
                col = (0, CMP_STRIDE - 1)[a]
                pool.dma_start(pos_i[0:N_CMP, NT + a:NT + a + 1], tok[:, col:col + 1],
                              allow_slow_non_contiguous=True).then_inc(pos_loaded, 16)
            pool.dma_start(invf_bc[:, :], inv_freq[0:1, :].broadcast_to([P, HD // 2])).then_inc(pos_loaded, 16)
            for r, v in enumerate((ln1_g, ln1_b, ln2_g, ln2_b)):
                pool.dma_start(vecs[r * KT:(r + 1) * KT, :], v[0].rearrange("(k p) -> k p", p=P)
                              ).then_inc(vecs_loaded, 16)
            pool.dma_start(vecs[4 * KT:P, :], cmp_pe[0].rearrange("j c d -> (j c) d")).then_inc(vecs_loaded, 16)
            pool.dma_start(b1rows[:, :], cmp_b1[0].rearrange("j (h p) -> (j h) p", p=P)).then_inc(vecs_loaded, 16)
            pool.wait_ge(in_turned, KT // 2)
            for t in range(NT):
                r = pool.tensor_scalar(resid[:, t, :], resid[:, t, :], ALPHA, None, ALU.mult)
            r.then_inc(resid_ready, 1)

            def scale_resid(g, b, bc, turned, n_before):
                pool.wait_ge(in_turned, turned)
                for q in range(DM // BC):
                    n = 3 * (n_before + q)
                    if q:
                        pool.wait_ge(resid_step, n)
                    cols = slice(q * BC, (q + 1) * BC)
                    for a, v in enumerate((g, b)):
                        pool.dma_start(bc[:, a, :], v[0:1, cols].broadcast_to([P, BC])).then_inc(bc_loaded, 16)
                    pool.wait_ge(bc_loaded, 32 * (n_before + q + 1))
                    pool.tensor_scalar(bc[:, :, :], bc[:, :, :], ALPHA, None, ALU.mult).then_inc(resid_step, 1)
                    for i, op in enumerate((ALU.mult, ALU.add)):
                        pool.wait_ge(resid_step, n + i + 1)
                        for t in range(NT):
                            r = pool.tensor_tensor(resid[:, t, cols], resid[:, t, cols], bc[:, i, :], op)
                        r.then_inc(resid_step, 1)
                pool.wait_ge(resid_step, 3 * (n_before + DM // BC))
                pool.sem_inc(resid_ready, 1)

            pool.wait_ge(block_used, 4 * Q_PROJ)
            pool.dma_start(wg[:, :, :], w_in[0][:, GATE_COL:IN_COLS].rearrange("(k p) n -> p k n", p=P)
                           ).then_inc(wg_loaded, 16)
            pool.wait_ge(in_ready, KT)
            pool.dma_start(dmask[:, :], dil_mask).then_inc(attn_loaded, 16)
            pool.dma_start(cmask[:, :], causal_mask).then_inc(attn_loaded, 16)
            pool.dma_start(cmpm[:, :, :, :], cmp_mask).then_inc(attn_loaded, 16)
            pool.dma_start(gate_bT[:, :], gate_b[0].rearrange("(n a) -> n a", a=1)).then_inc(attn_loaded, 16)
            pool.wait_ge(wg_loaded, 16)
            pool.tensor_copy(wg_hi[:, :, :], wg[:, :, :]).then_inc(wg_hi_ready, 1)
            pool.wait_ge(wg_hi_ready, 1)
            pool.tensor_tensor(wg_lo[:, :, :], wg[:, :, :], wg_hi[:, :, :], ALU.subtract).then_inc(wg_ready, 1)

            pool.wait_ge(wg_ready, 1)
            pool.wait_ge(tok_copied, 1)
            pool.wait_ge(vecs_ready, 1)
            for j in range(2):
                tok = tokT[:, 2 * j:2 * j + 2, :].rearrange("p g (n c) -> p c g n", c=CMP_STRIDE)
                for half in range(2):
                    pe_col = 4 * KT + j * CMP_BLOCK + half * CMP_STRIDE
                    for g in range(KV_GROUPS):
                        f = pool.tensor_tensor(
                            flat[:, half * CMP_STRIDE:(half + 1) * CMP_STRIDE, g * N_CMP:(g + 1) * N_CMP],
                            tok[:, :, g, half:half + N_CMP],
                            vecsT[:, pe_col:pe_col + CMP_STRIDE].unsqueeze(2).broadcast_to([P, CMP_STRIDE, N_CMP]),
                            ALU.add)
                f.then_inc(flat_step, 1)
                pool.wait_ge(flat_step, 2 * j + 1)
                part = slice(j * CMP_BLOCK, (j + 1) * CMP_BLOCK)
                pool.tensor_copy(flat_hi[:, part, :], flat[:, :, :]).then_inc(flat_step, 1)
                pool.wait_ge(flat_step, 2 * j + 2)
                pool.tensor_tensor(flat_lo[:, part, :], flat[:, :, :], flat_hi[:, part, :], ALU.subtract
                                   ).then_inc(flat_ready, 1)
                pool.wait_ge(flat_ready, j + 1)

            scale_resid(ln1_g, ln1_b, bc1, KT, 0)

            pool.wait_ge(trig_ready, 1)
            n = 0
            for p, col, heads in ROPE_RUNS:
                pool.wait_ge(proj_copied_a, p + 1)
                pool.wait_ge(proj_copied_v, p + 1)
                for t in range(NT):
                    cos = cos_t[:, t, :].unsqueeze(1).unsqueeze(1).broadcast_to([P, 2, 2, HD // 2])
                    sin = sin_t[:, t, :].unsqueeze(1).unsqueeze(1).broadcast_to([P, 2, 2, HD // 2])
                    for h in range(0, heads, 2):
                        v = proj[:, t, col + h * HD:col + (h + 2) * HD].rearrange("p (h x d) -> p h x d", h=2, x=2)
                        if n:
                            pool.wait_ge(rope_step, 2 * n)
                        pool.tensor_tensor(rt[:, 0], v, cos, ALU.mult)
                        pool.tensor_tensor(rt[:, 1], v, sin, ALU.mult).then_inc(rope_step, 1)
                        pool.wait_ge(rope_step, 2 * n + 1)
                        pool.tensor_tensor(v[:, :, 0, :], rt[:, 0, :, 0, :], rt[:, 1, :, 1, :], ALU.subtract)
                        pool.tensor_tensor(v[:, :, 1, :], rt[:, 0, :, 1, :], rt[:, 1, :, 0, :], ALU.add
                                           ).then_inc(rope_step, 1)
                        n += 1
                pool.wait_ge(rope_step, 2 * n)
                pool.sem_inc(roped, 1)

            pool.wait_ge(c_used, CMP_BLOCKS + 1)
            pool.dma_start(cw2[:, :, :], cmp_w2[0].rearrange("j (h p) d -> p (j h) d", p=P)).then_inc(cw2_loaded, 16)
            pool.dma_start(b2_bc[:, :, :], cmp_b2[0:1].broadcast_to([N_CMP, 2, HD])).then_inc(cw2_loaded, 16)

            pool.wait_ge(gates_ready, 1)
            for u, (h, br) in enumerate(UNITS):
                pool.wait_ge(inv_ready, u + 1)
                for t in range(NT):
                    e = probs[:, u % E_RING, t * P:(2 * t + 1) * P]
                    if br == "dil":
                        w = pool.tensor_scalar(e, e, rinv[:, u, t:t + 1], None, ALU.mult)
                    else:
                        c = (h - N_DIL) * N_BRANCH + (1 if br == "slc" else 2)
                        w = pool.tensor_scalar(e, e, rinv[:, u, t:t + 1], gates[:, t, c:c + 1], ALU.mult, ALU.mult)
                w.then_inc(probs_ready, 1)

            scale_resid(ln2_g, ln2_b, bc2, 3 * KT // 2, DM // BC)
            pool.wait_ge(block_used, 4 * Q_DOWN2)
            pool.dma_start(ln3_g_bc[:, :], ln3_g[0:1, :].broadcast_to([P, DM])).then_inc(ln3_loaded, 16)
            pool.dma_start(ln3_b_bc[:, :], ln3_b[0:1, :].broadcast_to([P, DM])).then_inc(ln3_loaded, 16)
            pool.wait_ge(ln3_loaded, 32)
            for q in range(4):
                piece = resid[:, 1, q * BN:(q + 1) * BN]
                pool.wait_ge(final_g, q + 1)
                pool.tensor_tensor(piece, piece, ln3_b_bc[:, q * BN:(q + 1) * BN], ALU.add
                                   ).then_inc(final_ready[1], 1)


_INS = ["x", "positions", "ln1_g", "ln1_b", "ffn1_w1", "ffn1_w3", "ffn1_w2", "w_in", "gate_b", "cmp_pe", "cmp_w1",
        "cmp_b1", "cmp_w2", "cmp_b2", "w_out", "ln2_g", "ln2_b", "ffn2_w1", "ffn2_w3", "ffn2_w2", "ln3_g", "ln3_b"]


def _constants():
    import numpy as np

    f = np.float32
    inv_freq = (f(10000.0) ** (-np.arange(0, HD, 2, dtype=f) / f(HD))).astype(f)[None, :]
    d = (P + np.arange(P)[:, None]) - np.arange(SEQ)[None, :]
    causal = np.where(d >= 0, 0.0, -1e30).astype(f)
    count = (d <= 128) * 1 + (d % 4 == 0) * 1 + (d % 16 == 0) * 1
    dil = np.where((d >= 0) & (count > 0), np.log(np.maximum(count, 1)) / SCALE, -1e30).astype(f)
    token = np.arange(SEQ).reshape(NT, P).T[:, :, None]
    seen = np.arange(N_CMP) * CMP_STRIDE + CMP_BLOCK - 1 <= token
    cmp = np.stack([np.where(seen, 0.0, -1e30), seen * 1.0], axis=1).astype(f)
    return {"inv_freq": inv_freq, "dil_mask": dil, "causal_mask": causal, "cmp_mask": cmp}


def kernel(**inputs):
    import numpy as _np
    import concourse.bacc as _bacc
    from concourse import mybir as _mybir
    from concourse.bass_utils import run_bass_kernel_spmd as _run

    nc = _bacc.Bacc("TRN2", target_bir_lowering=False, num_devices=1)
    arrays, args = {}, []
    given = {name: _np.ascontiguousarray(inputs[name]) for name in _INS}
    for name, a in {**given, **_constants()}.items():
        arrays[f"in_{name}"] = a
        args.append(nc.dram_tensor(f"in_{name}", a.shape, _mybir.dt.from_np(a.dtype), kind="ExternalInput").ap())
    args.append(nc.dram_tensor("out_0", (1, SEQ, DM), F32, kind="ExternalOutput").ap())
    layer(nc, *args)
    r = _run(nc, [arrays], core_ids=[0])
    return r.results[0]["out_0"]
```
